# Optimizing a Trainium2 kernel written in Bass

```python
import math
import jax
import jax.numpy as jnp
from jax import lax
import numpy as np
import jax, jax.numpy as jnp

D_MODEL = 1024
BATCH = 1
SEQ = 256
DEPTH = 1

EPS = 1e-6
CONV_WIDTH = 4
MIX_WIDTH = 2 * D_MODEL
ATT_HEAD_DIM = 64
ATT_WIDTH = MIX_WIDTH // 4
ATT_HEADS = ATT_WIDTH // ATT_HEAD_DIM
Q_BLOCK = 128
SSD_HEAD_DIM = 64
SSD_WIDTH = MIX_WIDTH // 2
SSD_HEADS = SSD_WIDTH // SSD_HEAD_DIM
SSD_GROUPS = 2
SSD_STATE = 128
SSD_CHUNK = 128
SSD_CONV_DIM = SSD_WIDTH + 2 * SSD_GROUPS * SSD_STATE
DT_MIN = 0.001
DT_MAX = 0.1
LRU_WIDTH = MIX_WIDTH // 4
LRU_BLOCKS = 8
LRU_BLOCK_DIM = LRU_WIDTH // LRU_BLOCKS
LRU_C = 8.0
IN_SIZES = (ATT_WIDTH, ATT_WIDTH, ATT_WIDTH, ATT_WIDTH, ATT_HEADS,
            SSD_WIDTH, SSD_CONV_DIM, SSD_HEADS,
            LRU_WIDTH, LRU_WIDTH)
D_IN = sum(IN_SIZES)


def rms_norm(x, g):
    xf = x.astype(jnp.float32)
    return xf * lax.rsqrt(jnp.mean(xf * xf, axis=-1, keepdims=True) + EPS) * g

def causal_dwconv(x, w, b):
    k = w.shape[0]
    y = lax.conv_general_dilated(
        x, w.astype(x.dtype)[:, None, :], window_strides=(1,),
        padding=((k - 1, 0),), dimension_numbers=('NWC', 'WIO', 'NWC'),
        feature_group_count=x.shape[-1])
    return y + b

def fox_attention(q, k, v, log_f, q_g, k_g):
    bsz, seq = q.shape[0], q.shape[1]
    nb = seq // Q_BLOCK
    q = rms_norm(q, q_g)
    k = rms_norm(k, k_g)
    c = jnp.cumsum(log_f.astype(jnp.float32), axis=1)
    qb = q.reshape(bsz, nb, Q_BLOCK, ATT_HEADS, ATT_HEAD_DIM).transpose(1, 0, 3, 2, 4)
    cq = c.reshape(bsz, nb, Q_BLOCK, ATT_HEADS).transpose(1, 0, 3, 2)
    kt = k.transpose(0, 2, 1, 3)
    vt = v.transpose(0, 2, 1, 3)
    ck = c.transpose(0, 2, 1)
    kpos = jnp.arange(seq)
    scale = ATT_HEAD_DIM ** -0.5

    def one_block(args):
        q_i, c_i, blk = args
        logits = jnp.einsum('bhqd,bhkd->bhqk', q_i, kt) * scale + (c_i[..., :, None] - ck[:, :, None, :])
        qpos = blk * Q_BLOCK + jnp.arange(Q_BLOCK)
        logits = jnp.where(kpos[None, :] <= qpos[:, None], logits, -jnp.inf)
        p = jax.nn.softmax(logits.astype(jnp.float32), axis=-1)
        return jnp.einsum('bhqk,bhkd->bhqd', p, vt)

    o = lax.map(one_block, (qb, cq, jnp.arange(nb)))
    return o.transpose(1, 0, 3, 2, 4).reshape(bsz, seq, ATT_WIDTH)

def ssd_mixer(xbc_raw, dt_raw, z, conv_w, conv_b, dt_bias, a_log, d_skip, norm_g):
    bsz, seq = xbc_raw.shape[0], xbc_raw.shape[1]
    nc = seq // SSD_CHUNK
    e = SSD_HEADS // SSD_GROUPS
    gn = SSD_GROUPS * SSD_STATE
    xbc = jax.nn.silu(causal_dwconv(xbc_raw, conv_w, conv_b))
    xs, bm, cm = jnp.split(xbc, [SSD_WIDTH, SSD_WIDTH + gn], axis=-1)
    dt = jax.nn.softplus(dt_raw + dt_bias)
    a = -jnp.exp(a_log.astype(jnp.float32))
    xh = xs.reshape(bsz, seq, SSD_HEADS, SSD_HEAD_DIM)
    xdt = (xh * dt[..., None]).reshape(bsz, nc, SSD_CHUNK, SSD_GROUPS, e, SSD_HEAD_DIM)
    adt = (dt * a).reshape(bsz, nc, SSD_CHUNK, SSD_GROUPS, e).transpose(0, 1, 3, 4, 2)
    bc = bm.reshape(bsz, nc, SSD_CHUNK, SSD_GROUPS, SSD_STATE)
    cc = cm.reshape(bsz, nc, SSD_CHUNK, SSD_GROUPS, SSD_STATE)
    a_cs = jnp.cumsum(adt, axis=-1)
    causal = jnp.tril(jnp.ones((SSD_CHUNK, SSD_CHUNK), dtype=bool))
    seg = a_cs[..., :, None] - a_cs[..., None, :]
    lmat = jnp.exp(jnp.where(causal, seg, -jnp.inf))
    cb = jnp.einsum('bclgn,bcsgn->bcgls', cc, bc)
    y_diag = jnp.einsum('bcgels,bcsgep->bclgep', cb[:, :, :, None] * lmat, xdt)
    decay_states = jnp.exp(a_cs[..., -1:] - a_cs)
    states = jnp.einsum('bclgn,bcgel,bclgep->bcgepn', bc, decay_states, xdt)
    tot = jnp.concatenate([jnp.zeros_like(a_cs[:, :1, ..., -1]), a_cs[..., -1]], axis=1)
    tot_cs = jnp.cumsum(tot, axis=1)
    seg_c = tot_cs[:, :, None] - tot_cs[:, None, :]
    causal_c = jnp.tril(jnp.ones((nc + 1, nc + 1), dtype=bool))[None, :, :, None, None]
    decay_chunk = jnp.exp(jnp.where(causal_c, seg_c, -jnp.inf))
    states_pad = jnp.concatenate([jnp.zeros_like(states[:, :1]), states], axis=1)
    new_states = jnp.einsum('bzcge,bcgepn->bzgepn', decay_chunk, states_pad)
    prev_states = new_states[:, :nc]
    y_off = jnp.einsum('bclgn,bcgepn,bcgel->bclgep', cc, prev_states, jnp.exp(a_cs))
    y = (y_diag + y_off).reshape(bsz, seq, SSD_HEADS, SSD_HEAD_DIM) + xh * d_skip[:, None]
    y = y.reshape(bsz, seq, SSD_WIDTH)
    gated = (y * jax.nn.silu(z)).reshape(bsz, seq, SSD_GROUPS, SSD_WIDTH // SSD_GROUPS)
    gated = rms_norm(gated, 1.0).reshape(bsz, seq, SSD_WIDTH)
    return gated * norm_g

def _lin_combine(c1, c2):
    a1, b1 = c1
    a2, b2 = c2
    return a1 * a2, a2 * b1 + b2

def rglru_mixer(x_raw, conv_w, conv_b, w_a, b_a, w_x, b_x, lam):
    bsz, seq = x_raw.shape[0], x_raw.shape[1]
    xc = causal_dwconv(x_raw, conv_w, conv_b)
    xb = xc.reshape(bsz, seq, LRU_BLOCKS, LRU_BLOCK_DIM)
    r = jax.nn.sigmoid(jnp.einsum('bsnd,nde->bsne', xb, w_a).reshape(bsz, seq, LRU_WIDTH) + b_a)
    i = jax.nn.sigmoid(jnp.einsum('bsnd,nde->bsne', xb, w_x).reshape(bsz, seq, LRU_WIDTH) + b_x)
    log_a = (-LRU_C * r * jax.nn.softplus(-lam)).astype(jnp.float32)
    a = jnp.exp(log_a)
    mult = jnp.sqrt(-jnp.expm1(2.0 * log_a))
    mult = jnp.where((jnp.arange(seq) == 0)[None, :, None], 1.0, mult)
    b = mult * (i * xc)
    _, h = lax.associative_scan(_lin_combine, (a, b), axis=1)
    return h

def first_inputs(seed: int = 0) -> dict:
    key = jax.random.key(seed)
    ks = jax.random.split(key, 24)
    f32 = jnp.float32
    L = DEPTH
    nrm = lambda k, s: jax.random.normal(k, s, f32)
    x = nrm(ks[0], (BATCH, SEQ, D_MODEL))
    norm_g = 1.0 + 0.05 * nrm(ks[1], (L, D_MODEL))
    w_in = nrm(ks[2], (L, D_MODEL, D_IN)) * D_MODEL ** -0.5
    q_norm_g = 1.0 + 0.05 * nrm(ks[3], (L, ATT_HEAD_DIM))
    k_norm_g = 1.0 + 0.05 * nrm(ks[4], (L, ATT_HEAD_DIM))
    forget_b = jax.random.uniform(ks[5], (L, ATT_HEADS), f32, minval=1.0, maxval=4.0)
    ssd_conv_w = nrm(ks[6], (L, CONV_WIDTH, SSD_CONV_DIM)) * CONV_WIDTH ** -0.5
    ssd_conv_b = 0.02 * nrm(ks[7], (L, SSD_CONV_DIM))
    dt0 = jnp.exp(jax.random.uniform(ks[8], (L, SSD_HEADS), f32) * (math.log(DT_MAX) - math.log(DT_MIN)) + math.log(DT_MIN))
    ssd_dt_bias = dt0 + jnp.log(-jnp.expm1(-dt0))
    ssd_a_log = jnp.log(jax.random.uniform(ks[9], (L, SSD_HEADS), f32, minval=1.0, maxval=16.0))
    ssd_d = 1.0 + 0.1 * nrm(ks[10], (L, SSD_HEADS))
    ssd_norm_g = 1.0 + 0.05 * nrm(ks[11], (L, SSD_WIDTH))
    lru_conv_w = nrm(ks[12], (L, CONV_WIDTH, LRU_WIDTH)) * CONV_WIDTH ** -0.5
    lru_conv_b = 0.02 * nrm(ks[13], (L, LRU_WIDTH))
    lru_w_a = nrm(ks[14], (L, LRU_BLOCKS, LRU_BLOCK_DIM, LRU_BLOCK_DIM)) * LRU_BLOCK_DIM ** -0.5
    lru_b_a = 0.02 * nrm(ks[15], (L, LRU_WIDTH))
    lru_w_x = nrm(ks[16], (L, LRU_BLOCKS, LRU_BLOCK_DIM, LRU_BLOCK_DIM)) * LRU_BLOCK_DIM ** -0.5
    lru_b_x = 0.02 * nrm(ks[17], (L, LRU_WIDTH))
    a_pow_c = jax.random.uniform(ks[18], (L, LRU_WIDTH), f32, minval=0.9, maxval=0.999)
    s = a_pow_c ** (1.0 / LRU_C)
    lru_lambda = jnp.log(s) - jnp.log1p(-s)
    w_out = nrm(ks[19], (L, MIX_WIDTH, D_MODEL)) * MIX_WIDTH ** -0.5
    return {'x': x, 'norm_g': norm_g, 'w_in': w_in, 'q_norm_g': q_norm_g, 'k_norm_g': k_norm_g,
            'forget_b': forget_b, 'ssd_conv_w': ssd_conv_w, 'ssd_conv_b': ssd_conv_b,
            'ssd_dt_bias': ssd_dt_bias, 'ssd_a_log': ssd_a_log, 'ssd_d': ssd_d,
            'ssd_norm_g': ssd_norm_g, 'lru_conv_w': lru_conv_w, 'lru_conv_b': lru_conv_b,
            'lru_w_a': lru_w_a, 'lru_b_a': lru_b_a, 'lru_w_x': lru_w_x, 'lru_b_x': lru_b_x,
            'lru_lambda': lru_lambda, 'w_out': w_out}

def first_block(x, norm_g, w_in, q_norm_g, k_norm_g, forget_b, ssd_conv_w, ssd_conv_b,
              ssd_dt_bias, ssd_a_log, ssd_d, ssd_norm_g, lru_conv_w, lru_conv_b,
              lru_w_a, lru_b_a, lru_w_x, lru_b_x, lru_lambda, w_out):
    out_dtype = x.dtype
    h = x.astype(jnp.float32)
    bsz, seq = h.shape[0], h.shape[1]
    split_points = np.cumsum(IN_SIZES)[:-1].tolist()
    for l in range(DEPTH):
        u = rms_norm(h, norm_g[l])
        proj = jnp.einsum('bsd,de->bse', u, w_in[l])
        (q, k, v, z_att, f_raw, z_ssd, xbc, dt_raw, x_lru, z_lru) = jnp.split(proj, split_points, axis=-1)
        hs = (bsz, seq, ATT_HEADS, ATT_HEAD_DIM)
        log_f = jax.nn.log_sigmoid(f_raw + forget_b[l])
        y_att = fox_attention(q.reshape(hs), k.reshape(hs), v.reshape(hs), log_f,
                              q_norm_g[l], k_norm_g[l]) * jax.nn.silu(z_att)
        y_ssd = ssd_mixer(xbc, dt_raw, z_ssd, ssd_conv_w[l], ssd_conv_b[l], ssd_dt_bias[l],
                          ssd_a_log[l], ssd_d[l], ssd_norm_g[l])
        y_lru = rglru_mixer(x_lru, lru_conv_w[l], lru_conv_b[l], lru_w_a[l], lru_b_a[l],
                            lru_w_x[l], lru_b_x[l], lru_lambda[l]) * jax.nn.silu(z_lru)
        mix = jnp.concatenate([y_att, y_ssd, y_lru], axis=-1)
        h = h + jnp.einsum('bse,ed->bsd', mix, w_out[l])
    return h.astype(out_dtype)


DEPTH_2 = 2

MIX_WIDTH_2 = D_MODEL // 2
RET_HEAD_DIM = 128
RET_HEADS = MIX_WIDTH_2 // RET_HEAD_DIM
RET_CHUNK = 128
ROPE_BASE = 10000.0
RWKV_HEAD_DIM = 64
RWKV_HEADS = MIX_WIDTH_2 // RWKV_HEAD_DIM
DECAY_LORA = 64
AAA_LORA = 64
GATE_LORA = 128
CONV_WIDTH_2 = 3
N_BRANCHES = 3
RET_COLS = 4 * MIX_WIDTH_2
RWKV_COLS = 3 * MIX_WIDTH_2 + DECAY_LORA + AAA_LORA + GATE_LORA
CONV_COLS = 3 * MIX_WIDTH_2
IN_COLS = RET_COLS + RWKV_COLS + CONV_COLS
N_GROUPS = 4
EXPERTS_PER_GROUP = 8
N_EXPERTS = N_GROUPS * EXPERTS_PER_GROUP
EXPERT_FF = D_MODEL // 2
TOP_K = 2
MOE_BLOCK = 128
NORM_EPS = 1e-6
HEAD_NORM_EPS = 1e-5
RWKV_NORM_EPS = 64e-5


F32 = jnp.float32

def rms_norm_2(x, g):
    xf = x.astype(F32)
    y = xf * lax.rsqrt(jnp.mean(xf * xf, axis=-1, keepdims=True) + NORM_EPS)
    return (y * g.astype(F32)).astype(x.dtype)

def modulate(h, shift, scale):
    return (h.astype(F32) * (1.0 + scale[:, None, :]) + shift[:, None, :]).astype(h.dtype)

def head_norm(y, g, eps):
    yf = y.astype(F32)
    mu = jnp.mean(yf, axis=-1, keepdims=True)
    var = jnp.mean(jnp.square(yf - mu), axis=-1, keepdims=True)
    return (yf - mu) * lax.rsqrt(var + eps) * g.astype(F32).reshape(y.shape[-2:])

def rotary(t, positions):
    half = t.shape[-1] // 2
    inv_freq = ROPE_BASE ** (-jnp.arange(half, dtype=F32) / half)
    ang = positions.astype(F32)[..., None] * inv_freq
    cos = jnp.cos(ang)[:, :, None, :]
    sin = jnp.sin(ang)[:, :, None, :]
    t1 = t[..., :half].astype(F32)
    t2 = t[..., half:].astype(F32)
    return jnp.concatenate([t1 * cos - t2 * sin, t1 * sin + t2 * cos], axis=-1)

def retention(q, k, v, g, positions, gn_g):
    bsz, seq, _ = q.shape
    split = lambda t: t.reshape(bsz, seq, RET_HEADS, RET_HEAD_DIM)
    qh = rotary(split(q), positions)
    kh = rotary(split(k), positions) * (RET_HEAD_DIM ** -0.5)
    vh = split(v).astype(F32)
    n_chunks = seq // RET_CHUNK

    def to_chunks(t):
        return t.reshape(bsz, n_chunks, RET_CHUNK, RET_HEADS, RET_HEAD_DIM).transpose(1, 0, 3, 2, 4)

    log_gamma = jnp.log1p(-jnp.exp2(-5.0 - jnp.arange(RET_HEADS, dtype=F32)))
    pos = jnp.arange(RET_CHUNK, dtype=F32)
    rel = pos[:, None] - pos[None, :]
    decay_in = jnp.where(rel >= 0, jnp.exp(log_gamma[:, None, None] * jnp.maximum(rel, 0.0)), 0.0)
    decay_k = jnp.exp(log_gamma[:, None] * (RET_CHUNK - 1 - pos))
    decay_q = jnp.exp(log_gamma[:, None] * (pos + 1.0))
    decay_chunk = jnp.exp(log_gamma * RET_CHUNK)

    def chunk_step(state, qkv):
        qc, kc, vc = qkv
        scores = jnp.einsum('bhid,bhjd->bhij', qc, kc) * decay_in
        inner = jnp.einsum('bhij,bhjv->bhiv', scores, vc)
        cross = jnp.einsum('bhid,bhdv->bhiv', qc, state) * decay_q[None, :, :, None]
        state = state * decay_chunk[None, :, None, None] + jnp.einsum(
            'bhjd,bhjv->bhdv', kc * decay_k[None, :, :, None], vc)
        return state, inner + cross

    state0 = jnp.zeros((bsz, RET_HEADS, RET_HEAD_DIM, RET_HEAD_DIM), F32)
    _, out = lax.scan(chunk_step, state0, (to_chunks(qh), to_chunks(kh), to_chunks(vh)))
    out = out.transpose(1, 0, 3, 2, 4).reshape(bsz, seq, RET_HEADS, RET_HEAD_DIM)
    out = head_norm(out, gn_g, HEAD_NORM_EPS).reshape(bsz, seq, MIX_WIDTH_2)
    return (jax.nn.silu(g.astype(F32)) * out).astype(q.dtype)

def rwkv7_time_mix(p, mu, w0, w_lora, a0, a_lora, g_lora, k_k, k_a, r_k, gn_g):
    bsz, seq, _ = p.shape
    mw = MIX_WIDTH_2
    pf = p.astype(F32)
    prev = jnp.pad(pf, ((0, 0), (1, 0), (0, 0)))[:, :-1]
    pf = pf + mu * (prev - pf)
    o_w = 3 * mw
    o_a = o_w + DECAY_LORA
    o_g = o_a + AAA_LORA
    r = pf[..., 0:mw]
    k = pf[..., mw:2 * mw]
    v = pf[..., 2 * mw:3 * mw]
    wd = pf[..., o_w:o_a]
    ad = pf[..., o_a:o_g]
    gd = pf[..., o_g:o_g + GATE_LORA]
    w = jnp.exp(-math.exp(-0.5) * jax.nn.sigmoid(w0 + jnp.tanh(wd) @ w_lora))
    a = jax.nn.sigmoid(a0 + ad @ a_lora)
    g = jax.nn.sigmoid(gd) @ g_lora
    heads = lambda t: t.reshape(bsz, seq, RWKV_HEADS, RWKV_HEAD_DIM)
    r, w, k, v, a = heads(r), heads(w), heads(k), heads(v), heads(a)
    kk = k * k_k.reshape(RWKV_HEADS, RWKV_HEAD_DIM)
    kh = kk * lax.rsqrt(jnp.maximum(jnp.sum(kk * kk, axis=-1, keepdims=True), 1e-12))
    kt = k * (1.0 + (a - 1.0) * k_a.reshape(RWKV_HEADS, RWKV_HEAD_DIM))

    def time_step(state, inp):
        rt, wt, ktt, vt, kht, at = inp
        sk = jnp.einsum('bhvk,bhk->bhv', state, kht)
        state = (state * wt[:, :, None, :]
                 - sk[..., None] * (at * kht)[:, :, None, :]
                 + vt[..., None] * ktt[:, :, None, :])
        return state, jnp.einsum('bhvk,bhk->bhv', state, rt)

    tm = lambda t: jnp.moveaxis(t, 1, 0)
    state0 = jnp.zeros((bsz, RWKV_HEADS, RWKV_HEAD_DIM, RWKV_HEAD_DIM), F32)
    _, y = lax.scan(time_step, state0, (tm(r), tm(w), tm(kt), tm(v), tm(kh), tm(a)))
    y = jnp.moveaxis(y, 0, 1)
    y = head_norm(y, gn_g, RWKV_NORM_EPS)
    y = y + jnp.sum(r * kt * r_k.astype(F32), axis=-1, keepdims=True) * v
    return (y.reshape(bsz, seq, mw) * g).astype(p.dtype)

def short_conv(p, conv_w):
    h, bgate, cgate = jnp.split(p, 3, axis=-1)
    u = cgate * h
    seq = u.shape[1]
    up = jnp.pad(u, ((0, 0), (CONV_WIDTH_2 - 1, 0), (0, 0)))
    conv = conv_w[0] * up[:, 0:seq]
    for i in range(1, CONV_WIDTH_2):
        conv = conv + conv_w[i] * up[:, i:i + seq]
    return bgate * conv

def hier_moe(h, w_router_group, b_router_group, w_router_expert, b_router_expert,
             w_exp_gate, w_exp_up, w_exp_down):
    bsz, seq, d = h.shape
    n_tok = bsz * seq
    xf = h.reshape(n_tok, d)
    g_logits = (xf @ w_router_group + b_router_group).astype(F32)
    g_prob = jax.nn.softmax(g_logits, axis=-1)
    g_sel = jnp.argmax(g_logits, axis=-1).astype(jnp.int32)
    p_group = jnp.take_along_axis(g_prob, g_sel[:, None], axis=-1)
    e_logits = (xf @ w_router_expert + b_router_expert).astype(F32).reshape(n_tok, N_GROUPS, EXPERTS_PER_GROUP)
    e_logits = jnp.take_along_axis(e_logits, g_sel[:, None, None], axis=1)[:, 0]
    top_v, top_i = lax.top_k(e_logits, TOP_K)
    weights = (jax.nn.softmax(top_v, axis=-1) * p_group).reshape(-1)
    eid = (g_sel[:, None] * EXPERTS_PER_GROUP + top_i).reshape(-1).astype(jnp.int32)
    tok = jnp.repeat(jnp.arange(n_tok, dtype=jnp.int32), TOP_K)
    n_assign = n_tok * TOP_K
    order = jnp.argsort(eid)
    eid_s, tok_s, w_s = eid[order], tok[order], weights[order]
    counts = jnp.bincount(eid, length=N_EXPERTS).astype(jnp.int32)
    starts = jnp.cumsum(counts) - counts
    padded = (counts + MOE_BLOCK - 1) // MOE_BLOCK * MOE_BLOCK
    pends = jnp.cumsum(padded)
    pstarts = pends - padded
    dest = pstarts[eid_s] + jnp.arange(n_assign, dtype=jnp.int32) - starts[eid_s]
    n_rows = n_assign + N_EXPERTS * MOE_BLOCK
    n_blocks = n_rows // MOE_BLOCK
    row_tok = jnp.full((n_rows,), n_tok, jnp.int32).at[dest].set(tok_s)
    row_w = jnp.zeros((n_rows,), F32).at[dest].set(w_s)
    block_e = jnp.minimum(
        jnp.searchsorted(pends, jnp.arange(n_blocks, dtype=jnp.int32) * MOE_BLOCK, side='right'),
        N_EXPERTS - 1)
    x_rows = jnp.concatenate([xf, jnp.zeros((1, d), xf.dtype)], axis=0)[row_tok]
    x_rows = x_rows.reshape(n_blocks, MOE_BLOCK, d)

    def expert_block(args):
        xb, e = args
        return (jax.nn.silu(xb @ w_exp_gate[e]) * (xb @ w_exp_up[e])) @ w_exp_down[e]

    y_rows = lax.map(expert_block, (x_rows, block_e)).reshape(n_rows, d)
    y_rows = y_rows.astype(F32) * row_w[:, None]
    out = jax.ops.segment_sum(y_rows, row_tok, num_segments=n_tok + 1)[:n_tok]
    return out.reshape(bsz, seq, d).astype(h.dtype)

def decoder_layer(x, c, positions, norm1_g, norm2_g, w_ada, b_ada, w_in, w_gate, b_gate,
                  ret_gn_g, rwkv_mu, rwkv_w0, rwkv_w_lora, rwkv_a0, rwkv_a_lora, rwkv_g_lora,
                  rwkv_k_k, rwkv_k_a, rwkv_r_k, rwkv_gn_g, conv_w, w_branch, w_o,
                  w_router_group, b_router_group, w_router_expert, b_router_expert,
                  w_exp_gate, w_exp_up, w_exp_down):
    d = D_MODEL
    mod = jax.nn.silu(c.astype(F32)) @ w_ada + b_ada
    shift1, scale1, gate1, shift2, scale2, gate2 = jnp.split(mod, 6, axis=-1)

    h = modulate(rms_norm_2(x, norm1_g), shift1, scale1)
    p = h @ w_in
    p_ret = p[..., :RET_COLS]
    p_rwkv = p[..., RET_COLS:RET_COLS + RWKV_COLS]
    p_conv = p[..., RET_COLS + RWKV_COLS:]
    q, k, v, g = jnp.split(p_ret, 4, axis=-1)
    y_ret = retention(q, k, v, g, positions, ret_gn_g)
    y_rwkv = rwkv7_time_mix(p_rwkv, rwkv_mu, rwkv_w0, rwkv_w_lora, rwkv_a0, rwkv_a_lora,
                            rwkv_g_lora, rwkv_k_k, rwkv_k_a, rwkv_r_k, rwkv_gn_g)
    y_conv = short_conv(p_conv, conv_w)
    gates = jax.nn.sigmoid((h @ w_gate + b_gate).astype(F32))
    merged = jnp.zeros(x.shape, F32)
    for i, y in enumerate((y_ret, y_rwkv, y_conv)):
        merged = merged + gates[..., i * d:(i + 1) * d] * (y @ w_branch[i])
    x = x + (gate1[:, None, :] * (merged.astype(x.dtype) @ w_o)).astype(x.dtype)

    h2 = modulate(rms_norm_2(x, norm2_g), shift2, scale2)
    y_moe = hier_moe(h2, w_router_group, b_router_group, w_router_expert, b_router_expert,
                     w_exp_gate, w_exp_up, w_exp_down)
    x = x + (gate2[:, None, :] * y_moe).astype(x.dtype)
    return x

def second_inputs(seed: int = 0) -> dict:
    key = jax.random.key(seed)
    k = jax.random.split(key, 32)
    L, D, MW = DEPTH_2, D_MODEL, MIX_WIDTH_2

    def nrm(kk, shape, scale):
        return scale * jax.random.normal(kk, shape, jnp.float32)

    return {
        'x': nrm(k[0], (BATCH, SEQ, D), 1.0),
        'c': nrm(k[1], (BATCH, D), 1.0),
        'positions': jnp.tile(jnp.arange(SEQ, dtype=jnp.int32)[None, :], (BATCH, 1)),
        'norm1_g': 1.0 + nrm(k[2], (L, D), 0.02),
        'norm2_g': 1.0 + nrm(k[3], (L, D), 0.02),
        'final_norm_g': 1.0 + nrm(k[4], (D,), 0.02),
        'w_ada': nrm(k[5], (L, D, 6 * D), 0.5 * D ** -0.5),
        'b_ada': nrm(k[6], (L, 6 * D), 0.01),
        'w_in': nrm(k[7], (L, D, IN_COLS), D ** -0.5),
        'w_gate': nrm(k[8], (L, D, N_BRANCHES * D), D ** -0.5),
        'b_gate': nrm(k[9], (L, N_BRANCHES * D), 0.01),
        'ret_gn_g': 1.0 + nrm(k[10], (L, MW), 0.02),
        'rwkv_mu': jax.random.uniform(k[11], (L, RWKV_COLS), jnp.float32),
        'rwkv_w0': nrm(k[12], (L, MW), 0.5),
        'rwkv_w_lora': nrm(k[13], (L, DECAY_LORA, MW), DECAY_LORA ** -0.5),
        'rwkv_a0': nrm(k[14], (L, MW), 0.5),
        'rwkv_a_lora': nrm(k[15], (L, AAA_LORA, MW), AAA_LORA ** -0.5),
        'rwkv_g_lora': nrm(k[16], (L, GATE_LORA, MW), GATE_LORA ** -0.5),
        'rwkv_k_k': 0.85 + nrm(k[17], (L, MW), 0.05),
        'rwkv_k_a': 1.0 + nrm(k[18], (L, MW), 0.05),
        'rwkv_r_k': nrm(k[19], (L, RWKV_HEADS, RWKV_HEAD_DIM), 0.1),
        'rwkv_gn_g': 1.0 + nrm(k[20], (L, MW), 0.02),
        'conv_w': nrm(k[21], (L, CONV_WIDTH_2, MW), CONV_WIDTH_2 ** -0.5),
        'w_branch': nrm(k[22], (L, N_BRANCHES, MW, D), MW ** -0.5),
        'w_o': nrm(k[23], (L, D, D), D ** -0.5),
        'w_router_group': nrm(k[24], (L, D, N_GROUPS), D ** -0.5),
        'b_router_group': nrm(k[25], (L, N_GROUPS), 0.01),
        'w_router_expert': nrm(k[26], (L, D, N_EXPERTS), D ** -0.5),
        'b_router_expert': nrm(k[27], (L, N_EXPERTS), 0.01),
        'w_exp_gate': nrm(k[28], (L, N_EXPERTS, D, EXPERT_FF), D ** -0.5),
        'w_exp_up': nrm(k[29], (L, N_EXPERTS, D, EXPERT_FF), D ** -0.5),
        'w_exp_down': nrm(k[30], (L, N_EXPERTS, EXPERT_FF, D), EXPERT_FF ** -0.5),
    }

def second_block(x, c, positions, norm1_g, norm2_g, final_norm_g, w_ada, b_ada, w_in, w_gate, b_gate,
              ret_gn_g, rwkv_mu, rwkv_w0, rwkv_w_lora, rwkv_a0, rwkv_a_lora, rwkv_g_lora,
              rwkv_k_k, rwkv_k_a, rwkv_r_k, rwkv_gn_g, conv_w, w_branch, w_o,
              w_router_group, b_router_group, w_router_expert, b_router_expert,
              w_exp_gate, w_exp_up, w_exp_down):
    for l in range(DEPTH_2):
        x = decoder_layer(
            x, c, positions, norm1_g[l], norm2_g[l], w_ada[l], b_ada[l], w_in[l], w_gate[l], b_gate[l],
            ret_gn_g[l], rwkv_mu[l], rwkv_w0[l], rwkv_w_lora[l], rwkv_a0[l], rwkv_a_lora[l],
            rwkv_g_lora[l], rwkv_k_k[l], rwkv_k_a[l], rwkv_r_k[l], rwkv_gn_g[l], conv_w[l],
            w_branch[l], w_o[l], w_router_group[l], b_router_group[l], w_router_expert[l],
            b_router_expert[l], w_exp_gate[l], w_exp_up[l], w_exp_down[l])
    return rms_norm_2(x, final_norm_g)


def setup_inputs(seed=0):
    out = dict(first_inputs(seed))
    for name, value in second_inputs(seed + 1).items():
        if name != "x":
            out[name + "_2"] = value
    return out


def reference(
    x, norm_g, w_in, q_norm_g, k_norm_g, forget_b, ssd_conv_w, ssd_conv_b, ssd_dt_bias,
    ssd_a_log, ssd_d, ssd_norm_g, lru_conv_w, lru_conv_b, lru_w_a, lru_b_a, lru_w_x, lru_b_x,
    lru_lambda, w_out, c_2, positions_2, norm1_g_2, norm2_g_2, final_norm_g_2, w_ada_2, b_ada_2,
    w_in_2, w_gate_2, b_gate_2, ret_gn_g_2, rwkv_mu_2, rwkv_w0_2, rwkv_w_lora_2, rwkv_a0_2,
    rwkv_a_lora_2, rwkv_g_lora_2, rwkv_k_k_2, rwkv_k_a_2, rwkv_r_k_2, rwkv_gn_g_2, conv_w_2,
    w_branch_2, w_o_2, w_router_group_2, b_router_group_2, w_router_expert_2, b_router_expert_2,
    w_exp_gate_2, w_exp_up_2, w_exp_down_2,
):
    x = first_block(
        x, norm_g, w_in, q_norm_g, k_norm_g, forget_b, ssd_conv_w, ssd_conv_b, ssd_dt_bias,
        ssd_a_log, ssd_d, ssd_norm_g, lru_conv_w, lru_conv_b, lru_w_a, lru_b_a, lru_w_x,
        lru_b_x, lru_lambda, w_out,
    )
    return second_block(
        x, c_2, positions_2, norm1_g_2, norm2_g_2, final_norm_g_2, w_ada_2, b_ada_2, w_in_2,
        w_gate_2, b_gate_2, ret_gn_g_2, rwkv_mu_2, rwkv_w0_2, rwkv_w_lora_2, rwkv_a0_2,
        rwkv_a_lora_2, rwkv_g_lora_2, rwkv_k_k_2, rwkv_k_a_2, rwkv_r_k_2, rwkv_gn_g_2, conv_w_2,
        w_branch_2, w_o_2, w_router_group_2, b_router_group_2, w_router_expert_2,
        b_router_expert_2, w_exp_gate_2, w_exp_up_2, w_exp_down_2,
    )


_drawn_inputs = setup_inputs


def setup_inputs(seed=0):
    import zlib

    import numpy as np

    out = dict(_drawn_inputs(seed))
    spreads = {}
    factors = {'q_norm_g': 7.177,
     'k_norm_g': 8.0,
     'ssd_conv_b': 2.712,
     'lru_b_a': 8.0,
     'lru_b_x': 8.0,
     'norm1_g_2': 4.027,
     'norm2_g_2': 4.43,
     'final_norm_g_2': 25.321,
     'b_ada_2': 3.425,
     'b_gate_2': 8.0,
     'ret_gn_g_2': 31.384,
     'rwkv_w_lora_2': 2.986,
     'rwkv_k_k_2': 200.0,
     'rwkv_k_a_2': 5.444,
     'rwkv_gn_g_2': 200.0,
     'b_router_group_2': 31.305,
     'b_router_expert_2': 21.041,
     'rwkv_w0_2': 3.062}
    for name, (base, spread) in spreads.items():
        noise = np.random.default_rng([zlib.crc32(name.encode()), seed]).standard_normal(out[name].shape)
        drawn = base * np.exp(spread * noise) if base else spread * noise
        out[name] = jnp.asarray(drawn.astype(out[name].dtype))
    for name, factor in factors.items():
        out[name] = (out[name] * factor).astype(out[name].dtype)
    return out
```

```python
import math
from contextlib import ExitStack, contextmanager

import numpy as np
import concourse.bass as bass
from concourse import mybir

F32 = mybir.dt.float32
I32 = mybir.dt.int32
ALU = mybir.AluOpType
ACT = mybir.ActivationFunctionType
AX = mybir.AxisListType

P = 128
S = 256
NT = S // P
D = 1024
ND = D // P
EPS = 1e-6
LAYERS = 2

A_H, A_D = 8, 64
A_W = A_H * A_D
N_A = A_W // P
X_H, X_D, X_G = 16, 64, 2
X_W = X_H * X_D
N_X = X_W // P
X_C = X_W + 2 * X_G * P
N_C = X_C // P
L_W = 512
N_L = L_W // P
TAPS = 4
COL_Q, COL_F = 0, 4 * A_W
COL_ZX = COL_F + A_H
COL_XBC = COL_ZX + X_W
COL_DT = COL_XBC + X_C
COL_XL = COL_DT + X_H
COL_ZL = COL_XL + L_W
D_IN = COL_ZL + L_W
MIX = A_W + X_W + L_W

MW = 512
N_M = MW // P
R_H = MW // P
K_H = MW // 64
N_K = 3 * N_M + 2
IN_COLS = 4 * MW + 3 * MW + 256 + 3 * MW
N_E, N_G, FF = 32, 4, 512
E_G = N_E // N_G
N_F = FF // P
LW_SCALE = -math.exp(-0.5)

SLOTS = 3
SLAB = 4096
BIG = 1e30



def constants():
    i = np.arange(P)
    r, c = i[:, None], i[None, :]
    out = {}
    out["ident"] = (r == c)
    out["mean_d"] = np.full((P, P), 1.0 / D)
    out["mean_512"] = np.full((P, P), 1.0 / 512)
    out["mean_128"] = np.full((P, P), 1.0 / P)
    out["sum_64"] = (r // 64 == c // 64)
    out["mean_64"] = (r // 64 == c // 64) / 64.0
    out["swap"] = np.where(r == c + 64, -1.0, np.where(c == r + 64, 1.0, 0.0))
    out["neg_upper"] = np.where(c > r, -BIG, 0.0)
    out["neg_lower"] = np.where(c < r, -BIG, 0.0)
    out["strict"] = (c > r)
    out["incl"] = (c >= r)
    n = 1
    while n < P:
        m = (r // (2 * n) == c // (2 * n)) & (r // n % 2 == 1) & (c // n % 2 == 0)
        out[f"level_{n}"] = m
        if n == 1:
            out["level_1t"] = m.T
        n *= 2
    out["inv_freq"] = (np.float32(10000.0) ** (-(np.arange(64, dtype=np.float32)) / np.float32(64)))[i % 64][:, None]
    rel = np.arange(S)[None, :] - i[:, None]
    for h in range(R_H):
        lg = math.log1p(-2.0 ** (-5.0 - h))
        out[f"decay_{h}"] = np.where(rel >= 0, np.exp(lg * np.maximum(rel, 0)), 0.0) * P ** -0.5
    out["iota_e"] = np.tile(np.arange(N_E, dtype=np.float64), (P, 1))
    return {k: np.asarray(v, np.float32) for k, v in out.items()}


def first_constants():
    r = np.arange(P)[:, None]
    out = {}
    out["pick_neg"] = -np.concatenate([np.tile(r == h, (1, P)) for h in range(A_H)], 1).astype(np.float32)
    out["pick"] = np.concatenate([np.tile(r == h, (1, P)) for h in range(X_H)], 1)
    half = np.arange(P)[None, :] // 64
    out["pick_pair"] = np.concatenate([r == 2 * j + half for j in range(N_X)], 1)
    return {k: np.asarray(v, np.float32) for k, v in out.items()}


def layout(pieces):
    at, out = 0, {}
    for name, a in pieces.items():
        out[name] = (at, a.shape[1])
        at += a.shape[1]
    return out, at



def chain(eng, sem):
    count = [0]

    def step(ins):
        count[0] += 1
        ins.then_inc(sem, 1)
        eng.wait_ge(sem, count[0])
    return step


class Core:

    def __init__(self, nc, ctx, io):
        self.nc, self.ctx, self.io = nc, ctx, io
        self.stages = 0
        self.live = []

    def sb(self, name, shape, dt=F32, ctx=None):
        return (ctx or self.ctx).enter_context(self.nc.sbuf_tensor(name, shape, dt))

    def const(self, name):
        at, n = self.columns[name]
        return self.consts[:, at:at + n]

    @contextmanager
    def stage(self, *names):
        self.stages += 1
        sems = [self.nc.alloc_semaphore(name=f"{n}_{self.stages}") for n in names]
        self.live += sems
        with self.nc.Block() as block:
            yield (block, *sems)

    def clear_semaphores(self):
        self.nc.all_engine_barrier()
        for sem in self.live:
            self.nc.sync.sem_clear(sem)
        self.nc.all_engine_barrier()
        for sem in reversed(self.live):
            self.nc.release_semaphore(sem)
        self.live = []


def slab_view(k, slot, rows, cols):
    n = rows // P
    return k.ring[:, slot, 0:n * cols].rearrange("p (k c) -> p k c", k=n)


def load_slabs(eng, k, slabs, loaded, used, per_slab):
    for i, src in enumerate(slabs):
        if i >= SLOTS:
            eng.wait_ge(used, sum(per_slab[:i - SLOTS + 1]))
        n, c = src.shape[1], src.shape[2]
        dst = k.ring[:, i % SLOTS, 0:n * c].rearrange("p (k c) -> p k c", k=n)
        eng.dma_start(dst, src).then_inc(loaded[i % SLOTS], 16)


LOADED = tuple(f"slot{i}_loaded" for i in range(SLOTS))


def wait_slab(eng, loaded, i):
    eng.wait_ge(loaded[i % SLOTS], 16 * (i // SLOTS + 1))


def project(k, slabs, tiles, rhs, evac_engine="scalar"):
    nc = k.nc
    per_slab = [sum(1 for t in tiles if t[0] == i) for i in range(len(slabs))]
    with k.stage(*LOADED, "tile_done", "tile_stored") as (block, *sems):
        loaded, (done, stored) = sems[:SLOTS], sems[SLOTS:]

        @block.sync
        def _(sp):
            load_slabs(sp, k, slabs, loaded, done, per_slab)

        @block.tensor
        def _(pe):
            last_slab = -1
            for n, (i, c0, w, how, _) in enumerate(tiles):
                if i != last_slab:
                    wait_slab(pe, loaded, i)
                    last_slab = i
                if n >= 4:
                    pe.wait_ge(stored, n - 3)
                nk = slabs[i].shape[1]
                slab = slab_view(k, i % SLOTS, nk * P, slabs[i].shape[2])
                ps = k.ps[:, n % 4, :]
                for j in range(nk):
                    if how == "f":
                        ins = nc.tensor.matmul(ps[0:w, 0:S], slab[:, j, c0:c0 + w], rhs[:, j, :],
                                               start=j == 0, stop=j == nk - 1)
                    else:
                        ins = nc.tensor.matmul(ps[:, 0:w], rhs[:, j, how * P:(how + 1) * P],
                                               slab[:, j, c0:c0 + w], start=j == 0, stop=j == nk - 1)
                ins.then_inc(done, 1)

        def store_all(eng):
            for n, (_, _, w, how, store) in enumerate(tiles):
                eng.wait_ge(done, n + 1)
                store(eng, k.ps[:, n % 4, :]).then_inc(stored, 1)

        if evac_engine == "scalar":
            block.scalar(store_all)
        else:
            block.vector(store_all)


def copy_to(dst, w=P, n=S, func=ACT.Copy):
    return lambda eng, ps: eng.activation(dst, ps[0:w, 0:n], func)


def rms_norm(k, src, dst, gain, shift=None):
    nc = k.nc
    with k.stage("squared", "mean_done", "rstd_done", "ln_done", "vec_chain") as (
            block, squared, mean_done, rstd_done, ln_done, vec_chain):

        @block.scalar
        def _(act):
            nc.scalar.activation(dst, src, ACT.Square).then_inc(squared, 1)
            act.wait_ge(mean_done, 1)
            nc.scalar.activation(k.rstd[:, :], k.ps[:, 0, 0:S], ACT.Ln, bias=k.eps[:, 0:1]).then_inc(ln_done, 1)
            act.wait_ge(ln_done, 1)
            nc.scalar.activation(k.rstd[:, :], k.rstd[:, :], ACT.Exp, scale=-0.5).then_inc(rstd_done, 1)

        @block.tensor
        def _(pe):
            pe.wait_ge(squared, 1)
            for j in range(ND):
                ins = nc.tensor.matmul(k.ps[:, 0, 0:S], k.const("mean_d"), dst[:, j, :],
                                       start=j == 0, stop=j == ND - 1)
            ins.then_inc(mean_done, 1)

        @block.vector
        def _(dve):
            dve.wait_ge(rstd_done, 1)
            for j in range(ND):
                nc.vector.scalar_tensor_tensor(dst[:, j, :], src[:, j, :], gain[:, j:j + 1], k.rstd[:, :],
                                               ALU.mult, ALU.mult).then_inc(vec_chain, 1)
            if shift is not None:
                for j in range(ND):
                    dve.wait_ge(vec_chain, j + 1)
                    nc.vector.tensor_scalar(dst[:, j, :], dst[:, j, :], shift[:, j:j + 1], None, ALU.add)


def log1p_steps(nc, step, out, z, w, w2):
    step(nc.vector.tensor_scalar(w2, z, 2.0, None, ALU.add))
    step(nc.vector.reciprocal(w2, w2))
    step(nc.vector.tensor_tensor(w, z, w2, ALU.mult))
    step(nc.vector.tensor_tensor(w2, w, w, ALU.mult))
    step(nc.vector.tensor_scalar(out, w2, 2.0 / 17, None, ALU.mult))
    for n in range(15, 1, -2):
        step(nc.vector.scalar_tensor_tensor(out, out, 2.0 / n, w2, ALU.add, ALU.mult))
    step(nc.vector.scalar_tensor_tensor(out, out, 2.0, w, ALU.add, ALU.mult))


def load_rows(k, parts):
    nc = k.nc
    at, where, used = 0, {}, [0, 0]
    for name, r, _ in parts:
        if at // P != (at + r - 1) // P:
            at = (at + P - 1) // P * P
        where[name] = (at, r)
        at += r
        used[(at - 1) // P] = (at - 1) % P + 1
    assert at <= 2 * P
    tiles = [g for g in range(2) if used[g]]
    loads = sum(len(pieces) for _, _, pieces in parts)
    with k.stage("rows_loaded", "rows_turned") as (block, loaded, turned):

        @block.sync
        def _(sp):
            for name, r, pieces in parts:
                a, g = where[name][0] % P, where[name][0] // P
                for c0, src in pieces:
                    w = math.prod(src.shape[1:])
                    dst = k.rows[a:a + r, g, c0:c0 + w]
                    if src.ndim == 3:
                        dst = dst.rearrange("r (a b) -> r a b", a=src.shape[1])
                    sp.dma_start(dst, src).then_inc(loaded, 16)

        @block.tensor
        def _(pe):
            pe.wait_ge(loaded, 16 * loads)
            for g in tiles:
                ins = nc.tensor.transpose(k.ps[:, g, 0:used[g]], k.rows[0:used[g], g, :],
                                          k.const("ident")[0:used[g], 0:used[g]])
            ins.then_inc(turned, 1)

        @block.vector
        def _(dve):
            dve.wait_ge(turned, 1)
            for g in tiles:
                nc.vector.tensor_copy(k.cols[:, g * P:g * P + used[g]], k.ps[:, g, 0:used[g]])
    return {name: k.cols[:, a:a + r] for name, (a, r) in where.items()}



def load_inputs(k):
    nc, io = k.nc, k.io
    with ExitStack() as tmp:
        x_tok = k.sb("x_tok", [P, NT, D], ctx=tmp)
        with k.stage("consts_loaded", "x_loaded", "turned", "copied") as (block, consts_loaded, x_loaded, turned, copied):

            @block.sync
            def _(sp):
                sp.dma_start(x_tok[:, :, :], io["x"][0].rearrange("(t p) d -> p t d", p=P)).then_inc(x_loaded, 16)
                sp.dma_start(k.consts[:, :], io["constants"]).then_inc(consts_loaded, 16)

            @block.gpsimd
            def _(pool):
                nc.gpsimd.memset(k.eps[:, 0:1], EPS)
                nc.gpsimd.memset(k.eps[:, 1:2], 1e-5)
                nc.gpsimd.memset(k.eps[:, 2:3], 64e-5)
                nc.gpsimd.memset(k.ones[:, :], 1.0)

            @block.tensor
            def _(pe):
                pe.wait_ge(consts_loaded, 16)
                pe.wait_ge(x_loaded, 16)
                for j in range(ND):
                    for t in range(NT):
                        ins = nc.tensor.transpose(k.ps[:, j, t * P:(t + 1) * P], x_tok[:, t, j * P:(j + 1) * P],
                                                  k.const("ident"))
                ins.then_inc(turned, 1)

            @block.vector
            def _(dve):
                dve.wait_ge(turned, 1)
                nc.vector.tensor_copy(k.x[:, :, :], k.ps[:, :, 0:S])


def attention(k, cols, u, mix):
    nc, io = k.nc, k.io
    w_in = io["w_in"][0].rearrange("(k p) c -> p k c", p=P)
    with ExitStack() as mem:
        q_raw = k.sb("q_raw", [P, N_A, S], ctx=mem)
        k_raw = k.sb("k_raw", [P, N_A, S], ctx=mem)
        z = k.sb("z_att", [P, N_A, S], ctx=mem)
        q_pad = k.sb("q_pad", [P, N_A, 2, S], ctx=mem)
        v_pad = k.sb("v_pad", [P, NT, A_H, P], ctx=mem)
        v_pairs = v_pad[:, :, :, :].rearrange("p t (j h) c -> p t j h c", h=2)
        f = k.sb("f", [P, S], ctx=mem)
        probs = k.sb("probs", [P, A_H, 3 * P], ctx=mem)
        probs_t = k.sb("probs_t", [P, A_H, 3 * P], ctx=mem)
        square = probs[:, :, :].rearrange("p h c -> p (h c)")[:, 0:N_A * S]
        peak = k.sb("peak", [P, A_H, 2], ctx=mem)
        total = k.sb("total", [P, A_H, 2], ctx=mem)
        small = k.sb("small_a", [P, 4, S], ctx=mem)

        with k.stage("cleared") as (block, cleared):
            @block.gpsimd
            def _(pool):
                nc.gpsimd.memset(v_pad[:, :, :, :], 0.0)
                nc.gpsimd.memset(q_pad[:, :, :, :], 0.0)
                nc.gpsimd.memset(f[:, :], 0.0)

        def store_v(t):
            def store(eng, ps):
                src = ps[:, 0:A_W].rearrange("p (j h c) -> p j h c", h=2, c=A_D)
                eng.activation(v_pairs[:, t, :, 0, 0:A_D], src[:, :, 0, :], ACT.Copy)
                return eng.activation(v_pairs[:, t, :, 1, A_D:P], src[:, :, 1, :], ACT.Copy)
            return store

        slabs = [w_in[:, :, i * A_W:(i + 1) * A_W] for i in range(4)] + [w_in[:, :, COL_F:COL_F + A_H]]
        tiles = [(0, j * P, P, "f", copy_to(q_raw[:, j, :])) for j in range(N_A)]
        tiles += [(1, j * P, P, "f", copy_to(k_raw[:, j, :])) for j in range(N_A)]
        tiles += [(2, 0, A_W, t, store_v(t)) for t in range(NT)]
        tiles += [(3, j * P, P, "f", copy_to(z[:, j, :], func=ACT.Silu)) for j in range(N_A)]
        tiles += [(4, 0, A_H, "f", copy_to(f[0:A_H, :], w=A_H))]
        project(k, slabs, tiles, u)

        flat = lambda t: t[:, :, :].rearrange("p j s -> p (j s)")
        with k.stage("squared", "summed", "rstd_done", "scaled", "neg_abs", "exp_done", "act_chain", "vec_chain") as (
                block, squared, summed, rstd_done, scaled, neg_abs, exp_done, act_chain, vec_chain):

            @block.scalar
            def _(act):
                step = chain(act, act_chain)
                for n, src in enumerate((k_raw, q_raw)):
                    if n:
                        act.wait_ge(scaled, 1)
                    nc.scalar.activation(square, flat(src), ACT.Square).then_inc(squared, 1)
                    act.wait_ge(summed, n + 1)
                    step(nc.scalar.activation(square.rearrange("p (b s) -> p b s", b=2), k.ps[:, 0:2, :], ACT.Ln,
                                              bias=k.eps[:, 0:1]))
                    nc.scalar.activation(square, square, ACT.Exp, scale=-0.5).then_inc(rstd_done, 1)
                act.wait_ge(neg_abs, 1)
                nc.scalar.activation(small[0:A_H, 1, :], small[0:A_H, 1, :], ACT.Exp).then_inc(exp_done, 1)

            @block.tensor
            def _(pe):
                for n in range(2):
                    pe.wait_ge(squared, n + 1)
                    for b in range(2):
                        ins = nc.tensor.matmul(k.ps[:, b, :], k.const("mean_64"), square[:, b * 512:(b + 1) * 512],
                                               start=True, stop=True)
                    ins.then_inc(summed, 1)

            @block.vector
            def _(dve):
                step = chain(dve, vec_chain)
                y, e, w, w2 = (small[0:A_H, i, :] for i in range(4))
                step(nc.vector.tensor_scalar(y, f[0:A_H, :], k.forget_b[0:A_H, :], -1.0, ALU.add, ALU.mult))
                nc.vector.scalar_tensor_tensor(e, y, -1.0, y, ALU.mult, ALU.min).then_inc(neg_abs, 1)
                dve.wait_ge(rstd_done, 1)
                nc.vector.scalar_tensor_tensor(flat(k_raw), flat(k_raw), cols["k_norm"], square,
                                               ALU.mult, ALU.mult).then_inc(scaled, 1)
                step(nc.vector.tensor_scalar(cols["q_norm"], cols["q_norm"], A_D ** -0.5, None, ALU.mult))
                dve.wait_ge(rstd_done, 2)
                sq = square.rearrange("p (j s) -> p j s", j=N_A)
                for h in range(2):
                    r = slice(h * 64, h * 64 + 64)
                    nc.vector.scalar_tensor_tensor(q_pad[r, :, h, :], q_raw[r, :, :], cols["q_norm"][r, :],
                                                   sq[r, :, :], ALU.mult, ALU.mult)
                dve.wait_ge(exp_done, 1)
                log1p_steps(nc, step, f[0:A_H, :], e, w, w2)
                step(nc.vector.scalar_tensor_tensor(e, y, 0.0, f[0:A_H, :], ALU.max, ALU.add))
                step(nc.vector.tensor_scalar(e, e, -1.0, None, ALU.mult))
                step(nc.vector.tensor_tensor_scan(f[0:A_H, :], k.ones[0:A_H, :], e, 0.0, ALU.mult, ALU.add))

        spans = ((0, 0, P), (1, P, 3 * P))
        with k.stage("logits_done", "peak_done", "exps_done", "scaled", "turned", "copied", "out_done", "vec_chain") as (
                block, logits_done, peak_done, exps_done, scaled, turned, copied, out_done, vec_chain):

            @block.tensor
            def _(pe):
                for g in range(2):
                    if g:
                        pe.wait_ge(exps_done, 8)
                    for h in range(4 * g, 4 * g + 4):
                        for t, a, b in spans:
                            ps = k.ps[:, h % 4, a:b]
                            nc.tensor.matmul(ps, q_pad[:, h // 2, h % 2, t * P:(t + 1) * P], k_raw[:, h // 2, 0:b - a],
                                             start=True, stop=False)
                            nc.tensor.matmul(ps, k.first_const("pick_neg", h), f[:, 0:b - a], start=False, stop=False)
                            ins = nc.tensor.matmul(k.ps[:, h % 4, b - P:b], k.const("ident"), k.const("neg_upper"),
                                                   start=False, stop=True)
                        ins.then_inc(logits_done, 1)
                for g in range(2):
                    pe.wait_ge(scaled, g + 1)
                    if g:
                        pe.wait_ge(copied, 4)
                    for h in range(4 * g, 4 * g + 4):
                        for b in range(3):
                            ins = nc.tensor.transpose(k.ps[:, 4 + h % 4, b * P:(b + 1) * P],
                                                      probs[:, h, b * P:(b + 1) * P], k.const("ident"))
                        ins.then_inc(turned, 1)
                pe.wait_ge(copied, 8)
                for j in range(N_A):
                    for t in range(NT):
                        todo = [(h, s) for h in (2 * j, 2 * j + 1) for s in range(t + 1)]
                        for n, (h, s) in enumerate(todo):
                            c = (0, 1, 2)[t if s == 0 else 2]
                            ins = nc.tensor.matmul(k.ps[:, j, t * P:(t + 1) * P], v_pad[:, s, h, :],
                                                   probs_t[:, h, c * P:(c + 1) * P],
                                                   start=n == 0, stop=n == len(todo) - 1)
                ins.then_inc(out_done, 1)

            @block.scalar
            def _(act):
                for h in range(A_H):
                    act.wait_ge(peak_done, h + 1)
                    for t, a, b in spans:
                        nc.scalar.activation(probs[:, h, a:b], k.ps[:, h % 4, a:b], ACT.Exp, bias=peak[:, h, t:t + 1],
                                             accum_out=total[:, h, t:t + 1]).then_inc(exps_done, 1)

            @block.vector
            def _(dve):
                step = chain(dve, vec_chain)
                for h in range(A_H):
                    dve.wait_ge(logits_done, h + 1)
                    for t, a, b in spans:
                        ins = nc.vector.tensor_reduce(peak[:, h, t:t + 1], k.ps[:, h % 4, a:b], AX.X, ALU.max)
                    step(ins)
                    nc.vector.tensor_scalar(peak[:, h, :], peak[:, h, :], -1.0, None, ALU.mult).then_inc(peak_done, 1)
                for g in range(2):
                    heads = slice(4 * g, 4 * g + 4)
                    dve.wait_ge(exps_done, 8 * (g + 1))
                    step(nc.vector.reciprocal(total[:, heads, :], total[:, heads, :]))
                    for t, a, b in spans:
                        ins = nc.vector.tensor_tensor(probs[:, heads, a:b], probs[:, heads, a:b],
                                                      total[:, heads, t:t + 1].broadcast_to([P, 4, b - a]), ALU.mult)
                    ins.then_inc(scaled, 1)
                for h in range(A_H):
                    dve.wait_ge(turned, h + 1)
                    nc.vector.tensor_copy(probs_t[:, h, :], k.ps[:, 4 + h % 4, 0:3 * P]).then_inc(copied, 1)
                dve.wait_ge(out_done, 1)
                nc.vector.tensor_tensor(mix[:, 0:N_A, :], k.ps[:, 0:N_A, 0:S], z[:, :, :], ALU.mult)


def causal_conv(nc, dve, sem, n_tiles, src, dst, weights, bias, first=0):
    for i in range(TAPS):
        for j in range(n_tiles):
            if i:
                dve.wait_ge(sem, first + (i - 1) * n_tiles + j + 1)
                ins = nc.vector.scalar_tensor_tensor(dst[:, j, :], src[:, j, i:i + S], weights(i)[:, j:j + 1],
                                                     dst[:, j, :], ALU.mult, ALU.add)
            else:
                ins = nc.vector.tensor_scalar(dst[:, j, :], src[:, j, 0:S], weights(0)[:, j:j + 1],
                                              bias[:, j:j + 1], ALU.mult, ALU.add)
            ins.then_inc(sem, 1)


def ssd(k, cols, u, mix):
    nc, io = k.nc, k.io
    w_in = io["w_in"][0].rearrange("(k p) c -> p k c", p=P)
    with ExitStack() as mem:
        xc = k.sb("xc", [P, N_C, S], ctx=mem)
        z = k.sb("z_ssd", [P, N_X, S], ctx=mem)
        dt = k.sb("dt", [P, S], ctx=mem)
        cs = k.sb("a_cs", [P, S], ctx=mem)
        neg_cs = k.sb("neg_a_cs", [P, S], ctx=mem)
        with ExitStack() as tmp:
            raw = k.sb("xbc_raw", [P, N_C, S + TAPS - 1], ctx=tmp)
            small = k.sb("small_x", [P, 4, S], ctx=tmp)
            with k.stage("cleared") as (block, cleared):
                @block.gpsimd
                def _(pool):
                    nc.gpsimd.memset(raw[:, :, 0:TAPS - 1], 0.0)
                    for t in (dt, cs, neg_cs):
                        nc.gpsimd.memset(t[:, :], 0.0)

            slabs = [w_in[:, :, COL_XBC + i * 512:COL_XBC + (i + 1) * 512] for i in range(3)]
            slabs += [w_in[:, :, COL_DT:COL_DT + X_H]]
            slabs += [w_in[:, :, COL_ZX + i * 512:COL_ZX + (i + 1) * 512] for i in range(2)]
            tiles = [(j // 4, j % 4 * P, P, "f", copy_to(raw[:, j, TAPS - 1:])) for j in range(N_C)]
            tiles += [(3, 0, X_H, "f", copy_to(dt[0:X_H, :], w=X_H))]
            tiles += [(4 + j // 4, j % 4 * P, P, "f", copy_to(z[:, j, :], func=ACT.Silu)) for j in range(N_X)]
            project(k, slabs, tiles, u)

            with k.stage("conv_done", "neg_abs", "exp_done", "rate_done", "vec_chain") as (
                    block, conv_done, neg_abs, exp_done, rate_done, vec_chain):

                @block.scalar
                def _(act):
                    act.wait_ge(neg_abs, 1)
                    nc.scalar.activation(small[0:X_H, 1, :], small[0:X_H, 1, :], ACT.Exp).then_inc(exp_done, 1)
                    nc.scalar.activation(k.a_log[0:X_H, :], k.a_log[0:X_H, :], ACT.Exp).then_inc(rate_done, 1)
                    act.wait_ge(conv_done, TAPS * N_C)
                    nc.scalar.activation(xc[:, :, :], xc[:, :, :], ACT.Silu)

                @block.vector
                def _(dve):
                    step = chain(dve, vec_chain)
                    y, e, w, w2 = (small[0:X_H, i, :] for i in range(4))
                    step(nc.vector.tensor_scalar(y, dt[0:X_H, :], k.dt_bias[0:X_H, :], None, ALU.add))
                    nc.vector.scalar_tensor_tensor(e, y, -1.0, y, ALU.mult, ALU.min).then_inc(neg_abs, 1)
                    dve.wait_ge(exp_done, 1)
                    log1p_steps(nc, step, dt[0:X_H, :], e, w, w2)
                    step(nc.vector.scalar_tensor_tensor(dt[0:X_H, :], y, 0.0, dt[0:X_H, :], ALU.max, ALU.add))
                    dve.wait_ge(rate_done, 1)
                    step(nc.vector.tensor_scalar(e, dt[0:X_H, :], k.a_log[0:X_H, :], -1.0, ALU.mult, ALU.mult))
                    for c in range(NT):
                        r = slice(c * P, (c + 1) * P)
                        step(nc.vector.tensor_tensor_scan(cs[0:X_H, r], k.ones[0:X_H, 0:P], e[:, r], 0.0,
                                                          ALU.mult, ALU.add))
                    step(nc.vector.tensor_scalar(neg_cs[0:X_H, :], cs[0:X_H, :], -1.0, None, ALU.mult))
                    causal_conv(nc, dve, conv_done, N_C, raw, xc, lambda i: cols["ssd_w"][:, i * N_C:(i + 1) * N_C],
                                cols["ssd_b"])

        x_dt = k.sb("x_dt", [P, NT, X_H, P], ctx=mem)
        x_pairs = x_dt[:, :, :, :].rearrange("p t (j h) c -> p t j h c", h=2)
        x_dec = k.sb("x_dec", [P, X_W], ctx=mem)
        b_tok = k.sb("b_tok", [P, X_G, P], ctx=mem)
        cb = k.sb("cb", [P, X_G * NT, P], ctx=mem)
        state = k.sb("state_x", [P, X_G, 512], ctx=mem)
        y_off = k.sb("y_off", [P, N_X, P], ctx=mem)
        grow = k.sb("grow", [P, N_X, P], ctx=mem)
        dec = k.sb("dec", [P, P], ctx=mem)
        dt_tok = k.sb("dt_tok", [P, 3, X_H], ctx=mem)
        with k.stage("dec_done", "dt_turned", "dt_copied", "turned", "x_copied", "cb_done", "cb_copied", "state_done",
                     "state_copied", "off_done", "grow_done", "cleared", "vec_chain") as (
                block, dec_done, dt_turned, dt_copied, turned, x_copied, cb_done, cb_copied, state_done,
                state_copied, off_done, grow_done, cleared, vec_chain):

            @block.gpsimd
            def _(pool):
                nc.gpsimd.memset(x_dt[:, :, :, :], 0.0).then_inc(cleared, 1)
                nc.gpsimd.memset(dec[:, :], 0.0).then_inc(cleared, 1)

            @block.scalar
            def _(act):
                act.wait_ge(cleared, 2)
                nc.scalar.activation(dec[0:X_H, :], cs[0:X_H, 0:P], ACT.Exp, bias=cs[0:X_H, P - 1:P],
                                     scale=-1.0).then_inc(dec_done, 1)
                act.wait_ge(cb_done, 1)
                nc.scalar.activation(cb[:, :, :], k.ps[:, 1, :].rearrange("p (n c) -> p n c", c=P), ACT.Copy)
                act.wait_ge(state_done, 1)
                nc.scalar.activation(state[:, :, :], k.ps[:, 2:4, :], ACT.Copy).then_inc(state_copied, 1)
                act.wait_ge(off_done, 2)
                nc.scalar.activation(grow[:, :, :].rearrange("p (b j) c -> p b (j c)", b=2), k.ps[:, 6:8, :],
                                     ACT.Exp).then_inc(grow_done, 1)

            @block.tensor
            def _(pe):
                pe.wait_ge(dec_done, 2)
                for n, src in enumerate((dt[:, 0:P], dt[:, P:S], dec[:, :])):
                    ins = nc.tensor.transpose(k.ps[:, 0, n * P:(n + 1) * P], src, k.const("ident"))
                ins.then_inc(dt_turned, 1)
                for g in range(X_G):
                    for c in range(NT):
                        r = slice(c * P, (c + 1) * P)
                        n = g * NT + c
                        ins = nc.tensor.matmul(k.ps[:, 1, n * P:(n + 1) * P], xc[:, N_X + g, r],
                                               xc[:, N_X + X_G + g, r], start=True, stop=True)
                ins.then_inc(cb_done, 1)
                for t in range(NT):
                    if t:
                        pe.wait_ge(x_copied, t)
                    for j in range(N_X):
                        ins = nc.tensor.transpose(k.ps[:, 4 + j // 4, j % 4 * P:(j % 4 + 1) * P],
                                                  xc[:, j, t * P:(t + 1) * P], k.const("ident"))
                    ins.then_inc(turned, 1)
                for g in range(X_G):
                    ins = nc.tensor.transpose(k.ps[:, 6, g * P:(g + 1) * P], xc[:, N_X + g, 0:P], k.const("ident"))
                ins.then_inc(turned, 1)
                pe.wait_ge(x_copied, 3)
                for g in range(X_G):
                    ins = nc.tensor.matmul(k.ps[:, 2 + g, :], b_tok[:, g, :], x_dec[:, g * 512:(g + 1) * 512],
                                           start=True, stop=True)
                ins.then_inc(state_done, 1)
                pe.wait_ge(state_copied, 1)
                for j in range(N_X):
                    ins = nc.tensor.matmul(k.ps[:, 4 + j // 4, j % 4 * P:(j % 4 + 1) * P],
                                           state[:, j // 4, j % 4 * P:(j % 4 + 1) * P],
                                           xc[:, N_X + X_G + j // 4, P:S], start=True, stop=True)
                ins.then_inc(off_done, 1)
                for j in range(N_X):
                    ins = nc.tensor.matmul(k.ps[:, 6 + j // 4, j % 4 * P:(j % 4 + 1) * P],
                                           k.first_const("pick_pair", j), cs[:, P:S], start=True, stop=True)
                ins.then_inc(off_done, 1)

            @block.vector
            def _(dve):
                step = chain(dve, vec_chain)
                dve.wait_ge(dec_done, 1)
                nc.vector.tensor_tensor(dec[0:X_H, :], dec[0:X_H, :], dt[0:X_H, 0:P], ALU.mult).then_inc(dec_done, 1)
                dve.wait_ge(dt_turned, 1)
                step(nc.vector.tensor_copy(dt_tok[:, :, :], k.ps[:, 0, 0:3 * P].rearrange("p (n c) -> p n c", c=P)[:, :, 0:X_H]))
                dve.wait_ge(cleared, 2)
                for t in range(NT):
                    dve.wait_ge(turned, t + 1)
                    src = k.ps[:, 4:6, :].rearrange("p b (j h c) -> p (b j) h c", h=2, c=X_D)
                    by = dt_tok[:, t, :].rearrange("p (j h) -> p j h", h=2)
                    if t == 0:
                        by_dec = dt_tok[:, 2, :].rearrange("p (j h) -> p j h", h=2)
                        out = x_dec[:, :].rearrange("p (j h c) -> p j h c", h=2, c=X_D)
                        for h in range(2):
                            nc.vector.tensor_tensor(out[:, :, h, :], src[:, :, h, :],
                                                    by_dec[:, :, h:h + 1].broadcast_to([P, N_X, X_D]), ALU.mult)
                    for h in range(2):
                        ins = nc.vector.tensor_tensor(x_pairs[:, t, :, h, h * X_D:(h + 1) * X_D], src[:, :, h, :],
                                                      by[:, :, h:h + 1].broadcast_to([P, N_X, X_D]), ALU.mult)
                    ins.then_inc(x_copied, 1)
                dve.wait_ge(turned, 3)
                nc.vector.tensor_copy(b_tok[:, :, :], k.ps[:, 6, 0:X_G * P].rearrange("p (g c) -> p g c", g=X_G)).then_inc(x_copied, 1)
                dve.wait_ge(grow_done, 1)
                nc.vector.tensor_tensor(y_off[:, :, :], k.ps[:, 4:6, :].rearrange("p b (j c) -> p (b j) c", c=P),
                                        grow[:, :, :], ALU.mult)

        lmat = k.sb("lmat", [P, 2, 4, P], ctx=mem)
        rounds = [(c, q) for c in range(NT) for q in range(4)]
        with k.stage("seg_done", "lmat_done", "masked", "y_done", "y_stored", "squared", "summed", "ln_done",
                     "rstd_done", "vec_chain", "gated") as (
                block, seg_done, lmat_done, masked, y_done, y_stored, squared, summed, ln_done, rstd_done,
                vec_chain, gated):
            rstd = grow[:, 0:4, :].rearrange("p (g t) c -> p g (t c)", g=X_G)
            sq = x_dec[:, :].rearrange("p (j s) -> p j s", s=S)

            @block.tensor
            def _(pe):
                def segments(n):
                    c, q = rounds[n]
                    r = slice(c * P, (c + 1) * P)
                    if n >= 2:
                        pe.wait_ge(lmat_done, n - 1)
                    for i in range(4):
                        h = 4 * q + i
                        ps = k.ps[:, n % 2, i * P:(i + 1) * P]
                        nc.tensor.matmul(ps, k.first_const("pick", h), cs[:, r], start=True, stop=False)
                        nc.tensor.matmul(ps, neg_cs[:, r], k.first_const("pick", h), start=False, stop=False)
                        ins = nc.tensor.matmul(ps, k.const("ident"), k.const("neg_lower"), start=False, stop=True)
                    ins.then_inc(seg_done, 1)

                segments(0)
                for n, (c, q) in enumerate(rounds):
                    if n + 1 < len(rounds):
                        segments(n + 1)
                    pe.wait_ge(masked, n + 1)
                    if n >= 2:
                        pe.wait_ge(y_stored, n - 1)
                    for j in range(2):
                        for i in range(2):
                            h = 4 * q + 2 * j + i
                            ins = nc.tensor.matmul(k.ps[:, 2 + n % 2, j * P:(j + 1) * P], x_dt[:, c, h, :],
                                                   lmat[:, n % 2, 2 * j + i, :], start=i == 0, stop=i == 1)
                    ins.then_inc(y_done, 1)
                for g in range(X_G):
                    pe.wait_ge(squared, g + 1)
                    for j in range(4):
                        ins = nc.tensor.matmul(k.ps[:, 4 + g, 0:S], k.const("mean_512"), sq[:, j, :],
                                               start=j == 0, stop=j == 3)
                    ins.then_inc(summed, 1)

            @block.scalar
            def _(act):
                for n in range(len(rounds)):
                    act.wait_ge(seg_done, n + 1)
                    if n >= 2:
                        act.wait_ge(y_done, n - 1)
                    nc.scalar.activation(lmat[:, n % 2, :, :].rearrange("p i c -> p (i c)"), k.ps[:, n % 2, :],
                                         ACT.Exp).then_inc(lmat_done, 1)
                act.wait_ge(gated, 1)
                for g in range(X_G):
                    if g:
                        act.wait_ge(summed, g)
                    nc.scalar.activation(sq, mix[:, N_A + 4 * g:N_A + 4 * g + 4, :], ACT.Square).then_inc(squared, 1)
                act.wait_ge(summed, 2)
                nc.scalar.activation(rstd, k.ps[:, 4:6, 0:S], ACT.Ln, bias=k.eps[:, 0:1]).then_inc(ln_done, 1)
                act.wait_ge(ln_done, 1)
                nc.scalar.activation(rstd, rstd, ACT.Exp, scale=-0.5).then_inc(rstd_done, 1)

            @block.vector
            def _(dve):
                for n, (c, q) in enumerate(rounds):
                    g = q // 2
                    dve.wait_ge(lmat_done, n + 1)
                    nc.vector.tensor_tensor(lmat[:, n % 2, :, :], lmat[:, n % 2, :, :],
                                            cb[:, g * NT + c:g * NT + c + 1, :].broadcast_to([P, 4, P]), ALU.mult
                                            ).then_inc(masked, 1)
                    dve.wait_ge(y_done, n + 1)
                    r = slice(c * P, (c + 1) * P)
                    for i in range(2):
                        j = 2 * q + i
                        ins = nc.vector.scalar_tensor_tensor(mix[:, N_A + j, r], xc[:, j, r], cols["ssd_d"][:, j:j + 1],
                                                             k.ps[:, 2 + n % 2, i * P:(i + 1) * P], ALU.mult, ALU.add)
                    ins.then_inc(y_stored, 1)
                dve.wait_ge(y_stored, len(rounds))
                y = mix[:, N_A:N_A + N_X, :]
                step = chain(dve, vec_chain)
                step(nc.vector.tensor_tensor(y[:, :, P:S], y[:, :, P:S], y_off[:, :, :], ALU.add))
                nc.vector.tensor_tensor(y, y, z[:, :, :], ALU.mult).then_inc(gated, 1)
                dve.wait_ge(rstd_done, 1)
                for j in range(N_X):
                    nc.vector.scalar_tensor_tensor(y[:, j, :], y[:, j, :], cols["ssd_g"][:, j:j + 1],
                                                   rstd[:, j // 4, :], ALU.mult, ALU.mult)


def lru(k, cols, u, mix):
    nc, io = k.nc, k.io
    w_in = io["w_in"][0].rearrange("(k p) c -> p k c", p=P)
    with ExitStack() as mem:
        raw = k.sb("lru_raw", [P, N_L, S + TAPS - 1], ctx=mem)
        z = k.sb("z_lru", [P, N_L, S], ctx=mem)
        xc = k.sb("lru_xc", [P, N_L, S], ctx=mem)
        r = k.sb("lru_r", [P, N_L, S], ctx=mem)
        gate = k.sb("lru_i", [P, N_L, S], ctx=mem)
        a = k.sb("lru_a", [P, N_L, S], ctx=mem)
        t = k.sb("lru_t", [P, N_L, S], ctx=mem)
        w = k.sb("lru_w", [P, 2, N_L, P], ctx=mem)
        small = k.sb("small_l", [P, 5, N_L], ctx=mem)

        with k.stage("cleared", "weights_loaded") as (block, cleared, weights_loaded):
            @block.gpsimd
            def _(pool):
                nc.gpsimd.memset(raw[:, :, 0:TAPS - 1], 0.0)
                nc.gpsimd.memset(w[:, :, :, :], 0.0).then_inc(cleared, 1)

            @block.sync
            def _(sp):
                sp.wait_ge(cleared, 1)
                for n, name in enumerate(("lru_w_a", "lru_w_x")):
                    for h in range(2):
                        src = io[name][0].rearrange("(j h) d e -> h d j e", h=2)[h]
                        sp.dma_start(w[h * 64:h * 64 + 64, n, :, h * 64:h * 64 + 64], src).then_inc(weights_loaded, 16)
                sp.wait_ge(weights_loaded, 64)

        slabs = [w_in[:, :, COL_XL:COL_XL + L_W], w_in[:, :, COL_ZL:COL_ZL + L_W]]
        tiles = [(0, j * P, P, "f", copy_to(raw[:, j, TAPS - 1:])) for j in range(N_L)]
        tiles += [(1, j * P, P, "f", copy_to(z[:, j, :], func=ACT.Silu)) for j in range(N_L)]
        project(k, slabs, tiles, u)

        with k.stage("conv_done", "gates_done", "sigmoids_done", "neg_abs", "exp_done", "rate_done", "a_done",
                     "tanh_done", "square_done", "root_done", "act_chain", "vec_chain") as (
                block, conv_done, gates_done, sigmoids_done, neg_abs, exp_done, rate_done, a_done, tanh_done,
                square_done, root_done, act_chain, vec_chain):

            @block.scalar
            def _(act):
                act.wait_ge(neg_abs, 1)
                nc.scalar.activation(small[:, 1, :], small[:, 1, :], ACT.Exp).then_inc(exp_done, 1)
                act.wait_ge(gates_done, 1)
                for n, (dst, b) in enumerate(((r, "lru_b_a"), (gate, "lru_b_x"))):
                    for j in range(N_L):
                        at = (4 * n + j) * S
                        src = k.ps[:, at // 512, at % 512:at % 512 + S]
                        nc.scalar.activation(dst[:, j, :], src, ACT.Sigmoid, bias=cols[b][:, j:j + 1]
                                             ).then_inc(sigmoids_done, 1)
                act.wait_ge(rate_done, 1)
                nc.scalar.activation(t[:, :, :], r[:, :, :], ACT.Tanh).then_inc(tanh_done, 1)
                nc.scalar.activation(a[:, :, :], r[:, :, :], ACT.Exp, scale=-1.0).then_inc(a_done, 1)
                act.wait_ge(square_done, 1)
                nc.scalar.activation(t[:, :, :], t[:, :, :], ACT.Sqrt).then_inc(root_done, 1)

            @block.tensor
            def _(pe):
                pe.wait_ge(conv_done, TAPS * N_L)
                for n in range(2):
                    for j in range(N_L):
                        at = (4 * n + j) * S
                        ins = nc.tensor.matmul(k.ps[:, at // 512, at % 512:at % 512 + S], w[:, n, j, :], xc[:, j, :],
                                               start=True, stop=True)
                ins.then_inc(gates_done, 1)

            @block.vector
            def _(dve):
                step = chain(dve, vec_chain)
                sp, e, w1, w2, rate = (small[:, i, :] for i in range(5))
                step(nc.vector.tensor_scalar(rate, cols["lru_lambda"], -1.0, None, ALU.mult))
                nc.vector.scalar_tensor_tensor(e, rate, -1.0, rate, ALU.mult, ALU.min).then_inc(neg_abs, 1)
                causal_conv(nc, dve, conv_done, N_L, raw, xc, lambda i: cols["lru_w"][:, i * N_L:(i + 1) * N_L],
                            cols["lru_b"])
                dve.wait_ge(exp_done, 1)
                log1p_steps(nc, step, sp, e, w1, w2)
                step(nc.vector.scalar_tensor_tensor(rate, rate, 0.0, sp, ALU.max, ALU.add))
                step(nc.vector.tensor_scalar(rate, rate, 8.0, None, ALU.mult))
                dve.wait_ge(sigmoids_done, 2 * N_L)
                for j in range(N_L):
                    ins = nc.vector.tensor_scalar(r[:, j, :], r[:, j, :], rate[:, j:j + 1], None, ALU.mult)
                ins.then_inc(rate_done, 1)
                step(nc.vector.tensor_tensor(gate[:, :, :], gate[:, :, :], xc[:, :, :], ALU.mult))
                dve.wait_ge(a_done, 1)
                step(nc.vector.tensor_scalar(r[:, :, :], t[:, :, :], 1.0, None, ALU.add))
                step(nc.vector.reciprocal(r[:, :, :], r[:, :, :]))
                nc.vector.scalar_tensor_tensor(t[:, :, :], t[:, :, :], 2.0, r[:, :, :], ALU.mult, ALU.mult).then_inc(square_done, 1)
                dve.wait_ge(root_done, 1)
                step(nc.vector.memset(t[:, :, 0:1], 1.0))
                step(nc.vector.tensor_tensor(gate[:, :, :], gate[:, :, :], t[:, :, :], ALU.mult))
                for j in range(N_L):
                    ins = nc.vector.tensor_tensor_scan(r[:, j, :], a[:, j, :], gate[:, j, :], 0.0, ALU.mult, ALU.add)
                step(ins)
                nc.vector.tensor_tensor(mix[:, N_A + N_X:, :], r[:, :, :], z[:, :, :], ALU.mult)


def add_product(k, slabs, tiles, rhs, gain=None):
    def store(j):
        def put(eng, ps):
            if gain is None:
                return eng.tensor_tensor(k.x[:, j, :], k.x[:, j, :], ps[:, 0:S], ALU.add)
            return eng.scalar_tensor_tensor(k.x[:, j, :], ps[:, 0:S], gain[:, j:j + 1], k.x[:, j, :],
                                            ALU.mult, ALU.add)
        return put
    project(k, slabs, [(i, c, P, "f", store(j)) for i, c, j in tiles], rhs, evac_engine="vector")


def first_block(k):
    nc, io = k.nc, k.io
    with ExitStack() as mem:
        pieces, n = layout(first_constants())
        buf = k.sb("first_constants", [P, n], ctx=mem)
        k.first_const = lambda name, h: buf[:, pieces[name][0] + h * P:pieces[name][0] + (h + 1) * P]
        k.forget_b = k.sb("forget_b", [P, 1], ctx=mem)
        k.dt_bias = k.sb("dt_bias", [P, 1], ctx=mem)
        k.a_log = k.sb("a_log", [P, 1], ctx=mem)
        d_head = k.sb("d_head", [P, 1], ctx=mem)
        d_pairs = k.sb("d_pairs", [P, N_X], ctx=mem)
        with k.stage("cleared", "params_loaded", "spread") as (block, cleared, loaded, spread):
            @block.gpsimd
            def _(pool):
                nc.gpsimd.memset(d_head[:, :], 0.0).then_inc(cleared, 1)

            @block.tensor
            def _(pe):
                pe.wait_ge(loaded, 16 * 5)
                for j in range(N_X):
                    ins = nc.tensor.matmul(k.ps[:, 0, j:j + 1], k.first_const("pick_pair", j), d_head[:, :],
                                           start=True, stop=True)
                ins.then_inc(spread, 1)

            @block.vector
            def _(dve):
                dve.wait_ge(spread, 1)
                nc.vector.tensor_copy(d_pairs[:, :], k.ps[:, 0, 0:N_X])

            @block.sync
            def _(sp):
                sp.wait_ge(cleared, 1)
                sp.dma_start(buf[:, :], io["first_constants"]).then_inc(loaded, 16)
                for dst, src, m in ((k.forget_b, "forget_b", A_H), (k.dt_bias, "ssd_dt_bias", X_H),
                                    (k.a_log, "ssd_a_log", X_H), (d_head, "ssd_d", X_H)):
                    sp.dma_start(dst[0:m, :], io[src][0].rearrange("(h o) -> h o", o=1)).then_inc(loaded, 16)
                sp.wait_ge(loaded, 16 * 5)
        tile_rows = lambda ap: ap.rearrange("(r c) -> r c", c=P)
        row = lambda name: tile_rows(io[name][0])
        taps = lambda name: [(0, io[name][0].rearrange("i (r c) -> (i r) c", c=P))]
        head = lambda name: [(0, io[name]), (A_D, io[name])]
        cols = load_rows(k, [
            ("norm", ND, [(0, row("norm_g"))]), ("q_norm", 1, head("q_norm_g")), ("k_norm", 1, head("k_norm_g")),
            ("ssd_w", TAPS * N_C, taps("ssd_conv_w")), ("ssd_b", N_C, [(0, row("ssd_conv_b"))]),
            ("ssd_g", N_X, [(0, row("ssd_norm_g"))]), ("lru_w", TAPS * N_L, taps("lru_conv_w")),
            ("lru_b", N_L, [(0, row("lru_conv_b"))]), ("lru_b_a", N_L, [(0, row("lru_b_a"))]),
            ("lru_b_x", N_L, [(0, row("lru_b_x"))]), ("lru_lambda", N_L, [(0, row("lru_lambda"))]),
        ])
        cols["ssd_d"] = d_pairs[:, :]
        mix = k.sb("mix", [P, MIX // P, S], ctx=mem)
        with ExitStack() as tmp:
            u = k.sb("u", [P, ND, S], ctx=tmp)
            rms_norm(k, k.x[:, :, :], u[:, :, :], cols["norm"])
            attention(k, cols, u, mix)
            k.clear_semaphores()
            ssd(k, cols, u, mix)
            k.clear_semaphores()
            lru(k, cols, u, mix)
        w_out = io["w_out"][0].rearrange("(k p) c -> p k c", p=P)
        add_product(k, [w_out[:, :, i * 2 * P:(i + 1) * 2 * P] for i in range(4)],
                    [(j // 2, j % 2 * P, j) for j in range(ND)], mix)
        k.clear_semaphores()



def rotation_tables(k):
    nc, io = k.nc, k.io
    parts = [6.28125]
    parts.append(float(np.float32(round((2 * math.pi - parts[0]) * 2 ** 21) / 2 ** 21)))
    parts.append(2 * math.pi - parts[0] - parts[1])
    magic = 1.5 * 2 ** 23
    with ExitStack() as mem:
        pos = k.sb("pos", [P, S], I32, ctx=mem)
        angle = k.sb("angle", [P, S], ctx=mem)
        turns = k.sb("turns", [P, S], ctx=mem)
        with k.stage("pos_loaded", "reduced", "vec_chain") as (block, pos_loaded, reduced, vec_chain):

            @block.sync
            def _(sp):
                src = io["positions_2"][0].rearrange("(o s) -> o s", o=1)
                sp.dma_start(pos[:, :], src.broadcast_to([P, S])).then_inc(pos_loaded, 16)

            @block.vector
            def _(dve):
                step = chain(dve, vec_chain)
                dve.wait_ge(pos_loaded, 16)
                step(nc.vector.tensor_copy(angle[:, :], pos[:, :]))
                step(nc.vector.tensor_scalar(angle[:, :], angle[:, :], k.const("inv_freq"), None, ALU.mult))
                for n, (dst, quarter) in enumerate(((k.sin, 0.0), (k.cos, 0.25))):
                    step(nc.vector.tensor_scalar(turns[:, :], angle[:, :], 1 / (2 * math.pi), quarter, ALU.mult, ALU.add))
                    step(nc.vector.tensor_scalar(turns[:, :], turns[:, :], magic, magic, ALU.add, ALU.subtract))
                    src = angle
                    for part in parts:
                        step(nc.vector.scalar_tensor_tensor(dst[:, :], turns[:, :], -part, src[:, :], ALU.mult, ALU.add))
                        src = dst
                    step(nc.vector.tensor_scalar(dst[:, :], dst[:, :], quarter * 2 * math.pi, 3.1415925, ALU.add, ALU.min))
                    nc.vector.tensor_scalar(dst[:, :], dst[:, :], -3.1415925, None, ALU.max).then_inc(reduced, 1)

            @block.scalar
            def _(act):
                for n, dst in enumerate((k.sin, k.cos)):
                    act.wait_ge(reduced, n + 1)
                    nc.scalar.activation(dst[:, :], dst[:, :], ACT.Sin)


def ada_modulation(k, l, cols):
    nc, io = k.nc, k.io
    w = io["w_ada_2"].rearrange("l (k p) c -> l p k c", p=P)
    n_slabs = 6 * D // 512
    slabs = [w[l, :, :, i * 512:(i + 1) * 512] for i in range(n_slabs)]
    with k.stage(*LOADED, "slab_used", "mod_chain") as (block, *sems):
        loaded, (used, mod_chain) = sems[:SLOTS], sems[SLOTS:]

        @block.sync
        def _(sp):
            load_slabs(sp, k, slabs, loaded, used, [1] * n_slabs)

        @block.tensor
        def _(pe):
            for i in range(n_slabs):
                wait_slab(pe, loaded, i)
                slab = slab_view(k, i % SLOTS, D, 512)
                for c in range(4):
                    for j in range(ND):
                        ins = nc.tensor.matmul(k.ps[:, 0, 4 * i + c:4 * i + c + 1], slab[:, j, c * P:(c + 1) * P],
                                               k.c_silu[:, j:j + 1], start=j == 0, stop=j == ND - 1)
                ins.then_inc(used, 1)

        @block.vector
        def _(dve):
            step = chain(dve, mod_chain)
            dve.wait_ge(used, n_slabs)
            step(nc.vector.tensor_tensor(k.mod[:, :], k.ps[:, 0, 0:6 * ND], cols["b_ada"], ALU.add))
            for n, name in enumerate(("norm1", "norm2")):
                scale = k.mod[:, (3 * n + 1) * ND:(3 * n + 2) * ND]
                nc.vector.scalar_tensor_tensor(scale, scale, 1.0, cols[name], ALU.add, ALU.mult)


def branch_projections(k, l, h, p, pr):
    nc, io = k.nc, k.io
    w = io["w_in_2"].rearrange("l (k p) c -> l p k c", p=P)
    slabs = [w[l, :, :, i * 512:min((i + 1) * 512, IN_COLS)] for i in range((IN_COLS + 511) // 512)]
    tiles = []
    for j in range(IN_COLS // P):
        i, c = j // 4, j % 4 * P
        if i == 2:
            if j % 4 < NT:
                at = 8 * S + j % 4 * MW
                dst = p[:, :, :].rearrange("p j s -> p (j s)")[:, at:at + MW]
                tiles.append((i, 0, MW, j % 4, copy_to(dst, n=MW)))
        elif j < 4 * N_M:
            tiles.append((i, c, P, "f", copy_to(p[:, j, :], func=ACT.Silu if i == 3 else ACT.Copy)))
        elif j < 4 * N_M + N_K:
            tiles.append((i, c, P, "f", copy_to(pr[:, j - 4 * N_M, 1:])))
        else:
            tiles.append((i, c, P, "f", copy_to(p[:, j - N_K, :])))
    with k.stage("cleared") as (block, cleared):
        @block.gpsimd
        def _(pool):
            nc.gpsimd.memset(pr[:, :, 0:1], 0.0)
    project(k, slabs, tiles, h)


def retention_and_conv(k, cols, p, y_ret, y_conv):
    nc = k.nc
    with ExitStack() as mem:
        rot = k.sb("rotated", [P, 8, S], ctx=mem)
        tmp = k.sb("rot_tmp", [P, 8, S], ctx=mem)
        sc = k.sb("ret_scores", [P, R_H, 3 * P], ctx=mem)
        conv_in = k.sb("conv_in", [P, N_M, S + 2], ctx=mem)
        y = tmp[:, 0:4, :].rearrange("p j s -> p (j s)")
        sq = tmp[:, 4:8, :].rearrange("p j s -> p (j s)")
        rstd = rot[:, 0:4, :].rearrange("p j s -> p (j s)")
        banks = lambda a: a.rearrange("p (b s) -> p b s", b=2)
        v = p[:, 8:12, :].rearrange("p j s -> p (j s)").rearrange("p (t c) -> p t c", t=NT)
        with k.stage("swapped", "rotated", "scores_done", "decayed", "out_done", "out_stored", "mean_done", "centred",
                     "squared", "var_done", "ln_done", "rstd_done", "cleared", "vec_chain") as (
                block, swapped, rotated, scores_done, decayed, out_done, out_stored, mean_done, centred,
                squared, var_done, ln_done, rstd_done, cleared, vec_chain):

            @block.gpsimd
            def _(pool):
                nc.gpsimd.memset(conv_in[:, :, 0:2], 0.0).then_inc(cleared, 1)

            @block.tensor
            def _(pe):
                flat = p[:, :, :].rearrange("p j s -> p (j s)")
                for b in range(4):
                    ins = nc.tensor.matmul(k.ps[:, b, :], k.const("swap"), flat[:, b * 512:(b + 1) * 512],
                                           start=True, stop=True)
                ins.then_inc(swapped, 1)
                pe.wait_ge(rotated, 1)
                for h in range(R_H):
                    nc.tensor.matmul(k.ps[:, 4 + h, 0:S], rot[:, R_H + h, 0:P], rot[:, h, :], start=True, stop=True)
                    ins = nc.tensor.matmul(k.ps[:, 4 + h, S:S + P], rot[:, R_H + h, P:S], rot[:, h, P:S],
                                           start=True, stop=True)
                ins.then_inc(scores_done, 1)
                pe.wait_ge(decayed, 1)
                for h in range(R_H):
                    c = slice(h * P, (h + 1) * P)
                    ps = k.ps[:, h // 2, h % 2 * S:h % 2 * S + S]
                    nc.tensor.matmul(ps[:, 0:P], v[:, 0, c], sc[:, h, 0:P], start=True, stop=True)
                    nc.tensor.matmul(ps[:, P:S], v[:, 0, c], sc[:, h, P:S], start=True, stop=False)
                    ins = nc.tensor.matmul(ps[:, P:S], v[:, 1, c], sc[:, h, S:S + P], start=False, stop=True)
                ins.then_inc(out_done, 1)
                pe.wait_ge(out_stored, 1)
                for b in range(2):
                    ins = nc.tensor.matmul(k.ps[:, 2 + b, :], k.const("mean_128"), y[:, b * 512:(b + 1) * 512],
                                           start=True, stop=True)
                ins.then_inc(mean_done, 1)
                pe.wait_ge(squared, 1)
                for b in range(2):
                    ins = nc.tensor.matmul(k.ps[:, 4 + b, :], k.const("mean_128"), sq[:, b * 512:(b + 1) * 512],
                                           start=True, stop=True)
                ins.then_inc(var_done, 1)

            @block.scalar
            def _(act):
                act.wait_ge(out_done, 1)
                nc.scalar.activation(banks(y), k.ps[:, 0:2, :], ACT.Copy).then_inc(out_stored, 1)
                act.wait_ge(centred, 1)
                nc.scalar.activation(sq, y, ACT.Square).then_inc(squared, 1)
                act.wait_ge(var_done, 1)
                nc.scalar.activation(banks(rstd), k.ps[:, 4:6, :], ACT.Ln, bias=k.eps[:, 1:2]).then_inc(ln_done, 1)
                act.wait_ge(ln_done, 1)
                nc.scalar.activation(rstd, rstd, ACT.Exp, scale=-0.5).then_inc(rstd_done, 1)

            @block.vector
            def _(dve):
                step = chain(dve, vec_chain)
                table = lambda t: t[:, :].rearrange("p (o s) -> p o s", o=1).broadcast_to([P, 8, S])
                nc.vector.tensor_tensor(rot[:, :, :], p[:, 0:8, :], table(k.cos), ALU.mult)
                dve.wait_ge(swapped, 1)
                step(nc.vector.tensor_tensor(tmp[:, :, :], k.ps[:, 0:4, :].rearrange("p b (j s) -> p (b j) s", s=S),
                                             table(k.sin), ALU.mult))
                nc.vector.tensor_tensor(rot[:, :, :], rot[:, :, :], tmp[:, :, :], ALU.add).then_inc(rotated, 1)
                dve.wait_ge(scores_done, 1)
                at = k.columns["decay_0"][0]
                decay = k.consts[:, at:at + R_H * S].rearrange("p (h s) -> p h s", h=R_H)
                nc.vector.tensor_tensor(sc[:, :, 0:S], k.ps[:, 4:8, 0:S], decay, ALU.mult)
                nc.vector.tensor_tensor(sc[:, :, S:S + P], k.ps[:, 4:8, S:S + P], decay[:, :, 0:P],
                                        ALU.mult).then_inc(decayed, 1)
                dve.wait_ge(cleared, 1)
                base = 4 * N_M
                step(nc.vector.tensor_tensor(conv_in[:, :, 2:], p[:, base:base + N_M, :],
                                             p[:, base + 2 * N_M:base + 3 * N_M, :], ALU.mult))
                for i in range(3):
                    for j in range(N_M):
                        w = cols["conv_w"][:, i * N_M + j:i * N_M + j + 1]
                        if i == 0:
                            ins = nc.vector.tensor_scalar(y_conv[:, j, :], conv_in[:, j, 0:S], w, None, ALU.mult)
                        else:
                            ins = nc.vector.scalar_tensor_tensor(y_conv[:, j, :], conv_in[:, j, i:i + S], w,
                                                                 y_conv[:, j, :], ALU.mult, ALU.add)
                        if j == N_M - 1:
                            step(ins)
                nc.vector.tensor_tensor(y_conv, y_conv, p[:, base + N_M:base + 2 * N_M, :], ALU.mult)
                dve.wait_ge(mean_done, 1)
                nc.vector.tensor_tensor(banks(y), banks(y), k.ps[:, 2:4, :], ALU.subtract).then_inc(centred, 1)
                dve.wait_ge(rstd_done, 1)
                step(nc.vector.tensor_tensor(y, y, rstd, ALU.mult))
                for h in range(R_H):
                    nc.vector.scalar_tensor_tensor(y_ret[:, h, :], tmp[:, h, :], cols["ret_g"][:, h:h + 1],
                                                   p[:, 12 + h, :], ALU.mult, ALU.mult)


def rwkv(k, cols, pr, y_out):
    nc = k.nc
    with ExitStack() as mem:
        g = k.sb("rwkv_gate", [P, N_M, S], ctx=mem)
        bonus = k.sb("bonus", [P, N_M, S], ctx=mem)
        ar = k.sb("alpha_rho", [P, N_M, 2, 2, S], ctx=mem)
        kap = k.sb("kappa", [P, N_M, S], ctx=mem)
        bet = k.sb("beta", [P, N_M, S], ctx=mem)
        v_pad = k.sb("rwkv_v", [P, NT, K_H, P], ctx=mem)
        ends = k.sb("chunk_ends", [P, 4, N_M], ctx=mem)
        pf = pr[:, :, 1:]
        with ExitStack() as tmp:
            work = k.sb("work", [P, N_K, S], ctx=tmp)
            a = k.sb("rwkv_a", [P, N_M, S], ctx=tmp)
            kh = k.sb("k_hat", [P, N_M, S], ctx=tmp)
            e = k.sb("decays", [P, N_M, S], ctx=tmp)
            sw, cs, dm = work[:, 0:4, :], work[:, 4:8, :], work[:, 8:12, :]
            flat = lambda t: t.rearrange("p j s -> p (j s)")
            two = lambda b: k.ps[:, b:b + 2, :].rearrange("p b (j s) -> p (b j) s", j=2)
            pair_ps = lambda b, j: k.ps[:, b + j // 2, j % 2 * S:j % 2 * S + S]
            halves = [(h, slice(h * 64, h * 64 + 64)) for h in range(2)]
            with k.stage("cleared", "shifted", "squashed", "w_done", "w_sig", "a_done", "a_sig", "g_done", "g_stored",
                         "kk_done", "kk_sq", "kk_sum", "kk_clamped", "kk_ln", "kk_rstd", "cs_done", "exps", "used",
                         "bonus_in", "bonus_sum", "v_turned", "vec_chain") as (
                    block, cleared, shifted, squashed, w_done, w_sig, a_done, a_sig, g_done, g_stored,
                    kk_done, kk_sq, kk_sum, kk_clamped, kk_ln, kk_rstd, cs_done, exps, used,
                    bonus_in, bonus_sum, v_turned, vec_chain):

                @block.gpsimd
                def _(pool):
                    nc.gpsimd.memset(ar[:, :, :, :, :], 0.0).then_inc(cleared, 1)
                    nc.gpsimd.memset(v_pad[:, :, :, :], 0.0).then_inc(cleared, 1)

                @block.tensor
                def _(pe):
                    pe.wait_ge(squashed, 1)
                    for j in range(N_M):
                        ins = nc.tensor.matmul(pair_ps(0, j), k.w_lora[:, j * P:(j + 1) * P], pf[:, 12, :],
                                               start=True, stop=True)
                    ins.then_inc(w_done, 1)
                    for j in range(N_M):
                        ins = nc.tensor.matmul(pair_ps(2, j), k.a_lora[:, j * P:(j + 1) * P], pf[:, 12, :],
                                               start=True, stop=True)
                    ins.then_inc(a_done, 1)
                    pe.wait_ge(squashed, 2)
                    for j in range(N_M):
                        ins = nc.tensor.matmul(pair_ps(4, j), k.g_lora[:, j * P:(j + 1) * P], pf[:, 13, :],
                                               start=True, stop=True)
                    ins.then_inc(g_done, 1)
                    pe.wait_ge(kk_sq, 1)
                    for b in range(2):
                        ins = nc.tensor.matmul(k.ps[:, 6 + b, :], k.const("sum_64"), flat(e[:, :, :])[:, b * 512:(b + 1) * 512],
                                               start=True, stop=True)
                    ins.then_inc(kk_sum, 1)
                    pe.wait_ge(w_sig, 1)
                    pe.wait_ge(a_sig, 1)
                    for t in range(NT):
                        for j in range(N_M):
                            ins = nc.tensor.transpose(k.ps[:, t, j * P:(j + 1) * P], pf[:, 8 + j, t * P:(t + 1) * P],
                                                      k.const("ident"))
                    ins.then_inc(v_turned, 1)
                    pe.wait_ge(bonus_in, 1)
                    for b in range(2):
                        ins = nc.tensor.matmul(k.ps[:, 2 + b, :], k.const("sum_64"), flat(bonus[:, :, :])[:, b * 512:(b + 1) * 512],
                                               start=True, stop=True)
                    ins.then_inc(bonus_sum, 1)

                @block.scalar
                def _(act):
                    act.wait_ge(shifted, 1)
                    nc.scalar.activation(pf[0:64, 12, :], pf[0:64, 12, :], ACT.Tanh).then_inc(squashed, 1)
                    nc.scalar.activation(pf[:, 13, :], pf[:, 13, :], ACT.Sigmoid).then_inc(squashed, 1)
                    act.wait_ge(w_done, 1)
                    for j in range(N_M):
                        ins = nc.scalar.activation(sw[:, j, :], pair_ps(0, j), ACT.Sigmoid, bias=cols["w0"][:, j:j + 1])
                    ins.then_inc(w_sig, 1)
                    act.wait_ge(a_done, 1)
                    for j in range(N_M):
                        ins = nc.scalar.activation(a[:, j, :], pair_ps(2, j), ACT.Sigmoid, bias=cols["a0"][:, j:j + 1])
                    ins.then_inc(a_sig, 1)
                    act.wait_ge(g_done, 1)
                    nc.scalar.activation(g[:, :, :], two(4), ACT.Copy).then_inc(g_stored, 1)
                    act.wait_ge(kk_done, 1)
                    nc.scalar.activation(e[:, :, :], kh[:, :, :], ACT.Square).then_inc(kk_sq, 1)
                    act.wait_ge(kk_clamped, 1)
                    nc.scalar.activation(e[:, :, :], e[:, :, :], ACT.Ln).then_inc(kk_ln, 1)
                    act.wait_ge(kk_ln, 1)
                    nc.scalar.activation(e[:, :, :], e[:, :, :], ACT.Exp, scale=-0.5).then_inc(kk_rstd, 1)
                    act.wait_ge(used, 1)
                    nc.scalar.activation(e[:, :, :], dm, ACT.Exp, scale=LW_SCALE).then_inc(exps, 1)
                    act.wait_ge(used, 2)
                    nc.scalar.activation(e[:, :, :], dm, ACT.Exp, scale=-LW_SCALE).then_inc(exps, 1)
                    act.wait_ge(used, 3)
                    nc.scalar.activation(e[:, :, :], dm, ACT.Exp, scale=LW_SCALE).then_inc(exps, 1)
                    nc.scalar.activation(ends[:, :, :], ends[:, :, :], ACT.Exp, scale=LW_SCALE)

                @block.vector
                def _(dve):
                    step = chain(dve, vec_chain)
                    step(nc.vector.tensor_tensor(work[:, :, :], pr[:, :, 0:S], pf, ALU.subtract))
                    for j in range(N_K):
                        ins = nc.vector.scalar_tensor_tensor(pf[:, j, :], work[:, j, :], cols["mu"][:, j:j + 1],
                                                             pf[:, j, :], ALU.mult, ALU.add)
                    ins.then_inc(shifted, 1)
                    dve.wait_ge(shifted, 1)
                    for j in range(N_M):
                        ins = nc.vector.tensor_scalar(kh[:, j, :], pf[:, 4 + j, :], cols["k_k"][:, j:j + 1], None, ALU.mult)
                    ins.then_inc(kk_done, 1)
                    dve.wait_ge(w_sig, 1)
                    for j in range(N_M):
                        for c in range(NT):
                            r = slice(c * P, (c + 1) * P)
                            ins = nc.vector.tensor_tensor_scan(cs[:, j, r], k.ones[:, 0:P], sw[:, j, r], 0.0,
                                                               ALU.mult, ALU.add)
                    step(ins)
                    for c in range(NT):
                        r = slice(c * P, (c + 1) * P)
                        mid = cs[:, :, c * P + 63:c * P + 64]
                        nc.vector.tensor_tensor(dm[:, :, r], cs[:, :, r], mid.broadcast_to([P, N_M, P]), ALU.subtract)
                        nc.vector.tensor_tensor(ends[:, c, :], cs[:, :, c * P + P - 1], cs[:, :, c * P + 63], ALU.subtract)
                        ins = nc.vector.tensor_copy(ends[:, 2 + c, :], cs[:, :, c * P + 63])
                    step(ins)
                    dve.wait_ge(a_sig, 1)
                    for j in range(N_M):
                        ins = nc.vector.tensor_scalar(cs[:, j, :], a[:, j, :], -1.0, cols["k_a"][:, j:j + 1], ALU.add, ALU.mult)
                    step(ins)
                    dve.wait_ge(kk_done, 1)
                    kt = pf[:, 4:8, :]
                    step(nc.vector.scalar_tensor_tensor(kt, cs, 1.0, kt, ALU.add, ALU.mult))
                    for j in range(N_M):
                        ins = nc.vector.scalar_tensor_tensor(bonus[:, j, :], pf[:, j, :], cols["r_k"][:, j:j + 1],
                                                             kt[:, j, :], ALU.mult, ALU.mult)
                    ins.then_inc(bonus_in, 1)
                    dve.wait_ge(kk_sum, 1)
                    nc.vector.tensor_scalar(e[:, :, :], two(6), 1e-12, None, ALU.max).then_inc(kk_clamped, 1)
                    dve.wait_ge(cleared, 2)
                    dve.wait_ge(kk_rstd, 1)
                    step(nc.vector.tensor_tensor(kh[:, :, :], kh[:, :, :], e[:, :, :], ALU.mult))
                    nc.vector.tensor_tensor(a[:, :, :], a[:, :, :], kh[:, :, :], ALU.mult).then_inc(used, 1)
                    dve.wait_ge(exps, 1)
                    for h, r in halves:
                        ins = nc.vector.tensor_tensor(ar[r, :, h, 1, :], pf[r, 0:4, :], e[r, :, :], ALU.mult)
                    ins.then_inc(used, 1)
                    dve.wait_ge(exps, 2)
                    nc.vector.tensor_tensor(kap[:, :, :], kt, e[:, :, :], ALU.mult)
                    nc.vector.tensor_tensor(bet[:, :, :], a[:, :, :], e[:, :, :], ALU.mult)
                    nc.vector.tensor_tensor(dm, dm, sw, ALU.subtract).then_inc(used, 1)
                    dve.wait_ge(exps, 3)
                    for h, r in halves:
                        nc.vector.tensor_tensor(ar[r, :, h, 0, :], kh[r, :, :], e[r, :, :], ALU.mult)
                    dve.wait_ge(v_turned, 1)
                    for t in range(NT):
                        dst = v_pad[:, t, :, :].rearrange("p (j h) c -> p j h c", h=2)
                        src = k.ps[:, t, :].rearrange("p (j h c) -> p j h c", h=2, c=64)
                        for h in range(2):
                            nc.vector.tensor_copy(dst[:, :, h, h * 64:h * 64 + 64], src[:, :, h, :])
                    dve.wait_ge(bonus_sum, 1)
                    nc.vector.tensor_tensor(bonus[:, :, :], two(2), pf[:, 8:12, :], ALU.mult)

        gram = k.sb("gram", [P, K_H, 4, P], ctx=mem)
        m = k.sb("m_target", [P, K_H, P], ctx=mem)
        inv = k.sb("inverse", [P, K_H, P], ctx=mem)
        inv_t = k.sb("inverse_t", [P, K_H, P], ctx=mem)
        z = k.sb("z_inv", [P, K_H, P], ctx=mem)
        block_m = k.sb("level_block", [P, K_H, P], ctx=mem)
        x = k.sb("x_rhs", [P, K_H, 64], ctx=mem)
        u_pad = k.sb("u_neg", [P, K_H, P], ctx=mem)
        s0 = k.sb("state", [P, N_M, P], ctx=mem)
        kb_tok = k.sb("kb_tok", [P, 2, N_M, P], ctx=mem)
        own = lambda t, c, h: t[:, c, h, h % 2 * 64:h % 2 * 64 + 64]
        for c in range(NT):
            cr = slice(c * P, (c + 1) * P)
            with k.stage("cleared", "gram_done", "gram_masked", "m_done", "z_done", "z_stored", "upd_done",
                         "inverse_ready", "block_ready", "x_done", "x_stored", "u_done", "u_stored", "y_done",
                         "kb_turned", "kb_stored", "s_done", "vec_chain") as (
                    block, cleared, gram_done, gram_masked, m_done, z_done, z_stored, upd_done,
                    inverse_ready, block_ready, x_done, x_stored, u_done, u_stored, y_done,
                    kb_turned, kb_stored, s_done, vec_chain):
                levels = [2 ** i for i in range(1, 7)]

                @block.gpsimd
                def _(pool):
                    if c == 0:
                        step = chain(pool, cleared)
                        step(nc.gpsimd.memset(u_pad[:, :, :], 0.0))
                        step(nc.gpsimd.memset(s0[:, :, :], 0.0))
                        step(nc.gpsimd.memset(gram[64:P, :, :, 0:64], 0.0))
                        step(nc.gpsimd.memset(m[0:64, :, 64:P], 0.0))

                @block.tensor
                def _(pe):
                    for h in range(K_H):
                        j = h // 2
                        if h >= 4:
                            pe.wait_ge(gram_masked, h - 3)
                        for n, src in enumerate((bet, kap)):
                            out = k.ps[:, h % 4, 256 * n:256 * n + 256].rearrange("p (q t) -> p q t", q=2)
                            nc.tensor.matmul(out[:, :, 64:P], src[:, j, cr], ar[:, j, h % 2, :, c * P + 64:(c + 1) * P],
                                             start=True, stop=True)
                            ins = nc.tensor.matmul(out[0:64, :, 0:64], src[:, j, c * P:c * P + 64],
                                                   ar[:, j, h % 2, :, c * P:c * P + 64], start=True, stop=True)
                        ins.then_inc(gram_done, 1)
                    for h in range(K_H):
                        j = h // 2
                        al = ar[:, j, h % 2, 0, :]
                        out = k.ps[:, 4 + h // 4, h % 4 * P:(h % 4 + 1) * P]
                        nc.tensor.matmul(out[:, 0:64], al[:, cr], bet[:, j, c * P:c * P + 64], start=True, stop=True)
                        ins = nc.tensor.matmul(out[64:P, 64:P], al[:, c * P + 64:(c + 1) * P],
                                               bet[:, j, c * P + 64:(c + 1) * P], start=True, stop=True)
                    ins.then_inc(m_done, 1)
                    if c == 0:
                        pe.wait_ge(gram_masked, K_H)
                        for n, src in enumerate((kap, bet)):
                            for j in range(N_M):
                                ins = nc.tensor.transpose(k.ps[:, n, j * P:(j + 1) * P], src[:, j, cr], k.const("ident"))
                        ins.then_inc(kb_turned, 1)
                        pe.wait_ge(kb_stored, 1)
                    pe.wait_ge(gram_masked, K_H)
                    for n, lv in enumerate(levels):
                        pe.wait_ge(block_ready, n + 1)
                        pe.wait_ge(inverse_ready, n + 1)
                        for h in range(K_H):
                            ins = nc.tensor.matmul(k.ps[:, h // 4, h % 4 * P:(h % 4 + 1) * P], block_m[:, h, :],
                                                   inv_t[:, h, :], start=True, stop=True)
                        ins.then_inc(z_done, 1)
                        pe.wait_ge(z_stored, n + 1)
                        for h in range(K_H):
                            ins = nc.tensor.matmul(k.ps[:, 2 + h // 4, h % 4 * P:(h % 4 + 1) * P], inv[:, h, :],
                                                   z[:, h, :], start=True, stop=True)
                        if n < len(levels) - 1:
                            for h in range(K_H):
                                ins = nc.tensor.matmul(k.ps[:, 6 + h // 4, h % 4 * P:(h % 4 + 1) * P], z[:, h, :],
                                                       inv[:, h, :], start=True, stop=True)
                        ins.then_inc(upd_done, 1)
                    for h in range(K_H):
                        out = k.ps[:, 0, h * 64:h * 64 + 64]
                        if c:
                            nc.tensor.matmul(out, ar[:, h // 2, h % 2, 0, cr], s0[:, h // 2, h % 2 * 64:h % 2 * 64 + 64],
                                             start=True, stop=False)
                        ins = nc.tensor.matmul(out, gram[:, h, 2, :], own(v_pad, c, h), start=c == 0, stop=True)
                    ins.then_inc(x_done, 1)
                    pe.wait_ge(x_stored, 1)
                    pe.wait_ge(inverse_ready, len(levels) + 1)
                    for h in range(K_H):
                        ins = nc.tensor.matmul(k.ps[:, 1, h * 64:h * 64 + 64], inv_t[:, h, :], x[:, h, :],
                                               start=True, stop=True)
                    ins.then_inc(u_done, 1)
                    pe.wait_ge(u_stored, 1)
                    for j in range(N_M):
                        out = k.ps[:, 2, j * P:(j + 1) * P]
                        for i in range(2):
                            h = 2 * j + i
                            nc.tensor.matmul(out, v_pad[:, c, h, :], gram[:, h, 3, :], start=i == 0, stop=False)
                            ins = nc.tensor.matmul(out, u_pad[:, h, :], gram[:, h, 1, :], start=False,
                                                   stop=c == 0 and i == 1)
                        if c:
                            for i in range(2):
                                ins = nc.tensor.matmul(out, s0[:, j, :], ar[:, j, i, 1, cr], start=False, stop=i == 1)
                    ins.then_inc(y_done, 1)
                    if c == 0:
                        for j in range(N_M):
                            for i in range(2):
                                h = 2 * j + i
                                out = k.ps[:, 3, j * P + i * 64:j * P + i * 64 + 64]
                                nc.tensor.matmul(out, kb_tok[:, 0, j, :], own(v_pad, 0, h), start=True, stop=False)
                                ins = nc.tensor.matmul(out, kb_tok[:, 1, j, :], u_pad[:, h, i * 64:i * 64 + 64],
                                                       start=False, stop=True)
                        ins.then_inc(s_done, 1)

                @block.scalar
                def _(act):
                    if c == 0:
                        act.wait_ge(kb_turned, 1)
                        nc.scalar.activation(kb_tok[:, :, :, :].rearrange("p n j c -> p n (j c)"), k.ps[:, 0:2, :],
                                             ACT.Copy).then_inc(kb_stored, 1)
                    for n in range(len(levels)):
                        act.wait_ge(z_done, n + 1)
                        nc.scalar.activation(z[:, :, :].rearrange("p (b i) c -> p b (i c)", b=2), k.ps[:, 0:2, :],
                                             ACT.Copy).then_inc(z_stored, 1)
                    act.wait_ge(x_done, 1)
                    nc.scalar.activation(x[:, :, :].rearrange("p h c -> p (h c)"), k.ps[:, 0, :], ACT.Copy
                                         ).then_inc(x_stored, 1)
                    act.wait_ge(y_done, 1)
                    nc.scalar.activation(y_out[:, :, cr], k.ps[:, 2, :].rearrange("p (j c) -> p j c", c=P), ACT.Copy)

                @block.vector
                def _(dve):
                    step = chain(dve, vec_chain)
                    at = k.columns["strict"][0]
                    both = k.consts[:, at:at + 2 * P].rearrange("p (q c) -> p q c", q=2)
                    for h in range(K_H):
                        dve.wait_ge(gram_done, h + 1)
                        for n in range(2):
                            src = k.ps[:, h % 4, 256 * n:256 * n + 256].rearrange("p (q t) -> p q t", q=2)
                            dst = gram[:, h, 2 * n:2 * n + 2, :]
                            nc.vector.tensor_tensor(dst[:, :, 64:P], src[:, :, 64:P], both[:, :, 64:P], ALU.mult)
                            ins = nc.vector.tensor_tensor(dst[0:64, :, 0:64], src[0:64, :, 0:64], both[0:64, :, 0:64], ALU.mult)
                        ins.then_inc(gram_masked, 1)
                    dve.wait_ge(m_done, 1)
                    if c == 0:
                        dve.wait_ge(cleared, 4)
                    src = k.ps[:, 4:6, :].rearrange("p b (i c) -> p (b i) c", c=P)
                    nc.vector.tensor_copy(m[:, :, 0:64], src[:, :, 0:64])
                    step(nc.vector.tensor_copy(m[64:P, :, 64:P], src[64:P, :, 64:P]))
                    every = lambda name, n=K_H: k.const(name).rearrange("p (o c) -> p o c", o=1).broadcast_to([P, n, P])
                    step(nc.vector.tensor_tensor(inv[:, :, :], m[:, :, :], every("level_1"), ALU.mult))
                    nc.vector.tensor_tensor(inv[:, :, :], every("ident"), inv[:, :, :], ALU.subtract)
                    dve.wait_ge(gram_masked, K_H)
                    step(nc.vector.tensor_tensor(inv_t[:, :, :], gram[:, :, 0, :], every("level_1t"), ALU.mult))
                    nc.vector.tensor_tensor(inv_t[:, :, :], every("ident"), inv_t[:, :, :], ALU.subtract).then_inc(inverse_ready, 1)
                    for n, lv in enumerate(levels):
                        if n:
                            dve.wait_ge(z_done, n)
                        nc.vector.tensor_tensor(block_m[:, :, :], m[:, :, :], every(f"level_{lv}"), ALU.mult
                                                ).then_inc(block_ready, 1)
                        dve.wait_ge(upd_done, n + 1)
                        dve.wait_ge(inverse_ready, n + 1)
                        if n < len(levels) - 1:
                            nc.vector.tensor_tensor(inv[:, :, :], inv[:, :, :],
                                                    k.ps[:, 6:8, :].rearrange("p b (i c) -> p (b i) c", c=P), ALU.subtract)
                        nc.vector.tensor_tensor(inv_t[:, :, :], inv_t[:, :, :],
                                                k.ps[:, 2:4, :].rearrange("p b (i c) -> p (b i) c", c=P), ALU.subtract
                                                ).then_inc(inverse_ready, 1)
                    dve.wait_ge(u_done, 1)
                    dst = u_pad[:, :, :].rearrange("p (j h) c -> p j h c", h=2)
                    src = k.ps[:, 1, :].rearrange("p (j h c) -> p j h c", h=2, c=64)
                    for h in range(2):
                        ins = nc.vector.tensor_scalar(dst[:, :, h, h * 64:h * 64 + 64], src[:, :, h, :], -1.0, None, ALU.mult)
                    ins.then_inc(u_stored, 1)
                    if c == 0:
                        dve.wait_ge(s_done, 1)
                        for h in range(2):
                            r = slice(h * 64, h * 64 + 64)
                            for j in range(N_M):
                                nc.vector.tensor_scalar(s0[r, j, r], k.ps[r, 3, j * P + h * 64:j * P + h * 64 + 64],
                                                        ends[r, 0, j:j + 1], ends[r, 3, j:j + 1], ALU.mult, ALU.mult)

        with k.stage("mean_done", "centred", "squared", "var_done", "ln_done", "rstd_done", "vec_chain") as (
                block, mean_done, centred, squared, var_done, ln_done, rstd_done, vec_chain):
            y2 = y_out.rearrange("p j s -> p (j s)")
            sq = gram[:, 0:2, :, :].rearrange("p a b c -> p (a b c)")
            rstd = gram[:, 2:4, :, :].rearrange("p a b c -> p (a b c)")
            banks = lambda t: t.rearrange("p (b s) -> p b s", b=2)

            @block.tensor
            def _(pe):
                for b in range(2):
                    ins = nc.tensor.matmul(k.ps[:, b, :], k.const("mean_64"), y2[:, b * 512:(b + 1) * 512], start=True, stop=True)
                ins.then_inc(mean_done, 1)
                pe.wait_ge(squared, 1)
                for b in range(2):
                    ins = nc.tensor.matmul(k.ps[:, 2 + b, :], k.const("mean_64"), sq[:, b * 512:(b + 1) * 512], start=True, stop=True)
                ins.then_inc(var_done, 1)

            @block.scalar
            def _(act):
                act.wait_ge(centred, 1)
                nc.scalar.activation(sq, y2, ACT.Square).then_inc(squared, 1)
                act.wait_ge(var_done, 1)
                nc.scalar.activation(banks(rstd), k.ps[:, 2:4, :], ACT.Ln, bias=k.eps[:, 2:3]).then_inc(ln_done, 1)
                act.wait_ge(ln_done, 1)
                nc.scalar.activation(rstd, rstd, ACT.Exp, scale=-0.5).then_inc(rstd_done, 1)

            @block.vector
            def _(dve):
                step = chain(dve, vec_chain)
                dve.wait_ge(mean_done, 1)
                nc.vector.tensor_tensor(banks(y2), banks(y2), k.ps[:, 0:2, :], ALU.subtract).then_inc(centred, 1)
                dve.wait_ge(rstd_done, 1)
                rs = rstd.rearrange("p (j s) -> p j s", j=N_M)
                for j in range(N_M):
                    ins = nc.vector.scalar_tensor_tensor(y_out[:, j, :], y_out[:, j, :], cols["rwkv_g"][:, j:j + 1],
                                                         rs[:, j, :], ALU.mult, ALU.mult)
                step(ins)
                step(nc.vector.tensor_tensor(y_out, y_out, bonus[:, :, :], ALU.add))
                nc.vector.tensor_tensor(y_out, y_out, g[:, :, :], ALU.mult)


def merge(k, l, cols, h, y, merged):
    nc, io = k.nc, k.io
    w_gate = io["w_gate_2"].rearrange("l (k p) c -> l p k c", p=P)
    w_branch = io["w_branch_2"].rearrange("l n (k p) c -> l n p k c", p=P)
    slabs = []
    for n in range(3):
        slabs += [w_gate[l, :, :, n * D + i * 512:n * D + (i + 1) * 512] for i in range(2)]
        slabs += [w_branch[l, n]]
    with ExitStack() as mem:
        gates = k.sb("gates", [P, ND, S], ctx=mem)
        with k.stage(*LOADED, "gate_done", "gate_stored", "product_done", "product_used", "vec_chain") as (block, *sems):
            loaded, (gate_done, gate_stored, product_done, product_used, vec_chain) = sems[:SLOTS], sems[SLOTS:]

            @block.sync
            def _(sp):
                for i, src in enumerate(slabs):
                    n, s = i // 3, i % 3
                    if n and s < 2:
                        sp.wait_ge(gate_done, (n - 1) * ND + 4 * (s + 1))
                    elif n:
                        sp.wait_ge(product_done, n * ND)
                    kk = src.shape[1]
                    sp.dma_start(slab_view(k, s, kk * P, SLAB // kk), src).then_inc(loaded[s], 16)

            @block.tensor
            def _(pe):
                for n in range(3):
                    for j in range(ND):
                        t = n * ND + j
                        if j % 4 == 0:
                            wait_slab(pe, loaded, 3 * n + j // 4)
                        if t >= 4:
                            pe.wait_ge(gate_stored, t - 3)
                        slab = slab_view(k, j // 4, D, 512)
                        for i in range(ND):
                            ins = nc.tensor.matmul(k.ps[:, t % 4, 0:S], slab[:, i, j % 4 * P:(j % 4 + 1) * P], h[:, i, :],
                                                   start=i == 0, stop=i == ND - 1)
                        ins.then_inc(gate_done, 1)
                    wait_slab(pe, loaded, 3 * n + 2)
                    slab = slab_view(k, 2, MW, D)
                    for j in range(ND):
                        t = n * ND + j
                        if t >= 4:
                            pe.wait_ge(product_used, t - 3)
                        for i in range(N_M):
                            ins = nc.tensor.matmul(k.ps[:, 4 + t % 4, 0:S], slab[:, i, j * P:(j + 1) * P],
                                                   y[:, n, i, :], start=i == 0, stop=i == N_M - 1)
                        ins.then_inc(product_done, 1)

            @block.scalar
            def _(act):
                for n in range(3):
                    for j in range(ND):
                        t = n * ND + j
                        act.wait_ge(gate_done, t + 1)
                        if n:
                            act.wait_ge(product_used, t - ND + 1)
                        nc.scalar.activation(gates[:, j, :], k.ps[:, t % 4, 0:S], ACT.Sigmoid,
                                             bias=cols["b_gate"][:, t:t + 1]).then_inc(gate_stored, 1)

            @block.vector
            def _(dve):
                step = chain(dve, vec_chain)
                for n in range(3):
                    for j in range(ND):
                        t = n * ND + j
                        dve.wait_ge(gate_stored, t + 1)
                        dve.wait_ge(product_done, t + 1)
                        ps = k.ps[:, 4 + t % 4, 0:S]
                        if n == 0:
                            ins = nc.vector.tensor_tensor(merged[:, j, :], ps, gates[:, j, :], ALU.mult)
                            ins.then_inc(product_used, 1)
                        else:
                            nc.vector.tensor_tensor(gates[:, j, :], ps, gates[:, j, :], ALU.mult).then_inc(vec_chain, 1)
                            dve.wait_ge(vec_chain, t - ND + 1)
                            dve.wait_ge(product_used, t - ND + 1)
                            nc.vector.tensor_tensor(merged[:, j, :], merged[:, j, :], gates[:, j, :], ALU.add
                                                    ).then_inc(product_used, 1)


def router(k, l, h2, weight_t, w_router, b_router):
    nc, io = k.nc, k.io
    n_all = N_G + N_E
    with ExitStack() as mem:
        lg = k.sb("logits", [P, NT, n_all], ctx=mem)
        hit = k.sb("hit", [P, NT, N_E], ctx=mem)
        group = k.sb("group", [P, NT, N_G], ctx=mem)
        prob = k.sb("prob", [P, NT, 1], ctx=mem)
        grp_exp = k.sb("grp_exp", [P, NT, N_G], ctx=mem)
        chosen = [k.sb(f"chosen{i}", [P, NT, N_E], ctx=mem) for i in range(2)]
        top = [k.sb(f"top{i}", [P, NT, 1], ctx=mem) for i in range(3)]
        index = k.sb("index", [P, NT, 1], ctx=mem)
        weight = k.sb("weight", [P, NT, P], ctx=mem)
        with k.stage("cleared", "logits_done", "grp_in", "grp_out", "exp_in", "exp_out", "weights_done", "turned",
                     "copied", "stored", "vec_chain") as (
                block, cleared, logits_done, grp_in, grp_out, exp_in, exp_out, weights_done, turned, copied,
                stored, vec_chain):

            @block.gpsimd
            def _(pool):
                nc.gpsimd.memset(weight[:, :, :], 0.0).then_inc(cleared, 1)

            @block.tensor
            def _(pe):
                for t in range(NT):
                    for j in range(ND):
                        ins = nc.tensor.matmul(k.ps[:, t, 0:n_all], h2[:, j, t * P:(t + 1) * P], w_router[:, j, :],
                                               start=j == 0, stop=j == ND - 1)
                ins.then_inc(logits_done, 1)
                pe.wait_ge(weights_done, 1)
                for t in range(NT):
                    ins = nc.tensor.transpose(k.ps[:, 2, t * P:(t + 1) * P], weight[:, t, :], k.const("ident"))
                ins.then_inc(turned, 1)

            @block.scalar
            def _(act):
                act.wait_ge(grp_in, 1)
                nc.scalar.activation(grp_exp[:, :, :], grp_exp[:, :, :], ACT.Exp).then_inc(grp_out, 1)
                act.wait_ge(exp_in, 1)
                nc.scalar.activation(top[2][:, :, :], top[2][:, :, :], ACT.Exp).then_inc(exp_out, 1)

            @block.vector
            def _(dve):
                step = chain(dve, vec_chain)
                wide = lambda a, n: a[:, :, :].broadcast_to([P, NT, n])
                iota = k.const("iota_e").rearrange("p (o c) -> p o c", o=1)

                def first_max(out, src, best, n):
                    ids = iota[:, :, 0:n].broadcast_to([P, NT, n])
                    step(nc.vector.tensor_reduce(best, src, AX.X, ALU.max))
                    step(nc.vector.tensor_tensor(out, src, wide(best, n), ALU.not_equal))
                    step(nc.vector.scalar_tensor_tensor(out, out, 64.0, ids, ALU.mult, ALU.add))
                    step(nc.vector.tensor_reduce(index[:, :, :], out, AX.X, ALU.min))
                    step(nc.vector.tensor_tensor(out, ids, wide(index[:, :, :], n), ALU.is_equal))

                dve.wait_ge(logits_done, 1)
                step(nc.vector.tensor_tensor(lg[:, :, :], k.ps[:, 0:NT, 0:n_all],
                                             b_router[:, :].rearrange("p (o c) -> p o c", o=1).broadcast_to([P, NT, n_all]),
                                             ALU.add))
                groups, experts = lg[:, :, 0:N_G], lg[:, :, N_G:]
                first_max(group[:, :, :], groups, top[0][:, :, :], N_G)
                nc.vector.tensor_tensor(grp_exp[:, :, :], groups, wide(top[0][:, :, :], N_G), ALU.subtract).then_inc(grp_in, 1)
                dve.wait_ge(grp_out, 1)
                step(nc.vector.tensor_reduce(prob[:, :, :], grp_exp[:, :, :], AX.X, ALU.add))
                step(nc.vector.reciprocal(prob[:, :, :], prob[:, :, :]))
                step(nc.vector.tensor_scalar(group[:, :, :], group[:, :, :], 1.0, BIG, ALU.subtract, ALU.mult))
                for t in range(NT):
                    e3 = experts[:, t, :].rearrange("p (g e) -> p g e", g=N_G)
                    g3 = group[:, t, :].rearrange("p (g o) -> p g o", o=1).broadcast_to([P, N_G, E_G])
                    ins = nc.vector.tensor_tensor(e3, e3, g3, ALU.add)
                step(ins)
                first_max(chosen[0][:, :, :], experts, top[0][:, :, :], N_E)
                step(nc.vector.scalar_tensor_tensor(hit[:, :, :], chosen[0][:, :, :], -4 * BIG, experts, ALU.mult, ALU.add))
                first_max(chosen[1][:, :, :], hit[:, :, :], top[1][:, :, :], N_E)
                nc.vector.tensor_tensor(top[2][:, :, :], top[1][:, :, :], top[0][:, :, :], ALU.subtract).then_inc(exp_in, 1)
                dve.wait_ge(exp_out, 1)
                step(nc.vector.tensor_scalar(top[0][:, :, :], top[2][:, :, :], 1.0, None, ALU.add))
                step(nc.vector.reciprocal(top[0][:, :, :], top[0][:, :, :]))
                step(nc.vector.tensor_tensor(top[0][:, :, :], top[0][:, :, :], prob[:, :, :], ALU.mult))
                step(nc.vector.tensor_tensor(top[1][:, :, :], top[0][:, :, :], top[2][:, :, :], ALU.mult))
                for i in range(2):
                    step(nc.vector.tensor_tensor(chosen[i][:, :, :], chosen[i][:, :, :], wide(top[i][:, :, :], N_E), ALU.mult))
                dve.wait_ge(cleared, 1)
                nc.vector.tensor_tensor(weight[:, :, 0:N_E], chosen[0][:, :, :], chosen[1][:, :, :], ALU.add).then_inc(weights_done, 1)
                dve.wait_ge(turned, 1)
                nc.vector.tensor_copy(weight_t[:, :], k.ps[:, 2, 0:S]).then_inc(copied, 1)

            @block.sync
            def _(sp):
                sp.wait_ge(copied, 1)
                sp.dma_start(io["expert_weights"], weight_t[0:N_E, :]).then_inc(stored, 16)
                sp.wait_ge(stored, 16)


def experts(k, l, h2, wide, gain):
    nc, io = k.nc, k.io
    views = [io["w_exp_gate_2"].rearrange("l e (k p) f -> l e p k f", p=P),
             io["w_exp_up_2"].rearrange("l e (k p) f -> l e p k f", p=P),
             io["w_exp_down_2"].rearrange("l e (k p) d -> l e p k d", p=P)]
    with ExitStack() as mem:
        gate = k.sb("gate_act", [P, 2, 2, S], ctx=mem)
        gu = k.sb("gate_up", [P, 2, 2, S], ctx=mem)
        zero = k.sb("zero", [P, 512], ctx=mem)
        with k.stage(*LOADED, "wide_loaded", "cleared", "sums_closed", "gate_done", "up_done", "act_done",
                     "scaled", "gu_done", "down_done") as (block, *sems):
            loaded, (wide_loaded, cleared, sums_closed, gate_done, up_done, act_done, scaled, gu_done, down_done) = (
                sems[:SLOTS], sems[SLOTS:])

            @block.gpsimd
            def _(pool):
                nc.gpsimd.memset(zero[:, :], 0.0).then_inc(cleared, 1)

            @block.sync
            def _(sp):
                src = io["expert_weights"].rearrange("(o e) s -> o (e s)", o=1).broadcast_to([P, N_E * S])
                sp.dma_start(wide[:, :, :].rearrange("p e s -> p (e s)"), src).then_inc(wide_loaded, 16)
                for n, view in enumerate(views):
                    kk = view.shape[3]
                    sp.dma_start(slab_view(k, n, kk * P, SLAB // kk), view[l, 0]).then_inc(loaded[n], 16)
                with sp.Fori(1, N_E) as e:
                    for n, (view, through) in enumerate(zip(views, (gate_done, up_done, down_done))):
                        kk = view.shape[3]
                        sp.wait_ge(through, e * 2 + n // 2)
                        sp.dma_start(slab_view(k, n, kk * P, SLAB // kk), view[l, e]).then_inc(loaded[n], 16)

            @block.tensor
            def _(pe):
                pe.wait_ge(cleared, 1)
                for b in range(4):
                    ins = nc.tensor.matmul(k.ps[:, 4 + b, :], zero[:, 0:P], zero[:, :], start=True, stop=False)
                ins.then_inc(down_done, 1)
                with pe.Fori(0, N_E) as e:
                    for half in range(2):
                        for n, (bank, done) in enumerate(((0, gate_done), (2, up_done))):
                            if half == 0:
                                pe.wait_ge(loaded[n], e * 16 + 16)
                            if n == 0:
                                pe.wait_ge(gu_done, e * 2 + 1)
                            slab = slab_view(k, n, D, FF)
                            for f in range(2):
                                c = (2 * half + f) * P
                                for j in range(ND):
                                    ins = nc.tensor.matmul(k.ps[:, bank + half, f * S:(f + 1) * S], slab[:, j, c:c + P],
                                                           h2[:, j, :], start=j == 0, stop=j == ND - 1)
                            ins.then_inc(done, 1)
                    slab = slab_view(k, 2, FF, D)
                    pe.wait_ge(loaded[2], e * 16 + 16)
                    for half in range(2):
                        pe.wait_ge(gu_done, e * 2 + half + 2)
                        for i in range(2):
                            for j in range(ND):
                                ins = nc.tensor.matmul(k.ps[:, 4 + j // 2, j % 2 * S:(j % 2 + 1) * S],
                                                       slab[:, 2 * half + i, j * P:(j + 1) * P], gu[:, half, i, :],
                                                       start=False, stop=False)
                        ins.then_inc(down_done, 1)
                for b in range(4):
                    ins = nc.tensor.matmul(k.ps[:, 4 + b, :], zero[:, 0:P], zero[:, :], start=False, stop=True)
                ins.then_inc(sums_closed, 1)

            @block.scalar
            def _(act):
                with act.Fori(0, N_E) as e:
                    for half in range(2):
                        act.wait_ge(gate_done, e * 2 + half + 1)
                        act.wait_ge(gu_done, e * 2 + 1)
                        nc.scalar.activation(gate[:, half, :, :].rearrange("p f s -> p (f s)"), k.ps[:, half, :],
                                             ACT.Silu).then_inc(act_done, 1)

            @block.vector
            def _(dve):
                dve.wait_ge(wide_loaded, 16)
                dve.sem_inc(gu_done, 1)
                with dve.Fori(0, N_E) as e:
                    for half in range(2):
                        dve.wait_ge(act_done, e * 2 + half + 1)
                        dve.wait_ge(up_done, e * 2 + half + 1)
                        dve.wait_ge(down_done, e * 2 + 1)
                        nc.vector.tensor_tensor(gate[:, half, :, :].rearrange("p f s -> p (f s)"),
                                                gate[:, half, :, :].rearrange("p f s -> p (f s)"),
                                                k.ps[:, 2 + half, :], ALU.mult).then_inc(scaled, 1)
                        dve.wait_ge(scaled, e * 2 + half + 1)
                        nc.vector.tensor_tensor(gu[:, half, :, :], gate[:, half, :, :],
                                                wide[:, bass.ds(e, 1), :].broadcast_to([P, 2, S]), ALU.mult).then_inc(gu_done, 1)
                dve.wait_ge(sums_closed, 1)
                for j in range(ND):
                    nc.vector.scalar_tensor_tensor(k.x[:, j, :], k.ps[:, 4 + j // 2, j % 2 * S:(j % 2 + 1) * S],
                                                   gain[:, j:j + 1], k.x[:, j, :], ALU.mult, ALU.add)


def second_block(k):
    nc, io = k.nc, k.io
    with ExitStack() as mem:
        k.sin = k.sb("sin", [P, S], ctx=mem)
        k.cos = k.sb("cos", [P, S], ctx=mem)
        k.c_silu = k.sb("c_silu", [P, ND], ctx=mem)
        k.mod = k.sb("mod", [P, 6 * ND], ctx=mem)
        k.w_lora = k.sb("w_lora", [P, MW], ctx=mem)
        k.a_lora = k.sb("a_lora", [P, MW], ctx=mem)
        k.g_lora = k.sb("g_lora", [P, MW], ctx=mem)
        w_router = k.sb("w_router", [P, ND, N_G + N_E], ctx=mem)
        b_router = k.sb("b_router", [P, N_G + N_E], ctx=mem)
        weight_t = k.sb("weight_t", [P, S], ctx=mem)
        tile_rows = lambda ap: ap.rearrange("(r c) -> r c", c=P)
        rotation_tables(k)
        cols = load_rows(k, [("c", ND, [(0, tile_rows(io["c_2"][0]))])])
        with k.stage("cleared") as (block, cleared):
            @block.scalar
            def _(act):
                nc.scalar.activation(k.c_silu[:, :], cols["c"], ACT.Silu)

            @block.gpsimd
            def _(pool):
                nc.gpsimd.memset(k.w_lora[64:P, :], 0.0).then_inc(cleared, 1)
                pool.wait_ge(cleared, 1)
                nc.gpsimd.memset(k.a_lora[0:64, :], 0.0)
        k.clear_semaphores()

        with nc.Fori(0, LAYERS) as l:
            row = lambda name: tile_rows(io[name][l])
            cols = load_rows(k, [
                ("b_ada", 6 * ND, [(0, row("b_ada_2"))]), ("b_gate", 3 * ND, [(0, row("b_gate_2"))]),
                ("norm1", ND, [(0, row("norm1_g_2"))]), ("norm2", ND, [(0, row("norm2_g_2"))]),
                ("mu", N_K, [(0, row("rwkv_mu_2"))]), ("ret_g", N_M, [(0, row("ret_gn_g_2"))]),
                ("w0", N_M, [(0, row("rwkv_w0_2"))]), ("a0", N_M, [(0, row("rwkv_a0_2"))]),
                ("k_k", N_M, [(0, row("rwkv_k_k_2"))]), ("k_a", N_M, [(0, row("rwkv_k_a_2"))]),
                ("r_k", N_M, [(0, io["rwkv_r_k_2"][l].rearrange("(j h) c -> j (h c)", h=2))]),
                ("rwkv_g", N_M, [(0, row("rwkv_gn_g_2"))]),
                ("conv_w", 3 * N_M, [(0, io["conv_w_2"][l].rearrange("i (r c) -> (i r) c", c=P))]),
            ])
            with k.stage("small_loaded") as (block, loaded):
                @block.sync
                def _(sp):
                    wide = lambda name, n: io[name][l].rearrange("(o c) -> o c", o=1).broadcast_to([P, n])
                    for dst, src in (
                            (k.w_lora[0:64, :], io["rwkv_w_lora_2"][l]), (k.a_lora[64:P, :], io["rwkv_a_lora_2"][l]),
                            (k.g_lora[:, :], io["rwkv_g_lora_2"][l]),
                            (w_router[:, :, 0:N_G], io["w_router_group_2"].rearrange("l (k p) c -> l p k c", p=P)[l]),
                            (w_router[:, :, N_G:], io["w_router_expert_2"].rearrange("l (k p) c -> l p k c", p=P)[l]),
                            (b_router[:, 0:N_G], wide("b_router_group_2", N_G)),
                            (b_router[:, N_G:], wide("b_router_expert_2", N_E))):
                        sp.dma_start(dst, src).then_inc(loaded, 16)
                    sp.wait_ge(loaded, 16 * 7)
            ada_modulation(k, l, cols)
            mod = lambda i: k.mod[:, i * ND:(i + 1) * ND]
            with ExitStack() as tmp:
                h = k.sb("h", [P, ND, S], ctx=tmp)
                y = k.sb("y_branches", [P, 3, N_M, S], ctx=tmp)
                rms_norm(k, k.x[:, :, :], h[:, :, :], mod(1), mod(0))
                with ExitStack() as tmp2:
                    pr = k.sb("p_rwkv", [P, N_K, S + 1], ctx=tmp2)
                    with ExitStack() as tmp3:
                        p = k.sb("p", [P, 4 * N_M + 3 * N_M, S], ctx=tmp3)
                        branch_projections(k, l, h, p, pr)
                        retention_and_conv(k, cols, p, y[:, 0, :, :], y[:, 2, :, :])
                    k.clear_semaphores()
                    rwkv(k, cols, pr, y[:, 1, :, :])
                k.clear_semaphores()
                merged = k.sb("merged", [P, ND, S], ctx=tmp)
                merge(k, l, cols, h, y, merged)
                w_o = io["w_o_2"].rearrange("l (k p) c -> l p k c", p=P)
                add_product(k, [w_o[l, :, :, i * 512:(i + 1) * 512] for i in range(2)],
                            [(j // 4, j % 4 * P, j) for j in range(ND)], merged, mod(2))
            k.clear_semaphores()
            with ExitStack() as tmp:
                h2 = k.sb("h2", [P, ND, S], ctx=tmp)
                rms_norm(k, k.x[:, :, :], h2[:, :, :], mod(4), mod(3))
                router(k, l, h2, weight_t, w_router, b_router)
                wide = k.sb("expert_weights_wide", [P, N_E, S], ctx=tmp)
                experts(k, l, h2, wide, mod(5))
            k.clear_semaphores()


def finish(k):
    nc, io = k.nc, k.io
    cols = load_rows(k, [("final", ND, [(0, io["final_norm_g_2"].rearrange("(r c) -> r c", c=P))])])
    with ExitStack() as mem:
        y = k.sb("y_final", [P, ND, S], ctx=mem)
        y_tok = k.sb("y_tok", [P, NT, D], ctx=mem)
        rms_norm(k, k.x[:, :, :], y[:, :, :], cols["final"])
        with k.stage("turned", "copied", "stored") as (block, turned, copied, stored):

            @block.tensor
            def _(pe):
                for t in range(NT):
                    for j in range(ND):
                        ins = nc.tensor.transpose(k.ps[:, 2 * t + j // 4, j % 4 * P:(j % 4 + 1) * P],
                                                  y[:, j, t * P:(t + 1) * P], k.const("ident"))
                    ins.then_inc(turned, 1)

            @block.vector
            def _(dve):
                for t in range(NT):
                    dve.wait_ge(turned, t + 1)
                    nc.vector.tensor_copy(y_tok[:, t, :].rearrange("p (b c) -> p b c", b=2),
                                          k.ps[:, 2 * t:2 * t + 2, :]).then_inc(copied, 1)

            @block.sync
            def _(sp):
                for t in range(NT):
                    sp.wait_ge(copied, t + 1)
                    sp.dma_start(io["out"][0, t * P:(t + 1) * P, :], y_tok[:, t, :]).then_inc(stored, 16)
                sp.wait_ge(stored, 16 * NT)


def program(nc, io):
    with ExitStack() as ctx:
        k = Core(nc, ctx, io)
        k.columns, n = layout(constants())
        k.consts = k.sb("constants", [P, n])
        k.eps = k.sb("eps", [P, 3])
        k.ones = k.sb("ones", [P, S])
        k.rows = k.sb("rows", [P, 2, P])
        k.cols = k.sb("cols", [P, 2 * P])
        k.x = k.sb("x", [P, ND, S])
        k.rstd = k.sb("rstd", [P, S])
        k.ring = k.sb("ring", [P, SLOTS, SLAB])
        k.ps = ctx.enter_context(nc.psum_tensor("ps", [P, 8, 512], F32))
        load_inputs(k)
        first_block(k)
        second_block(k)
        finish(k)


INPUTS = [
    "x", "norm_g", "w_in", "q_norm_g", "k_norm_g", "forget_b", "ssd_conv_w", "ssd_conv_b", "ssd_dt_bias", "ssd_a_log",
    "ssd_d", "ssd_norm_g", "lru_conv_w", "lru_conv_b", "lru_w_a", "lru_b_a", "lru_w_x", "lru_b_x", "lru_lambda", "w_out",
    "c_2", "positions_2", "norm1_g_2", "norm2_g_2", "final_norm_g_2", "w_ada_2", "b_ada_2", "w_in_2", "w_gate_2",
    "b_gate_2", "ret_gn_g_2", "rwkv_mu_2", "rwkv_w0_2", "rwkv_w_lora_2", "rwkv_a0_2", "rwkv_a_lora_2", "rwkv_g_lora_2",
    "rwkv_k_k_2", "rwkv_k_a_2", "rwkv_r_k_2", "rwkv_gn_g_2", "conv_w_2", "w_branch_2", "w_o_2", "w_router_group_2",
    "b_router_group_2", "w_router_expert_2", "b_router_expert_2", "w_exp_gate_2", "w_exp_up_2", "w_exp_down_2",
]


def kernel(**inputs):
    import concourse.bacc as bacc
    from concourse.bass_utils import run_bass_kernel_spmd

    nc = bacc.Bacc("TRN2", target_bir_lowering=False, num_devices=1)
    arrays = {name: np.ascontiguousarray(inputs[name]) for name in INPUTS}
    for name, pieces in (("constants", constants()), ("first_constants", first_constants())):
        arrays[name] = np.concatenate(list(pieces.values()), axis=1)
    io = {name: nc.dram_tensor(f"in_{name}", a.shape, mybir.dt.from_np(a.dtype), kind="ExternalInput").ap()
          for name, a in arrays.items()}
    io["out"] = nc.dram_tensor("out", (1, S, D), F32, kind="ExternalOutput").ap()
    io["expert_weights"] = nc.dram_tensor("expert_weights", (N_E, S), F32, kind="Internal").ap()
    program(nc, io)
    result = run_bass_kernel_spmd(nc, [{f"in_{name}": a for name, a in arrays.items()}], core_ids=[0])
    return result.results[0]["out"]
```

```python
import math
from contextlib import ExitStack, contextmanager

import numpy as np
import concourse.bass as bass
from concourse import mybir

F32 = mybir.dt.float32
I32 = mybir.dt.int32
ALU = mybir.AluOpType
ACT = mybir.ActivationFunctionType
AX = mybir.AxisListType

P = 128
S = 256
NT = S // P
D = 1024
ND = D // P
EPS = 1e-6
LAYERS = 2

A_H, A_D = 8, 64
A_W = A_H * A_D
N_A = A_W // P
X_H, X_D, X_G = 16, 64, 2
X_W = X_H * X_D
N_X = X_W // P
X_C = X_W + 2 * X_G * P
N_C = X_C // P
L_W = 512
N_L = L_W // P
TAPS = 4
COL_Q, COL_F = 0, 4 * A_W
COL_ZX = COL_F + A_H
COL_XBC = COL_ZX + X_W
COL_DT = COL_XBC + X_C
COL_XL = COL_DT + X_H
COL_ZL = COL_XL + L_W
D_IN = COL_ZL + L_W
MIX = A_W + X_W + L_W

MW = 512
N_M = MW // P
R_H = MW // P
K_H = MW // 64
N_K = 3 * N_M + 2
IN_COLS = 4 * MW + 3 * MW + 256 + 3 * MW
N_E, N_G, FF = 32, 4, 512
E_G = N_E // N_G
N_F = FF // P
LW_SCALE = -math.exp(-0.5)

SLOTS = 3
SLAB = 4096
ADA = 256
ADA_SLOTS = 3
ADA_SUMS = 5
CAP = 64
N_PAIR = N_E // 2
BIG = 1e30



def constants():
    i = np.arange(P)
    r, c = i[:, None], i[None, :]
    out = {}
    out["ident"] = (r == c)
    out["mean_d"] = np.full((P, P), 1.0 / D)
    out["mean_512"] = np.full((P, P), 1.0 / 512)
    out["mean_128"] = np.full((P, P), 1.0 / P)
    out["sum_64"] = (r // 64 == c // 64)
    out["mean_64"] = (r // 64 == c // 64) / 64.0
    out["swap"] = np.where(r == c + 64, -1.0, np.where(c == r + 64, 1.0, 0.0))
    out["neg_upper"] = np.where(c > r, -BIG, 0.0)
    out["neg_lower"] = np.where(c < r, -BIG, 0.0)
    out["strict"] = (c > r)
    out["incl"] = (c >= r)
    n = 1
    while n < P:
        m = (r // (2 * n) == c // (2 * n)) & (r // n % 2 == 1) & (c // n % 2 == 0)
        out[f"level_{n}"] = m
        if n == 1:
            out["level_1t"] = m.T
        n *= 2
    out["inv_freq"] = (np.float32(10000.0) ** (-(np.arange(64, dtype=np.float32)) / np.float32(64)))[i % 64][:, None]
    rel = np.arange(S)[None, :] - i[:, None]
    for h in range(R_H):
        lg = math.log1p(-2.0 ** (-5.0 - h))
        out[f"decay_{h}"] = np.where(rel >= 0, np.exp(lg * np.maximum(rel, 0)), 0.0) * P ** -0.5
    out["iota"] = np.tile(np.arange(CAP, dtype=np.float64), (P, 1))
    return {k: np.asarray(v, np.float32) for k, v in out.items()}


def first_constants():
    r = np.arange(P)[:, None]
    out = {}
    out["pick_neg"] = -np.concatenate([np.tile(r == h, (1, P)) for h in range(A_H)], 1).astype(np.float32)
    out["pick"] = np.concatenate([np.tile(r == h, (1, P)) for h in range(X_H)], 1)
    half = np.arange(P)[None, :] // 64
    out["pick_pair"] = np.concatenate([r == 2 * j + half for j in range(N_X)], 1)
    return {k: np.asarray(v, np.float32) for k, v in out.items()}


def layout(pieces):
    at, out = 0, {}
    for name, a in pieces.items():
        out[name] = (at, a.shape[1])
        at += a.shape[1]
    return out, at



def chain(eng, sem):
    count = [0]

    def step(ins):
        count[0] += 1
        ins.then_inc(sem, 1)
        eng.wait_ge(sem, count[0])
    return step


class Core:

    def __init__(self, nc, ctx, io):
        self.nc, self.ctx, self.io = nc, ctx, io
        self.stages = 0
        self.live = []

    def sb(self, name, shape, dt=F32, ctx=None):
        return (ctx or self.ctx).enter_context(self.nc.sbuf_tensor(name, shape, dt))

    def const(self, name):
        at, n = self.columns[name]
        return self.consts[:, at:at + n]

    @contextmanager
    def stage(self, *names):
        self.stages += 1
        sems = [self.nc.alloc_semaphore(name=f"{n}_{self.stages}") for n in names]
        self.live += sems
        with self.nc.Block() as block:
            yield (block, *sems)

    def clear_semaphores(self):
        self.nc.all_engine_barrier()
        for sem in self.live:
            self.nc.sync.sem_clear(sem)
        self.nc.all_engine_barrier()
        for sem in reversed(self.live):
            self.nc.release_semaphore(sem)
        self.live = []


def slab_view(k, slot, rows, cols):
    n = rows // P
    return k.ring[:, slot, 0:n * cols].rearrange("p (k c) -> p k c", k=n)


def load_slabs(eng, k, slabs, loaded, used, per_slab):
    for i, src in enumerate(slabs):
        if i >= SLOTS:
            eng.wait_ge(used, sum(per_slab[:i - SLOTS + 1]))
        n, c = src.shape[1], src.shape[2]
        dst = k.ring[:, i % SLOTS, 0:n * c].rearrange("p (k c) -> p k c", k=n)
        eng.dma_start(dst, src).then_inc(loaded[i % SLOTS], 16)


LOADED = tuple(f"slot{i}_loaded" for i in range(SLOTS))


def wait_slab(eng, loaded, i):
    eng.wait_ge(loaded[i % SLOTS], 16 * (i // SLOTS + 1))


def ada_sources(io):
    w = io["w_ada_2"].rearrange("l (k p) c -> l p k c", p=P)
    return [w[l, :, :, i * ADA:(i + 1) * ADA] for l in range(LAYERS) for i in range(6 * D // ADA)]


def project(k, slabs, tiles, rhs, evac_engine="scalar", side=0):
    nc = k.nc
    per_slab = [sum(1 for t in tiles if t[0] == i) for i in range(len(slabs))]
    first = k.ada_at
    k.ada_at += side
    pieces = ada_sources(k.io)[first:first + side]
    due = [[p for p in range(side) if p * len(tiles) // side == n] for n in range(len(tiles))]
    names = (*(f"ada{i}_loaded" for i in range(ADA_SLOTS)), "ada_used", "ada_step", "ada_summed", "ada_turned") if side else ()
    with k.stage(*LOADED, "tile_done", "tile_stored", *names) as (block, *sems):
        loaded, (done, stored) = sems[:SLOTS], sems[SLOTS:SLOTS + 2]
        if side:
            ada_loaded, (ada_used, ada_step, ada_summed, ada_turned) = sems[SLOTS + 2:-4], sems[-4:]

        @block.sync
        def _(sp):
            load_slabs(sp, k, slabs, loaded, done, per_slab)

        def load_piece(act, p):
            if p >= ADA_SLOTS:
                act.wait_ge(ada_used, p - ADA_SLOTS + 1)
            act.dma_start(k.ada_ring[:, p % ADA_SLOTS, :, :], pieces[p]).then_inc(ada_loaded[p % ADA_SLOTS], 16)

        def sum_piece(dve, p):
            dve.wait_ge(ada_loaded[p % ADA_SLOTS], 16 * (p // ADA_SLOTS + 1))
            if p >= ADA_SUMS:
                dve.wait_ge(ada_turned, p - ADA_SUMS + 1)
            acc = k.ada_sum[:, p % ADA_SUMS, :]
            for j in range(ND):
                src, c = k.ada_ring[:, p % ADA_SLOTS, j, :], k.c_silu[:, j:j + 1]
                if j == 0:
                    ins = nc.vector.tensor_scalar(acc, src, c, None, ALU.mult)
                else:
                    dve.wait_ge(ada_step, p * (ND - 1) + j)
                    ins = nc.vector.scalar_tensor_tensor(acc, src, c, acc, ALU.mult, ALU.add)
                if j < ND - 1:
                    ins.then_inc(ada_step, 1)
            ins.then_inc(ada_used, 1)
            dve.wait_ge(ada_used, p + 1)
            dve.sem_inc(ada_summed, 1)

        def turn_piece(pe, p):
            pe.wait_ge(ada_summed, p + 1)
            for c in range(ADA // P):
                ins = nc.tensor.matmul(k.ps[:, 7, p * ADA // P + c:p * ADA // P + c + 1],
                                       k.ada_sum[:, p % ADA_SUMS, c * P:(c + 1) * P], k.ones[:, 0:1], start=True, stop=True)
            ins.then_inc(ada_turned, 1)

        @block.tensor
        def _(pe):
            last_slab = -1
            for n, (i, c0, w, how, _) in enumerate(tiles):
                if i != last_slab:
                    wait_slab(pe, loaded, i)
                    last_slab = i
                if n >= 4:
                    pe.wait_ge(stored, n - 3)
                nk = slabs[i].shape[1]
                slab = slab_view(k, i % SLOTS, nk * P, slabs[i].shape[2])
                ps = k.ps[:, n % 4, :]
                for j in range(nk):
                    if how == "f":
                        ins = nc.tensor.matmul(ps[0:w, 0:S], slab[:, j, c0:c0 + w], rhs[:, j, :],
                                               start=j == 0, stop=j == nk - 1)
                    else:
                        ins = nc.tensor.matmul(ps[:, 0:w], rhs[:, j, how * P:(how + 1) * P],
                                               slab[:, j, c0:c0 + w], start=j == 0, stop=j == nk - 1)
                ins.then_inc(done, 1)
                for p in due[n - 2] if n >= 2 else ():
                    turn_piece(pe, p)
            for p in due[-2] + due[-1]:
                turn_piece(pe, p)

        def store(eng, n):
            eng.wait_ge(done, n + 1)
            tiles[n][4](eng, k.ps[:, n % 4, :]).then_inc(stored, 1)

        if side or evac_engine == "scalar":
            @block.scalar
            def _(act):
                if side:
                    for p in range(ADA_SLOTS - 1):
                        load_piece(act, p)
                for n in range(len(tiles)):
                    for p in due[n]:
                        if p + ADA_SLOTS - 1 < side:
                            load_piece(act, p + ADA_SLOTS - 1)
                    if evac_engine == "scalar":
                        store(act, n)

        if side or evac_engine == "vector":
            @block.vector
            def _(dve):
                for n in range(len(tiles)):
                    for p in due[n]:
                        sum_piece(dve, p)
                    if evac_engine == "vector":
                        store(dve, n)
                if side:
                    dve.wait_ge(ada_turned, side)
                    at, n = first * ADA // P, side * ADA // P
                    nc.vector.tensor_copy(k.mods[:, at:at + n], k.ps[:, 7, 0:n])


def copy_to(dst, w=P, n=S, func=ACT.Copy):
    return lambda eng, ps: eng.activation(dst, ps[0:w, 0:n], func)


def rms_norm(k, src, dst, gain, shift=None):
    nc = k.nc
    with k.stage("squared", "mean_done", "rstd_done", "ln_done", "vec_chain") as (
            block, squared, mean_done, rstd_done, ln_done, vec_chain):

        @block.scalar
        def _(act):
            nc.scalar.activation(dst, src, ACT.Square).then_inc(squared, 1)
            act.wait_ge(mean_done, 1)
            nc.scalar.activation(k.rstd[:, :], k.ps[:, 0, 0:S], ACT.Ln, bias=k.eps[:, 0:1]).then_inc(ln_done, 1)
            act.wait_ge(ln_done, 1)
            nc.scalar.activation(k.rstd[:, :], k.rstd[:, :], ACT.Exp, scale=-0.5).then_inc(rstd_done, 1)

        @block.tensor
        def _(pe):
            pe.wait_ge(squared, 1)
            for j in range(ND):
                ins = nc.tensor.matmul(k.ps[:, 0, 0:S], k.const("mean_d"), dst[:, j, :],
                                       start=j == 0, stop=j == ND - 1)
            ins.then_inc(mean_done, 1)

        @block.vector
        def _(dve):
            dve.wait_ge(rstd_done, 1)
            for j in range(ND):
                nc.vector.scalar_tensor_tensor(dst[:, j, :], src[:, j, :], gain[:, j:j + 1], k.rstd[:, :],
                                               ALU.mult, ALU.mult).then_inc(vec_chain, 1)
            if shift is not None:
                for j in range(ND):
                    dve.wait_ge(vec_chain, j + 1)
                    nc.vector.tensor_scalar(dst[:, j, :], dst[:, j, :], shift[:, j:j + 1], None, ALU.add)


def log1p_steps(nc, step, out, z, w, w2):
    step(nc.vector.tensor_scalar(w2, z, 2.0, None, ALU.add))
    step(nc.vector.reciprocal(w2, w2))
    step(nc.vector.tensor_tensor(w, z, w2, ALU.mult))
    step(nc.vector.tensor_tensor(w2, w, w, ALU.mult))
    step(nc.vector.tensor_scalar(out, w2, 2.0 / 17, None, ALU.mult))
    for n in range(15, 1, -2):
        step(nc.vector.scalar_tensor_tensor(out, out, 2.0 / n, w2, ALU.add, ALU.mult))
    step(nc.vector.scalar_tensor_tensor(out, out, 2.0, w, ALU.add, ALU.mult))


def load_rows(k, parts):
    nc = k.nc
    at, where, used = 0, {}, [0, 0]
    for name, r, _ in parts:
        if at // P != (at + r - 1) // P:
            at = (at + P - 1) // P * P
        where[name] = (at, r)
        at += r
        used[(at - 1) // P] = (at - 1) % P + 1
    assert at <= 2 * P
    tiles = [g for g in range(2) if used[g]]
    loads = sum(len(pieces) for _, _, pieces in parts)
    with k.stage("rows_loaded", "rows_turned") as (block, loaded, turned):

        @block.sync
        def _(sp):
            for name, r, pieces in parts:
                a, g = where[name][0] % P, where[name][0] // P
                for c0, src in pieces:
                    w = math.prod(src.shape[1:])
                    dst = k.rows[a:a + r, g, c0:c0 + w]
                    if src.ndim == 3:
                        dst = dst.rearrange("r (a b) -> r a b", a=src.shape[1])
                    sp.dma_start(dst, src).then_inc(loaded, 16)

        @block.tensor
        def _(pe):
            pe.wait_ge(loaded, 16 * loads)
            for g in tiles:
                ins = nc.tensor.transpose(k.ps[:, g, 0:used[g]], k.rows[0:used[g], g, :],
                                          k.const("ident")[0:used[g], 0:used[g]])
            ins.then_inc(turned, 1)

        @block.vector
        def _(dve):
            dve.wait_ge(turned, 1)
            for g in tiles:
                nc.vector.tensor_copy(k.cols[:, g * P:g * P + used[g]], k.ps[:, g, 0:used[g]])
    return {name: k.cols[:, a:a + r] for name, (a, r) in where.items()}



def load_inputs(k):
    nc, io = k.nc, k.io
    with ExitStack() as tmp:
        x_tok = k.sb("x_tok", [P, NT, D], ctx=tmp)
        with k.stage("consts_loaded", "x_loaded", "turned", "copied") as (block, consts_loaded, x_loaded, turned, copied):

            @block.sync
            def _(sp):
                sp.dma_start(x_tok[:, :, :], io["x"][0].rearrange("(t p) d -> p t d", p=P)).then_inc(x_loaded, 16)
                sp.dma_start(k.consts[:, :], io["constants"]).then_inc(consts_loaded, 16)

            @block.gpsimd
            def _(pool):
                nc.gpsimd.memset(k.eps[:, 0:1], EPS)
                nc.gpsimd.memset(k.eps[:, 1:2], 1e-5)
                nc.gpsimd.memset(k.eps[:, 2:3], 64e-5)
                nc.gpsimd.memset(k.ones[:, :], 1.0)

            @block.tensor
            def _(pe):
                pe.wait_ge(consts_loaded, 16)
                pe.wait_ge(x_loaded, 16)
                for j in range(ND):
                    for t in range(NT):
                        ins = nc.tensor.transpose(k.ps[:, j, t * P:(t + 1) * P], x_tok[:, t, j * P:(j + 1) * P],
                                                  k.const("ident"))
                ins.then_inc(turned, 1)

            @block.vector
            def _(dve):
                dve.wait_ge(turned, 1)
                nc.vector.tensor_copy(k.x[:, :, :], k.ps[:, :, 0:S])


def attention(k, cols, u, mix):
    nc, io = k.nc, k.io
    w_in = io["w_in"][0].rearrange("(k p) c -> p k c", p=P)
    with ExitStack() as mem:
        q_raw = k.sb("q_raw", [P, N_A, S], ctx=mem)
        k_raw = k.sb("k_raw", [P, N_A, S], ctx=mem)
        z = k.sb("z_att", [P, N_A, S], ctx=mem)
        q_pad = k.sb("q_pad", [P, N_A, 2, S], ctx=mem)
        v_pad = k.sb("v_pad", [P, NT, A_H, P], ctx=mem)
        v_pairs = v_pad[:, :, :, :].rearrange("p t (j h) c -> p t j h c", h=2)
        f = k.sb("f", [P, S], ctx=mem)
        probs = k.sb("probs", [P, A_H, 3 * P], ctx=mem)
        probs_t = k.sb("probs_t", [P, A_H, 3 * P], ctx=mem)
        square = probs[:, :, :].rearrange("p h c -> p (h c)")[:, 0:N_A * S]
        peak = k.sb("peak", [P, A_H, 2], ctx=mem)
        total = k.sb("total", [P, A_H, 2], ctx=mem)
        small = k.sb("small_a", [P, 4, S], ctx=mem)

        with k.stage("cleared") as (block, cleared):
            @block.gpsimd
            def _(pool):
                nc.gpsimd.memset(v_pad[:, :, :, :], 0.0)
                nc.gpsimd.memset(q_pad[:, :, :, :], 0.0)
                nc.gpsimd.memset(f[:, :], 0.0)

        def store_v(t):
            def store(eng, ps):
                src = ps[:, 0:A_W].rearrange("p (j h c) -> p j h c", h=2, c=A_D)
                eng.activation(v_pairs[:, t, :, 0, 0:A_D], src[:, :, 0, :], ACT.Copy)
                return eng.activation(v_pairs[:, t, :, 1, A_D:P], src[:, :, 1, :], ACT.Copy)
            return store

        slabs = [w_in[:, :, i * A_W:(i + 1) * A_W] for i in range(4)] + [w_in[:, :, COL_F:COL_F + A_H]]
        tiles = [(0, j * P, P, "f", copy_to(q_raw[:, j, :])) for j in range(N_A)]
        tiles += [(1, j * P, P, "f", copy_to(k_raw[:, j, :])) for j in range(N_A)]
        tiles += [(2, 0, A_W, t, store_v(t)) for t in range(NT)]
        tiles += [(3, j * P, P, "f", copy_to(z[:, j, :], func=ACT.Silu)) for j in range(N_A)]
        tiles += [(4, 0, A_H, "f", copy_to(f[0:A_H, :], w=A_H))]
        project(k, slabs, tiles, u, side=13)

        flat = lambda t: t[:, :, :].rearrange("p j s -> p (j s)")
        with k.stage("squared", "summed", "rstd_done", "scaled", "neg_abs", "exp_done", "act_chain", "vec_chain") as (
                block, squared, summed, rstd_done, scaled, neg_abs, exp_done, act_chain, vec_chain):

            @block.scalar
            def _(act):
                step = chain(act, act_chain)
                for n, src in enumerate((k_raw, q_raw)):
                    if n:
                        act.wait_ge(scaled, 1)
                    nc.scalar.activation(square, flat(src), ACT.Square).then_inc(squared, 1)
                    act.wait_ge(summed, n + 1)
                    step(nc.scalar.activation(square.rearrange("p (b s) -> p b s", b=2), k.ps[:, 0:2, :], ACT.Ln,
                                              bias=k.eps[:, 0:1]))
                    nc.scalar.activation(square, square, ACT.Exp, scale=-0.5).then_inc(rstd_done, 1)
                act.wait_ge(neg_abs, 1)
                nc.scalar.activation(small[0:A_H, 1, :], small[0:A_H, 1, :], ACT.Exp).then_inc(exp_done, 1)

            @block.tensor
            def _(pe):
                for n in range(2):
                    pe.wait_ge(squared, n + 1)
                    for b in range(2):
                        ins = nc.tensor.matmul(k.ps[:, b, :], k.const("mean_64"), square[:, b * 512:(b + 1) * 512],
                                               start=True, stop=True)
                    ins.then_inc(summed, 1)

            @block.vector
            def _(dve):
                step = chain(dve, vec_chain)
                y, e, w, w2 = (small[0:A_H, i, :] for i in range(4))
                step(nc.vector.tensor_scalar(y, f[0:A_H, :], k.forget_b[0:A_H, :], -1.0, ALU.add, ALU.mult))
                nc.vector.scalar_tensor_tensor(e, y, -1.0, y, ALU.mult, ALU.min).then_inc(neg_abs, 1)
                dve.wait_ge(rstd_done, 1)
                nc.vector.scalar_tensor_tensor(flat(k_raw), flat(k_raw), cols["k_norm"], square,
                                               ALU.mult, ALU.mult).then_inc(scaled, 1)
                step(nc.vector.tensor_scalar(cols["q_norm"], cols["q_norm"], A_D ** -0.5, None, ALU.mult))
                dve.wait_ge(rstd_done, 2)
                sq = square.rearrange("p (j s) -> p j s", j=N_A)
                for h in range(2):
                    r = slice(h * 64, h * 64 + 64)
                    nc.vector.scalar_tensor_tensor(q_pad[r, :, h, :], q_raw[r, :, :], cols["q_norm"][r, :],
                                                   sq[r, :, :], ALU.mult, ALU.mult)
                dve.wait_ge(exp_done, 1)
                log1p_steps(nc, step, f[0:A_H, :], e, w, w2)
                step(nc.vector.scalar_tensor_tensor(e, y, 0.0, f[0:A_H, :], ALU.max, ALU.add))
                step(nc.vector.tensor_scalar(e, e, -1.0, None, ALU.mult))
                step(nc.vector.tensor_tensor_scan(f[0:A_H, :], k.ones[0:A_H, :], e, 0.0, ALU.mult, ALU.add))

        spans = ((0, 0, P), (1, P, 3 * P))
        with k.stage("logits_done", "peak_done", "exps_done", "scaled", "turned", "copied", "out_done", "vec_chain") as (
                block, logits_done, peak_done, exps_done, scaled, turned, copied, out_done, vec_chain):

            @block.tensor
            def _(pe):
                for g in range(2):
                    if g:
                        pe.wait_ge(exps_done, 8)
                    for h in range(4 * g, 4 * g + 4):
                        for t, a, b in spans:
                            ps = k.ps[:, h % 4, a:b]
                            nc.tensor.matmul(ps, q_pad[:, h // 2, h % 2, t * P:(t + 1) * P], k_raw[:, h // 2, 0:b - a],
                                             start=True, stop=False)
                            nc.tensor.matmul(ps, k.first_const("pick_neg", h), f[:, 0:b - a], start=False, stop=False)
                            ins = nc.tensor.matmul(k.ps[:, h % 4, b - P:b], k.const("ident"), k.const("neg_upper"),
                                                   start=False, stop=True)
                        ins.then_inc(logits_done, 1)
                for g in range(2):
                    pe.wait_ge(scaled, g + 1)
                    if g:
                        pe.wait_ge(copied, 4)
                    for h in range(4 * g, 4 * g + 4):
                        for b in range(3):
                            ins = nc.tensor.transpose(k.ps[:, 4 + h % 4, b * P:(b + 1) * P],
                                                      probs[:, h, b * P:(b + 1) * P], k.const("ident"))
                        ins.then_inc(turned, 1)
                pe.wait_ge(copied, 8)
                for j in range(N_A):
                    for t in range(NT):
                        todo = [(h, s) for h in (2 * j, 2 * j + 1) for s in range(t + 1)]
                        for n, (h, s) in enumerate(todo):
                            c = (0, 1, 2)[t if s == 0 else 2]
                            ins = nc.tensor.matmul(k.ps[:, j, t * P:(t + 1) * P], v_pad[:, s, h, :],
                                                   probs_t[:, h, c * P:(c + 1) * P],
                                                   start=n == 0, stop=n == len(todo) - 1)
                ins.then_inc(out_done, 1)

            @block.scalar
            def _(act):
                for h in range(A_H):
                    act.wait_ge(peak_done, h + 1)
                    for t, a, b in spans:
                        nc.scalar.activation(probs[:, h, a:b], k.ps[:, h % 4, a:b], ACT.Exp, bias=peak[:, h, t:t + 1],
                                             accum_out=total[:, h, t:t + 1]).then_inc(exps_done, 1)

            @block.vector
            def _(dve):
                step = chain(dve, vec_chain)
                for h in range(A_H):
                    dve.wait_ge(logits_done, h + 1)
                    for t, a, b in spans:
                        ins = nc.vector.tensor_reduce(peak[:, h, t:t + 1], k.ps[:, h % 4, a:b], AX.X, ALU.max)
                    step(ins)
                    nc.vector.tensor_scalar(peak[:, h, :], peak[:, h, :], -1.0, None, ALU.mult).then_inc(peak_done, 1)
                for g in range(2):
                    heads = slice(4 * g, 4 * g + 4)
                    dve.wait_ge(exps_done, 8 * (g + 1))
                    step(nc.vector.reciprocal(total[:, heads, :], total[:, heads, :]))
                    for t, a, b in spans:
                        ins = nc.vector.tensor_tensor(probs[:, heads, a:b], probs[:, heads, a:b],
                                                      total[:, heads, t:t + 1].broadcast_to([P, 4, b - a]), ALU.mult)
                    ins.then_inc(scaled, 1)
                for h in range(A_H):
                    dve.wait_ge(turned, h + 1)
                    nc.vector.tensor_copy(probs_t[:, h, :], k.ps[:, 4 + h % 4, 0:3 * P]).then_inc(copied, 1)
                dve.wait_ge(out_done, 1)
                nc.vector.tensor_tensor(mix[:, 0:N_A, :], k.ps[:, 0:N_A, 0:S], z[:, :, :], ALU.mult)


def causal_conv(nc, dve, sem, n_tiles, src, dst, weights, bias, first=0):
    for i in range(TAPS):
        for j in range(n_tiles):
            if i:
                dve.wait_ge(sem, first + (i - 1) * n_tiles + j + 1)
                ins = nc.vector.scalar_tensor_tensor(dst[:, j, :], src[:, j, i:i + S], weights(i)[:, j:j + 1],
                                                     dst[:, j, :], ALU.mult, ALU.add)
            else:
                ins = nc.vector.tensor_scalar(dst[:, j, :], src[:, j, 0:S], weights(0)[:, j:j + 1],
                                              bias[:, j:j + 1], ALU.mult, ALU.add)
            ins.then_inc(sem, 1)


def ssd(k, cols, u, mix):
    nc, io = k.nc, k.io
    w_in = io["w_in"][0].rearrange("(k p) c -> p k c", p=P)
    with ExitStack() as mem:
        xc = k.sb("xc", [P, N_C, S], ctx=mem)
        z = k.sb("z_ssd", [P, N_X, S], ctx=mem)
        dt = k.sb("dt", [P, S], ctx=mem)
        cs = k.sb("a_cs", [P, S], ctx=mem)
        neg_cs = k.sb("neg_a_cs", [P, S], ctx=mem)
        with ExitStack() as tmp:
            raw = k.sb("xbc_raw", [P, N_C, S + TAPS - 1], ctx=tmp)
            small = k.sb("small_x", [P, 4, S], ctx=tmp)
            with k.stage("cleared") as (block, cleared):
                @block.gpsimd
                def _(pool):
                    nc.gpsimd.memset(raw[:, :, 0:TAPS - 1], 0.0)
                    for t in (dt, cs, neg_cs):
                        nc.gpsimd.memset(t[:, :], 0.0)

            slabs = [w_in[:, :, COL_XBC + i * 512:COL_XBC + (i + 1) * 512] for i in range(3)]
            slabs += [w_in[:, :, COL_DT:COL_DT + X_H]]
            slabs += [w_in[:, :, COL_ZX + i * 512:COL_ZX + (i + 1) * 512] for i in range(2)]
            tiles = [(j // 4, j % 4 * P, P, "f", copy_to(raw[:, j, TAPS - 1:])) for j in range(N_C)]
            tiles += [(3, 0, X_H, "f", copy_to(dt[0:X_H, :], w=X_H))]
            tiles += [(4 + j // 4, j % 4 * P, P, "f", copy_to(z[:, j, :], func=ACT.Silu)) for j in range(N_X)]
            project(k, slabs, tiles, u, side=15)

            with k.stage("conv_done", "neg_abs", "exp_done", "rate_done", "vec_chain") as (
                    block, conv_done, neg_abs, exp_done, rate_done, vec_chain):

                @block.scalar
                def _(act):
                    act.wait_ge(neg_abs, 1)
                    nc.scalar.activation(small[0:X_H, 1, :], small[0:X_H, 1, :], ACT.Exp).then_inc(exp_done, 1)
                    nc.scalar.activation(k.a_log[0:X_H, :], k.a_log[0:X_H, :], ACT.Exp).then_inc(rate_done, 1)
                    act.wait_ge(conv_done, TAPS * N_C)
                    nc.scalar.activation(xc[:, :, :], xc[:, :, :], ACT.Silu)

                @block.vector
                def _(dve):
                    step = chain(dve, vec_chain)
                    y, e, w, w2 = (small[0:X_H, i, :] for i in range(4))
                    step(nc.vector.tensor_scalar(y, dt[0:X_H, :], k.dt_bias[0:X_H, :], None, ALU.add))
                    nc.vector.scalar_tensor_tensor(e, y, -1.0, y, ALU.mult, ALU.min).then_inc(neg_abs, 1)
                    dve.wait_ge(exp_done, 1)
                    log1p_steps(nc, step, dt[0:X_H, :], e, w, w2)
                    step(nc.vector.scalar_tensor_tensor(dt[0:X_H, :], y, 0.0, dt[0:X_H, :], ALU.max, ALU.add))
                    dve.wait_ge(rate_done, 1)
                    step(nc.vector.tensor_scalar(e, dt[0:X_H, :], k.a_log[0:X_H, :], -1.0, ALU.mult, ALU.mult))
                    for c in range(NT):
                        r = slice(c * P, (c + 1) * P)
                        step(nc.vector.tensor_tensor_scan(cs[0:X_H, r], k.ones[0:X_H, 0:P], e[:, r], 0.0,
                                                          ALU.mult, ALU.add))
                    step(nc.vector.tensor_scalar(neg_cs[0:X_H, :], cs[0:X_H, :], -1.0, None, ALU.mult))
                    causal_conv(nc, dve, conv_done, N_C, raw, xc, lambda i: cols["ssd_w"][:, i * N_C:(i + 1) * N_C],
                                cols["ssd_b"])

        x_dt = k.sb("x_dt", [P, NT, X_H, P], ctx=mem)
        x_pairs = x_dt[:, :, :, :].rearrange("p t (j h) c -> p t j h c", h=2)
        x_dec = k.sb("x_dec", [P, X_W], ctx=mem)
        b_tok = k.sb("b_tok", [P, X_G, P], ctx=mem)
        cb = k.sb("cb", [P, X_G * NT, P], ctx=mem)
        state = k.sb("state_x", [P, X_G, 512], ctx=mem)
        y_off = k.sb("y_off", [P, N_X, P], ctx=mem)
        grow = k.sb("grow", [P, N_X, P], ctx=mem)
        dec = k.sb("dec", [P, P], ctx=mem)
        dt_tok = k.sb("dt_tok", [P, 3, X_H], ctx=mem)
        with k.stage("dec_done", "dt_turned", "dt_copied", "turned", "x_copied", "cb_done", "cb_copied", "state_done",
                     "state_copied", "off_done", "grow_done", "cleared", "vec_chain") as (
                block, dec_done, dt_turned, dt_copied, turned, x_copied, cb_done, cb_copied, state_done,
                state_copied, off_done, grow_done, cleared, vec_chain):

            @block.gpsimd
            def _(pool):
                nc.gpsimd.memset(x_dt[:, :, :, :], 0.0).then_inc(cleared, 1)
                nc.gpsimd.memset(dec[:, :], 0.0).then_inc(cleared, 1)

            @block.scalar
            def _(act):
                act.wait_ge(cleared, 2)
                nc.scalar.activation(dec[0:X_H, :], cs[0:X_H, 0:P], ACT.Exp, bias=cs[0:X_H, P - 1:P],
                                     scale=-1.0).then_inc(dec_done, 1)
                act.wait_ge(cb_done, 1)
                nc.scalar.activation(cb[:, :, :], k.ps[:, 1, :].rearrange("p (n c) -> p n c", c=P), ACT.Copy)
                act.wait_ge(state_done, 1)
                nc.scalar.activation(state[:, :, :], k.ps[:, 2:4, :], ACT.Copy).then_inc(state_copied, 1)
                act.wait_ge(off_done, 2)
                nc.scalar.activation(grow[:, :, :].rearrange("p (b j) c -> p b (j c)", b=2), k.ps[:, 6:8, :],
                                     ACT.Exp).then_inc(grow_done, 1)

            @block.tensor
            def _(pe):
                pe.wait_ge(dec_done, 2)
                for n, src in enumerate((dt[:, 0:P], dt[:, P:S], dec[:, :])):
                    ins = nc.tensor.transpose(k.ps[:, 0, n * P:(n + 1) * P], src, k.const("ident"))
                ins.then_inc(dt_turned, 1)
                for g in range(X_G):
                    for c in range(NT):
                        r = slice(c * P, (c + 1) * P)
                        n = g * NT + c
                        ins = nc.tensor.matmul(k.ps[:, 1, n * P:(n + 1) * P], xc[:, N_X + g, r],
                                               xc[:, N_X + X_G + g, r], start=True, stop=True)
                ins.then_inc(cb_done, 1)
                for t in range(NT):
                    if t:
                        pe.wait_ge(x_copied, t)
                    for j in range(N_X):
                        ins = nc.tensor.transpose(k.ps[:, 4 + j // 4, j % 4 * P:(j % 4 + 1) * P],
                                                  xc[:, j, t * P:(t + 1) * P], k.const("ident"))
                    ins.then_inc(turned, 1)
                for g in range(X_G):
                    ins = nc.tensor.transpose(k.ps[:, 6, g * P:(g + 1) * P], xc[:, N_X + g, 0:P], k.const("ident"))
                ins.then_inc(turned, 1)
                pe.wait_ge(x_copied, 3)
                for g in range(X_G):
                    ins = nc.tensor.matmul(k.ps[:, 2 + g, :], b_tok[:, g, :], x_dec[:, g * 512:(g + 1) * 512],
                                           start=True, stop=True)
                ins.then_inc(state_done, 1)
                pe.wait_ge(state_copied, 1)
                for j in range(N_X):
                    ins = nc.tensor.matmul(k.ps[:, 4 + j // 4, j % 4 * P:(j % 4 + 1) * P],
                                           state[:, j // 4, j % 4 * P:(j % 4 + 1) * P],
                                           xc[:, N_X + X_G + j // 4, P:S], start=True, stop=True)
                ins.then_inc(off_done, 1)
                for j in range(N_X):
                    ins = nc.tensor.matmul(k.ps[:, 6 + j // 4, j % 4 * P:(j % 4 + 1) * P],
                                           k.first_const("pick_pair", j), cs[:, P:S], start=True, stop=True)
                ins.then_inc(off_done, 1)

            @block.vector
            def _(dve):
                step = chain(dve, vec_chain)
                dve.wait_ge(dec_done, 1)
                nc.vector.tensor_tensor(dec[0:X_H, :], dec[0:X_H, :], dt[0:X_H, 0:P], ALU.mult).then_inc(dec_done, 1)
                dve.wait_ge(dt_turned, 1)
                step(nc.vector.tensor_copy(dt_tok[:, :, :], k.ps[:, 0, 0:3 * P].rearrange("p (n c) -> p n c", c=P)[:, :, 0:X_H]))
                dve.wait_ge(cleared, 2)
                for t in range(NT):
                    dve.wait_ge(turned, t + 1)
                    src = k.ps[:, 4:6, :].rearrange("p b (j h c) -> p (b j) h c", h=2, c=X_D)
                    by = dt_tok[:, t, :].rearrange("p (j h) -> p j h", h=2)
                    if t == 0:
                        by_dec = dt_tok[:, 2, :].rearrange("p (j h) -> p j h", h=2)
                        out = x_dec[:, :].rearrange("p (j h c) -> p j h c", h=2, c=X_D)
                        for h in range(2):
                            nc.vector.tensor_tensor(out[:, :, h, :], src[:, :, h, :],
                                                    by_dec[:, :, h:h + 1].broadcast_to([P, N_X, X_D]), ALU.mult)
                    for h in range(2):
                        ins = nc.vector.tensor_tensor(x_pairs[:, t, :, h, h * X_D:(h + 1) * X_D], src[:, :, h, :],
                                                      by[:, :, h:h + 1].broadcast_to([P, N_X, X_D]), ALU.mult)
                    ins.then_inc(x_copied, 1)
                dve.wait_ge(turned, 3)
                nc.vector.tensor_copy(b_tok[:, :, :], k.ps[:, 6, 0:X_G * P].rearrange("p (g c) -> p g c", g=X_G)).then_inc(x_copied, 1)
                dve.wait_ge(grow_done, 1)
                nc.vector.tensor_tensor(y_off[:, :, :], k.ps[:, 4:6, :].rearrange("p b (j c) -> p (b j) c", c=P),
                                        grow[:, :, :], ALU.mult)

        lmat = k.sb("lmat", [P, 2, 4, P], ctx=mem)
        rounds = [(c, q) for c in range(NT) for q in range(4)]
        with k.stage("seg_done", "lmat_done", "masked", "y_done", "y_stored", "squared", "summed", "ln_done",
                     "rstd_done", "vec_chain", "gated") as (
                block, seg_done, lmat_done, masked, y_done, y_stored, squared, summed, ln_done, rstd_done,
                vec_chain, gated):
            rstd = grow[:, 0:4, :].rearrange("p (g t) c -> p g (t c)", g=X_G)
            sq = x_dec[:, :].rearrange("p (j s) -> p j s", s=S)

            @block.tensor
            def _(pe):
                def segments(n):
                    c, q = rounds[n]
                    r = slice(c * P, (c + 1) * P)
                    if n >= 2:
                        pe.wait_ge(lmat_done, n - 1)
                    for i in range(4):
                        h = 4 * q + i
                        ps = k.ps[:, n % 2, i * P:(i + 1) * P]
                        nc.tensor.matmul(ps, k.first_const("pick", h), cs[:, r], start=True, stop=False)
                        nc.tensor.matmul(ps, neg_cs[:, r], k.first_const("pick", h), start=False, stop=False)
                        ins = nc.tensor.matmul(ps, k.const("ident"), k.const("neg_lower"), start=False, stop=True)
                    ins.then_inc(seg_done, 1)

                segments(0)
                for n, (c, q) in enumerate(rounds):
                    if n + 1 < len(rounds):
                        segments(n + 1)
                    pe.wait_ge(masked, n + 1)
                    if n >= 2:
                        pe.wait_ge(y_stored, n - 1)
                    for j in range(2):
                        for i in range(2):
                            h = 4 * q + 2 * j + i
                            ins = nc.tensor.matmul(k.ps[:, 2 + n % 2, j * P:(j + 1) * P], x_dt[:, c, h, :],
                                                   lmat[:, n % 2, 2 * j + i, :], start=i == 0, stop=i == 1)
                    ins.then_inc(y_done, 1)
                for g in range(X_G):
                    pe.wait_ge(squared, g + 1)
                    for j in range(4):
                        ins = nc.tensor.matmul(k.ps[:, 4 + g, 0:S], k.const("mean_512"), sq[:, j, :],
                                               start=j == 0, stop=j == 3)
                    ins.then_inc(summed, 1)

            @block.scalar
            def _(act):
                for n in range(len(rounds)):
                    act.wait_ge(seg_done, n + 1)
                    if n >= 2:
                        act.wait_ge(y_done, n - 1)
                    nc.scalar.activation(lmat[:, n % 2, :, :].rearrange("p i c -> p (i c)"), k.ps[:, n % 2, :],
                                         ACT.Exp).then_inc(lmat_done, 1)
                act.wait_ge(gated, 1)
                for g in range(X_G):
                    if g:
                        act.wait_ge(summed, g)
                    nc.scalar.activation(sq, mix[:, N_A + 4 * g:N_A + 4 * g + 4, :], ACT.Square).then_inc(squared, 1)
                act.wait_ge(summed, 2)
                nc.scalar.activation(rstd, k.ps[:, 4:6, 0:S], ACT.Ln, bias=k.eps[:, 0:1]).then_inc(ln_done, 1)
                act.wait_ge(ln_done, 1)
                nc.scalar.activation(rstd, rstd, ACT.Exp, scale=-0.5).then_inc(rstd_done, 1)

            @block.vector
            def _(dve):
                for n, (c, q) in enumerate(rounds):
                    g = q // 2
                    dve.wait_ge(lmat_done, n + 1)
                    nc.vector.tensor_tensor(lmat[:, n % 2, :, :], lmat[:, n % 2, :, :],
                                            cb[:, g * NT + c:g * NT + c + 1, :].broadcast_to([P, 4, P]), ALU.mult
                                            ).then_inc(masked, 1)
                    dve.wait_ge(y_done, n + 1)
                    r = slice(c * P, (c + 1) * P)
                    for i in range(2):
                        j = 2 * q + i
                        ins = nc.vector.scalar_tensor_tensor(mix[:, N_A + j, r], xc[:, j, r], cols["ssd_d"][:, j:j + 1],
                                                             k.ps[:, 2 + n % 2, i * P:(i + 1) * P], ALU.mult, ALU.add)
                    ins.then_inc(y_stored, 1)
                dve.wait_ge(y_stored, len(rounds))
                y = mix[:, N_A:N_A + N_X, :]
                step = chain(dve, vec_chain)
                step(nc.vector.tensor_tensor(y[:, :, P:S], y[:, :, P:S], y_off[:, :, :], ALU.add))
                nc.vector.tensor_tensor(y, y, z[:, :, :], ALU.mult).then_inc(gated, 1)
                dve.wait_ge(rstd_done, 1)
                for j in range(N_X):
                    nc.vector.scalar_tensor_tensor(y[:, j, :], y[:, j, :], cols["ssd_g"][:, j:j + 1],
                                                   rstd[:, j // 4, :], ALU.mult, ALU.mult)


def lru(k, cols, u, mix):
    nc, io = k.nc, k.io
    w_in = io["w_in"][0].rearrange("(k p) c -> p k c", p=P)
    with ExitStack() as mem:
        raw = k.sb("lru_raw", [P, N_L, S + TAPS - 1], ctx=mem)
        z = k.sb("z_lru", [P, N_L, S], ctx=mem)
        xc = k.sb("lru_xc", [P, N_L, S], ctx=mem)
        r = k.sb("lru_r", [P, N_L, S], ctx=mem)
        gate = k.sb("lru_i", [P, N_L, S], ctx=mem)
        a = k.sb("lru_a", [P, N_L, S], ctx=mem)
        t = k.sb("lru_t", [P, N_L, S], ctx=mem)
        w = k.sb("lru_w", [P, 2, N_L, P], ctx=mem)
        small = k.sb("small_l", [P, 5, N_L], ctx=mem)

        with k.stage("cleared", "weights_loaded") as (block, cleared, weights_loaded):
            @block.gpsimd
            def _(pool):
                nc.gpsimd.memset(raw[:, :, 0:TAPS - 1], 0.0)
                nc.gpsimd.memset(w[:, :, :, :], 0.0).then_inc(cleared, 1)

            @block.sync
            def _(sp):
                sp.wait_ge(cleared, 1)
                for n, name in enumerate(("lru_w_a", "lru_w_x")):
                    for h in range(2):
                        src = io[name][0].rearrange("(j h) d e -> h d j e", h=2)[h]
                        sp.dma_start(w[h * 64:h * 64 + 64, n, :, h * 64:h * 64 + 64], src).then_inc(weights_loaded, 16)
                sp.wait_ge(weights_loaded, 64)

        slabs = [w_in[:, :, COL_XL:COL_XL + L_W], w_in[:, :, COL_ZL:COL_ZL + L_W]]
        tiles = [(0, j * P, P, "f", copy_to(raw[:, j, TAPS - 1:])) for j in range(N_L)]
        tiles += [(1, j * P, P, "f", copy_to(z[:, j, :], func=ACT.Silu)) for j in range(N_L)]
        project(k, slabs, tiles, u, side=6)

        with k.stage("conv_done", "gates_done", "sigmoids_done", "neg_abs", "exp_done", "rate_done", "a_done",
                     "tanh_done", "square_done", "root_done", "act_chain", "vec_chain") as (
                block, conv_done, gates_done, sigmoids_done, neg_abs, exp_done, rate_done, a_done, tanh_done,
                square_done, root_done, act_chain, vec_chain):

            @block.scalar
            def _(act):
                act.wait_ge(neg_abs, 1)
                nc.scalar.activation(small[:, 1, :], small[:, 1, :], ACT.Exp).then_inc(exp_done, 1)
                act.wait_ge(gates_done, 1)
                for n, (dst, b) in enumerate(((r, "lru_b_a"), (gate, "lru_b_x"))):
                    for j in range(N_L):
                        at = (4 * n + j) * S
                        src = k.ps[:, at // 512, at % 512:at % 512 + S]
                        nc.scalar.activation(dst[:, j, :], src, ACT.Sigmoid, bias=cols[b][:, j:j + 1]
                                             ).then_inc(sigmoids_done, 1)
                act.wait_ge(rate_done, 1)
                nc.scalar.activation(t[:, :, :], r[:, :, :], ACT.Tanh).then_inc(tanh_done, 1)
                nc.scalar.activation(a[:, :, :], r[:, :, :], ACT.Exp, scale=-1.0).then_inc(a_done, 1)
                act.wait_ge(square_done, 1)
                nc.scalar.activation(t[:, :, :], t[:, :, :], ACT.Sqrt).then_inc(root_done, 1)

            @block.tensor
            def _(pe):
                pe.wait_ge(conv_done, TAPS * N_L)
                for n in range(2):
                    for j in range(N_L):
                        at = (4 * n + j) * S
                        ins = nc.tensor.matmul(k.ps[:, at // 512, at % 512:at % 512 + S], w[:, n, j, :], xc[:, j, :],
                                               start=True, stop=True)
                ins.then_inc(gates_done, 1)

            @block.vector
            def _(dve):
                step = chain(dve, vec_chain)
                sp, e, w1, w2, rate = (small[:, i, :] for i in range(5))
                step(nc.vector.tensor_scalar(rate, cols["lru_lambda"], -1.0, None, ALU.mult))
                nc.vector.scalar_tensor_tensor(e, rate, -1.0, rate, ALU.mult, ALU.min).then_inc(neg_abs, 1)
                causal_conv(nc, dve, conv_done, N_L, raw, xc, lambda i: cols["lru_w"][:, i * N_L:(i + 1) * N_L],
                            cols["lru_b"])
                dve.wait_ge(exp_done, 1)
                log1p_steps(nc, step, sp, e, w1, w2)
                step(nc.vector.scalar_tensor_tensor(rate, rate, 0.0, sp, ALU.max, ALU.add))
                step(nc.vector.tensor_scalar(rate, rate, 8.0, None, ALU.mult))
                dve.wait_ge(sigmoids_done, 2 * N_L)
                for j in range(N_L):
                    ins = nc.vector.tensor_scalar(r[:, j, :], r[:, j, :], rate[:, j:j + 1], None, ALU.mult)
                ins.then_inc(rate_done, 1)
                step(nc.vector.tensor_tensor(gate[:, :, :], gate[:, :, :], xc[:, :, :], ALU.mult))
                dve.wait_ge(a_done, 1)
                step(nc.vector.tensor_scalar(r[:, :, :], t[:, :, :], 1.0, None, ALU.add))
                step(nc.vector.reciprocal(r[:, :, :], r[:, :, :]))
                nc.vector.scalar_tensor_tensor(t[:, :, :], t[:, :, :], 2.0, r[:, :, :], ALU.mult, ALU.mult).then_inc(square_done, 1)
                dve.wait_ge(root_done, 1)
                step(nc.vector.memset(t[:, :, 0:1], 1.0))
                step(nc.vector.tensor_tensor(gate[:, :, :], gate[:, :, :], t[:, :, :], ALU.mult))
                for j in range(N_L):
                    ins = nc.vector.tensor_tensor_scan(r[:, j, :], a[:, j, :], gate[:, j, :], 0.0, ALU.mult, ALU.add)
                step(ins)
                nc.vector.tensor_tensor(mix[:, N_A + N_X:, :], r[:, :, :], z[:, :, :], ALU.mult)


def add_product(k, slabs, tiles, rhs, gain=None, side=0):
    def store(j):
        def put(eng, ps):
            if gain is None:
                return eng.tensor_tensor(k.x[:, j, :], k.x[:, j, :], ps[:, 0:S], ALU.add)
            return eng.scalar_tensor_tensor(k.x[:, j, :], ps[:, 0:S], gain[:, j:j + 1], k.x[:, j, :],
                                            ALU.mult, ALU.add)
        return put
    project(k, slabs, [(i, c, P, "f", store(j)) for i, c, j in tiles], rhs, evac_engine="vector",
            side=side)


def first_block(k):
    nc, io = k.nc, k.io
    with ExitStack() as mem:
        pieces, n = layout(first_constants())
        buf = k.sb("first_constants", [P, n], ctx=mem)
        k.first_const = lambda name, h: buf[:, pieces[name][0] + h * P:pieces[name][0] + (h + 1) * P]
        k.forget_b = k.sb("forget_b", [P, 1], ctx=mem)
        k.dt_bias = k.sb("dt_bias", [P, 1], ctx=mem)
        k.a_log = k.sb("a_log", [P, 1], ctx=mem)
        d_head = k.sb("d_head", [P, 1], ctx=mem)
        d_pairs = k.sb("d_pairs", [P, N_X], ctx=mem)
        with k.stage("cleared", "params_loaded", "spread") as (block, cleared, loaded, spread):
            @block.gpsimd
            def _(pool):
                nc.gpsimd.memset(d_head[:, :], 0.0).then_inc(cleared, 1)

            @block.tensor
            def _(pe):
                pe.wait_ge(loaded, 16 * 5)
                for j in range(N_X):
                    ins = nc.tensor.matmul(k.ps[:, 0, j:j + 1], k.first_const("pick_pair", j), d_head[:, :],
                                           start=True, stop=True)
                ins.then_inc(spread, 1)

            @block.vector
            def _(dve):
                dve.wait_ge(spread, 1)
                nc.vector.tensor_copy(d_pairs[:, :], k.ps[:, 0, 0:N_X])

            @block.sync
            def _(sp):
                sp.wait_ge(cleared, 1)
                sp.dma_start(buf[:, :], io["first_constants"]).then_inc(loaded, 16)
                for dst, src, m in ((k.forget_b, "forget_b", A_H), (k.dt_bias, "ssd_dt_bias", X_H),
                                    (k.a_log, "ssd_a_log", X_H), (d_head, "ssd_d", X_H)):
                    sp.dma_start(dst[0:m, :], io[src][0].rearrange("(h o) -> h o", o=1)).then_inc(loaded, 16)
                sp.wait_ge(loaded, 16 * 5)
        tile_rows = lambda ap: ap.rearrange("(r c) -> r c", c=P)
        row = lambda name: tile_rows(io[name][0])
        taps = lambda name: [(0, io[name][0].rearrange("i (r c) -> (i r) c", c=P))]
        head = lambda name: [(0, io[name]), (A_D, io[name])]
        cols = load_rows(k, [
            ("norm", ND, [(0, row("norm_g"))]), ("q_norm", 1, head("q_norm_g")), ("k_norm", 1, head("k_norm_g")),
            ("ssd_w", TAPS * N_C, taps("ssd_conv_w")), ("ssd_b", N_C, [(0, row("ssd_conv_b"))]),
            ("ssd_g", N_X, [(0, row("ssd_norm_g"))]), ("lru_w", TAPS * N_L, taps("lru_conv_w")),
            ("lru_b", N_L, [(0, row("lru_conv_b"))]), ("lru_b_a", N_L, [(0, row("lru_b_a"))]),
            ("lru_b_x", N_L, [(0, row("lru_b_x"))]), ("lru_lambda", N_L, [(0, row("lru_lambda"))]),
            ("c", ND, [(0, tile_rows(io["c_2"][0]))]),
        ])
        cols["ssd_d"] = d_pairs[:, :]
        k.ada_at = 0
        k.ada_ring = k.sb("ada_ring", [P, ADA_SLOTS, ND, ADA], ctx=mem)
        k.ada_sum = k.sb("ada_sum", [P, ADA_SUMS, ADA], ctx=mem)
        k.c_silu = k.sb("c_silu", [P, ND], ctx=mem)
        with k.stage("none") as (block, _):
            @block.scalar
            def _(act):
                nc.scalar.activation(k.c_silu[:, :], cols["c"], ACT.Silu)

        mix = k.sb("mix", [P, MIX // P, S], ctx=mem)
        with ExitStack() as tmp:
            u = k.sb("u", [P, ND, S], ctx=tmp)
            rms_norm(k, k.x[:, :, :], u[:, :, :], cols["norm"])
            attention(k, cols, u, mix)
            k.clear_semaphores()
            ssd(k, cols, u, mix)
            k.clear_semaphores()
            lru(k, cols, u, mix)
        w_out = io["w_out"][0].rearrange("(k p) c -> p k c", p=P)
        add_product(k, [w_out[:, :, i * 2 * P:(i + 1) * 2 * P] for i in range(4)],
                    [(j // 2, j % 2 * P, j) for j in range(ND)], mix, side=LAYERS * 6 * D // ADA - k.ada_at)
        k.clear_semaphores()



def rotation_tables(k):
    nc, io = k.nc, k.io
    parts = [6.28125]
    parts.append(float(np.float32(round((2 * math.pi - parts[0]) * 2 ** 21) / 2 ** 21)))
    parts.append(2 * math.pi - parts[0] - parts[1])
    magic = 1.5 * 2 ** 23
    with ExitStack() as mem:
        pos = k.sb("pos", [P, S], I32, ctx=mem)
        angle = k.sb("angle", [P, S], ctx=mem)
        turns = k.sb("turns", [P, S], ctx=mem)
        with k.stage("pos_loaded", "reduced", "vec_chain") as (block, pos_loaded, reduced, vec_chain):

            @block.sync
            def _(sp):
                src = io["positions_2"][0].rearrange("(o s) -> o s", o=1)
                sp.dma_start(pos[:, :], src.broadcast_to([P, S])).then_inc(pos_loaded, 16)

            @block.vector
            def _(dve):
                step = chain(dve, vec_chain)
                dve.wait_ge(pos_loaded, 16)
                step(nc.vector.tensor_copy(angle[:, :], pos[:, :]))
                step(nc.vector.tensor_scalar(angle[:, :], angle[:, :], k.const("inv_freq"), None, ALU.mult))
                for n, (dst, quarter) in enumerate(((k.sin, 0.0), (k.cos, 0.25))):
                    step(nc.vector.tensor_scalar(turns[:, :], angle[:, :], 1 / (2 * math.pi), quarter, ALU.mult, ALU.add))
                    step(nc.vector.tensor_scalar(turns[:, :], turns[:, :], magic, magic, ALU.add, ALU.subtract))
                    src = angle
                    for part in parts:
                        step(nc.vector.scalar_tensor_tensor(dst[:, :], turns[:, :], -part, src[:, :], ALU.mult, ALU.add))
                        src = dst
                    step(nc.vector.tensor_scalar(dst[:, :], dst[:, :], quarter * 2 * math.pi, 3.1415925, ALU.add, ALU.min))
                    nc.vector.tensor_scalar(dst[:, :], dst[:, :], -3.1415925, None, ALU.max).then_inc(reduced, 1)

            @block.scalar
            def _(act):
                for n, dst in enumerate((k.sin, k.cos)):
                    act.wait_ge(reduced, n + 1)
                    nc.scalar.activation(dst[:, :], dst[:, :], ACT.Sin)


def ada_modulation(k, l, cols):
    nc = k.nc
    with k.stage("mod_chain") as (block, mod_chain):

        @block.vector
        def _(dve):
            step = chain(dve, mod_chain)
            mods = k.mods[:, :].rearrange("p (l c) -> p l c", l=LAYERS)
            step(nc.vector.tensor_tensor(k.mod[:, :].rearrange("p (o c) -> p o c", o=1), mods[:, bass.ds(l, 1), :],
                                         cols["b_ada"].rearrange("p (o c) -> p o c", o=1), ALU.add))
            for n, name in enumerate(("norm1", "norm2")):
                scale = k.mod[:, (3 * n + 1) * ND:(3 * n + 2) * ND]
                nc.vector.scalar_tensor_tensor(scale, scale, 1.0, cols[name], ALU.add, ALU.mult)


def branch_projections(k, l, h, p, pr):
    nc, io = k.nc, k.io
    w = io["w_in_2"].rearrange("l (k p) c -> l p k c", p=P)
    slabs = [w[l, :, :, i * 512:min((i + 1) * 512, IN_COLS)] for i in range((IN_COLS + 511) // 512)]
    tiles = []
    for j in range(IN_COLS // P):
        i, c = j // 4, j % 4 * P
        if i == 2:
            if j % 4 < NT:
                at = 8 * S + j % 4 * MW
                dst = p[:, :, :].rearrange("p j s -> p (j s)")[:, at:at + MW]
                tiles.append((i, 0, MW, j % 4, copy_to(dst, n=MW)))
        elif j < 4 * N_M:
            tiles.append((i, c, P, "f", copy_to(p[:, j, :], func=ACT.Silu if i == 3 else ACT.Copy)))
        elif j < 4 * N_M + N_K:
            tiles.append((i, c, P, "f", copy_to(pr[:, j - 4 * N_M, 1:])))
        else:
            tiles.append((i, c, P, "f", copy_to(p[:, j - N_K, :])))
    with k.stage("cleared") as (block, cleared):
        @block.gpsimd
        def _(pool):
            nc.gpsimd.memset(pr[:, :, 0:1], 0.0)
    project(k, slabs, tiles, h)


def retention_and_conv(k, cols, p, y_ret, y_conv):
    nc = k.nc
    with ExitStack() as mem:
        rot = k.sb("rotated", [P, 8, S], ctx=mem)
        tmp = k.sb("rot_tmp", [P, 8, S], ctx=mem)
        sc = k.sb("ret_scores", [P, R_H, 3 * P], ctx=mem)
        conv_in = k.sb("conv_in", [P, N_M, S + 2], ctx=mem)
        y = tmp[:, 0:4, :].rearrange("p j s -> p (j s)")
        sq = tmp[:, 4:8, :].rearrange("p j s -> p (j s)")
        rstd = rot[:, 0:4, :].rearrange("p j s -> p (j s)")
        banks = lambda a: a.rearrange("p (b s) -> p b s", b=2)
        v = p[:, 8:12, :].rearrange("p j s -> p (j s)").rearrange("p (t c) -> p t c", t=NT)
        with k.stage("swapped", "rotated", "scores_done", "decayed", "out_done", "out_stored", "mean_done", "centred",
                     "squared", "var_done", "ln_done", "rstd_done", "cleared", "vec_chain") as (
                block, swapped, rotated, scores_done, decayed, out_done, out_stored, mean_done, centred,
                squared, var_done, ln_done, rstd_done, cleared, vec_chain):

            @block.gpsimd
            def _(pool):
                nc.gpsimd.memset(conv_in[:, :, 0:2], 0.0).then_inc(cleared, 1)

            @block.tensor
            def _(pe):
                flat = p[:, :, :].rearrange("p j s -> p (j s)")
                for b in range(4):
                    ins = nc.tensor.matmul(k.ps[:, b, :], k.const("swap"), flat[:, b * 512:(b + 1) * 512],
                                           start=True, stop=True)
                ins.then_inc(swapped, 1)
                pe.wait_ge(rotated, 1)
                for h in range(R_H):
                    nc.tensor.matmul(k.ps[:, 4 + h, 0:S], rot[:, R_H + h, 0:P], rot[:, h, :], start=True, stop=True)
                    ins = nc.tensor.matmul(k.ps[:, 4 + h, S:S + P], rot[:, R_H + h, P:S], rot[:, h, P:S],
                                           start=True, stop=True)
                ins.then_inc(scores_done, 1)
                pe.wait_ge(decayed, 1)
                for h in range(R_H):
                    c = slice(h * P, (h + 1) * P)
                    ps = k.ps[:, h // 2, h % 2 * S:h % 2 * S + S]
                    nc.tensor.matmul(ps[:, 0:P], v[:, 0, c], sc[:, h, 0:P], start=True, stop=True)
                    nc.tensor.matmul(ps[:, P:S], v[:, 0, c], sc[:, h, P:S], start=True, stop=False)
                    ins = nc.tensor.matmul(ps[:, P:S], v[:, 1, c], sc[:, h, S:S + P], start=False, stop=True)
                ins.then_inc(out_done, 1)
                pe.wait_ge(out_stored, 1)
                for b in range(2):
                    ins = nc.tensor.matmul(k.ps[:, 2 + b, :], k.const("mean_128"), y[:, b * 512:(b + 1) * 512],
                                           start=True, stop=True)
                ins.then_inc(mean_done, 1)
                pe.wait_ge(squared, 1)
                for b in range(2):
                    ins = nc.tensor.matmul(k.ps[:, 4 + b, :], k.const("mean_128"), sq[:, b * 512:(b + 1) * 512],
                                           start=True, stop=True)
                ins.then_inc(var_done, 1)

            @block.scalar
            def _(act):
                act.wait_ge(out_done, 1)
                nc.scalar.activation(banks(y), k.ps[:, 0:2, :], ACT.Copy).then_inc(out_stored, 1)
                act.wait_ge(centred, 1)
                nc.scalar.activation(sq, y, ACT.Square).then_inc(squared, 1)
                act.wait_ge(var_done, 1)
                nc.scalar.activation(banks(rstd), k.ps[:, 4:6, :], ACT.Ln, bias=k.eps[:, 1:2]).then_inc(ln_done, 1)
                act.wait_ge(ln_done, 1)
                nc.scalar.activation(rstd, rstd, ACT.Exp, scale=-0.5).then_inc(rstd_done, 1)

            @block.vector
            def _(dve):
                step = chain(dve, vec_chain)
                table = lambda t: t[:, :].rearrange("p (o s) -> p o s", o=1).broadcast_to([P, 8, S])
                nc.vector.tensor_tensor(rot[:, :, :], p[:, 0:8, :], table(k.cos), ALU.mult)
                dve.wait_ge(swapped, 1)
                step(nc.vector.tensor_tensor(tmp[:, :, :], k.ps[:, 0:4, :].rearrange("p b (j s) -> p (b j) s", s=S),
                                             table(k.sin), ALU.mult))
                nc.vector.tensor_tensor(rot[:, :, :], rot[:, :, :], tmp[:, :, :], ALU.add).then_inc(rotated, 1)
                dve.wait_ge(scores_done, 1)
                at = k.columns["decay_0"][0]
                decay = k.consts[:, at:at + R_H * S].rearrange("p (h s) -> p h s", h=R_H)
                nc.vector.tensor_tensor(sc[:, :, 0:S], k.ps[:, 4:8, 0:S], decay, ALU.mult)
                nc.vector.tensor_tensor(sc[:, :, S:S + P], k.ps[:, 4:8, S:S + P], decay[:, :, 0:P],
                                        ALU.mult).then_inc(decayed, 1)
                dve.wait_ge(cleared, 1)
                base = 4 * N_M
                step(nc.vector.tensor_tensor(conv_in[:, :, 2:], p[:, base:base + N_M, :],
                                             p[:, base + 2 * N_M:base + 3 * N_M, :], ALU.mult))
                for i in range(3):
                    for j in range(N_M):
                        w = cols["conv_w"][:, i * N_M + j:i * N_M + j + 1]
                        if i == 0:
                            ins = nc.vector.tensor_scalar(y_conv[:, j, :], conv_in[:, j, 0:S], w, None, ALU.mult)
                        else:
                            ins = nc.vector.scalar_tensor_tensor(y_conv[:, j, :], conv_in[:, j, i:i + S], w,
                                                                 y_conv[:, j, :], ALU.mult, ALU.add)
                        if j == N_M - 1:
                            step(ins)
                nc.vector.tensor_tensor(y_conv, y_conv, p[:, base + N_M:base + 2 * N_M, :], ALU.mult)
                dve.wait_ge(mean_done, 1)
                nc.vector.tensor_tensor(banks(y), banks(y), k.ps[:, 2:4, :], ALU.subtract).then_inc(centred, 1)
                dve.wait_ge(rstd_done, 1)
                step(nc.vector.tensor_tensor(y, y, rstd, ALU.mult))
                for h in range(R_H):
                    nc.vector.scalar_tensor_tensor(y_ret[:, h, :], tmp[:, h, :], cols["ret_g"][:, h:h + 1],
                                                   p[:, 12 + h, :], ALU.mult, ALU.mult)


def rwkv(k, cols, pr, y_out):
    nc = k.nc
    with ExitStack() as mem:
        g = k.sb("rwkv_gate", [P, N_M, S], ctx=mem)
        bonus = k.sb("bonus", [P, N_M, S], ctx=mem)
        ar = k.sb("alpha_rho", [P, N_M, 2, 2, S], ctx=mem)
        kap = k.sb("kappa", [P, N_M, S], ctx=mem)
        bet = k.sb("beta", [P, N_M, S], ctx=mem)
        v_pad = k.sb("rwkv_v", [P, NT, K_H, P], ctx=mem)
        ends = k.sb("chunk_ends", [P, 4, N_M], ctx=mem)
        pf = pr[:, :, 1:]
        with ExitStack() as tmp:
            work = k.sb("work", [P, N_K, S], ctx=tmp)
            a = k.sb("rwkv_a", [P, N_M, S], ctx=tmp)
            kh = k.sb("k_hat", [P, N_M, S], ctx=tmp)
            e = k.sb("decays", [P, N_M, S], ctx=tmp)
            sw, cs, dm = work[:, 0:4, :], work[:, 4:8, :], work[:, 8:12, :]
            flat = lambda t: t.rearrange("p j s -> p (j s)")
            two = lambda b: k.ps[:, b:b + 2, :].rearrange("p b (j s) -> p (b j) s", j=2)
            pair_ps = lambda b, j: k.ps[:, b + j // 2, j % 2 * S:j % 2 * S + S]
            halves = [(h, slice(h * 64, h * 64 + 64)) for h in range(2)]
            with k.stage("cleared", "shifted", "squashed", "w_done", "w_sig", "a_done", "a_sig", "g_done", "g_stored",
                         "kk_done", "kk_sq", "kk_sum", "kk_clamped", "kk_ln", "kk_rstd", "cs_done", "exps", "used",
                         "bonus_in", "bonus_sum", "v_turned", "vec_chain") as (
                    block, cleared, shifted, squashed, w_done, w_sig, a_done, a_sig, g_done, g_stored,
                    kk_done, kk_sq, kk_sum, kk_clamped, kk_ln, kk_rstd, cs_done, exps, used,
                    bonus_in, bonus_sum, v_turned, vec_chain):

                @block.gpsimd
                def _(pool):
                    nc.gpsimd.memset(ar[:, :, :, :, :], 0.0).then_inc(cleared, 1)
                    nc.gpsimd.memset(v_pad[:, :, :, :], 0.0).then_inc(cleared, 1)

                @block.tensor
                def _(pe):
                    pe.wait_ge(squashed, 1)
                    for j in range(N_M):
                        ins = nc.tensor.matmul(pair_ps(0, j), k.w_lora[:, j * P:(j + 1) * P], pf[:, 12, :],
                                               start=True, stop=True)
                    ins.then_inc(w_done, 1)
                    for j in range(N_M):
                        ins = nc.tensor.matmul(pair_ps(2, j), k.a_lora[:, j * P:(j + 1) * P], pf[:, 12, :],
                                               start=True, stop=True)
                    ins.then_inc(a_done, 1)
                    pe.wait_ge(squashed, 2)
                    for j in range(N_M):
                        ins = nc.tensor.matmul(pair_ps(4, j), k.g_lora[:, j * P:(j + 1) * P], pf[:, 13, :],
                                               start=True, stop=True)
                    ins.then_inc(g_done, 1)
                    pe.wait_ge(kk_sq, 1)
                    for b in range(2):
                        ins = nc.tensor.matmul(k.ps[:, 6 + b, :], k.const("sum_64"), flat(e[:, :, :])[:, b * 512:(b + 1) * 512],
                                               start=True, stop=True)
                    ins.then_inc(kk_sum, 1)
                    pe.wait_ge(w_sig, 1)
                    pe.wait_ge(a_sig, 1)
                    for t in range(NT):
                        for j in range(N_M):
                            ins = nc.tensor.transpose(k.ps[:, t, j * P:(j + 1) * P], pf[:, 8 + j, t * P:(t + 1) * P],
                                                      k.const("ident"))
                    ins.then_inc(v_turned, 1)
                    pe.wait_ge(bonus_in, 1)
                    for b in range(2):
                        ins = nc.tensor.matmul(k.ps[:, 2 + b, :], k.const("sum_64"), flat(bonus[:, :, :])[:, b * 512:(b + 1) * 512],
                                               start=True, stop=True)
                    ins.then_inc(bonus_sum, 1)

                @block.scalar
                def _(act):
                    act.wait_ge(shifted, 1)
                    nc.scalar.activation(pf[0:64, 12, :], pf[0:64, 12, :], ACT.Tanh).then_inc(squashed, 1)
                    nc.scalar.activation(pf[:, 13, :], pf[:, 13, :], ACT.Sigmoid).then_inc(squashed, 1)
                    act.wait_ge(w_done, 1)
                    for j in range(N_M):
                        ins = nc.scalar.activation(sw[:, j, :], pair_ps(0, j), ACT.Sigmoid, bias=cols["w0"][:, j:j + 1])
                    ins.then_inc(w_sig, 1)
                    act.wait_ge(a_done, 1)
                    for j in range(N_M):
                        ins = nc.scalar.activation(a[:, j, :], pair_ps(2, j), ACT.Sigmoid, bias=cols["a0"][:, j:j + 1])
                    ins.then_inc(a_sig, 1)
                    act.wait_ge(g_done, 1)
                    nc.scalar.activation(g[:, :, :], two(4), ACT.Copy).then_inc(g_stored, 1)
                    act.wait_ge(kk_done, 1)
                    nc.scalar.activation(e[:, :, :], kh[:, :, :], ACT.Square).then_inc(kk_sq, 1)
                    act.wait_ge(kk_clamped, 1)
                    nc.scalar.activation(e[:, :, :], e[:, :, :], ACT.Ln).then_inc(kk_ln, 1)
                    act.wait_ge(kk_ln, 1)
                    nc.scalar.activation(e[:, :, :], e[:, :, :], ACT.Exp, scale=-0.5).then_inc(kk_rstd, 1)
                    act.wait_ge(used, 1)
                    nc.scalar.activation(e[:, :, :], dm, ACT.Exp, scale=LW_SCALE).then_inc(exps, 1)
                    act.wait_ge(used, 2)
                    nc.scalar.activation(e[:, :, :], dm, ACT.Exp, scale=-LW_SCALE).then_inc(exps, 1)
                    act.wait_ge(used, 3)
                    nc.scalar.activation(e[:, :, :], dm, ACT.Exp, scale=LW_SCALE).then_inc(exps, 1)
                    nc.scalar.activation(ends[:, :, :], ends[:, :, :], ACT.Exp, scale=LW_SCALE)

                @block.vector
                def _(dve):
                    step = chain(dve, vec_chain)
                    step(nc.vector.tensor_tensor(work[:, :, :], pr[:, :, 0:S], pf, ALU.subtract))
                    for j in range(N_K):
                        ins = nc.vector.scalar_tensor_tensor(pf[:, j, :], work[:, j, :], cols["mu"][:, j:j + 1],
                                                             pf[:, j, :], ALU.mult, ALU.add)
                    ins.then_inc(shifted, 1)
                    dve.wait_ge(shifted, 1)
                    for j in range(N_M):
                        ins = nc.vector.tensor_scalar(kh[:, j, :], pf[:, 4 + j, :], cols["k_k"][:, j:j + 1], None, ALU.mult)
                    ins.then_inc(kk_done, 1)
                    dve.wait_ge(w_sig, 1)
                    for j in range(N_M):
                        for c in range(NT):
                            r = slice(c * P, (c + 1) * P)
                            ins = nc.vector.tensor_tensor_scan(cs[:, j, r], k.ones[:, 0:P], sw[:, j, r], 0.0,
                                                               ALU.mult, ALU.add)
                    step(ins)
                    for c in range(NT):
                        r = slice(c * P, (c + 1) * P)
                        mid = cs[:, :, c * P + 63:c * P + 64]
                        nc.vector.tensor_tensor(dm[:, :, r], cs[:, :, r], mid.broadcast_to([P, N_M, P]), ALU.subtract)
                        nc.vector.tensor_tensor(ends[:, c, :], cs[:, :, c * P + P - 1], cs[:, :, c * P + 63], ALU.subtract)
                        ins = nc.vector.tensor_copy(ends[:, 2 + c, :], cs[:, :, c * P + 63])
                    step(ins)
                    dve.wait_ge(a_sig, 1)
                    for j in range(N_M):
                        ins = nc.vector.tensor_scalar(cs[:, j, :], a[:, j, :], -1.0, cols["k_a"][:, j:j + 1], ALU.add, ALU.mult)
                    step(ins)
                    dve.wait_ge(kk_done, 1)
                    kt = pf[:, 4:8, :]
                    step(nc.vector.scalar_tensor_tensor(kt, cs, 1.0, kt, ALU.add, ALU.mult))
                    for j in range(N_M):
                        ins = nc.vector.scalar_tensor_tensor(bonus[:, j, :], pf[:, j, :], cols["r_k"][:, j:j + 1],
                                                             kt[:, j, :], ALU.mult, ALU.mult)
                    ins.then_inc(bonus_in, 1)
                    dve.wait_ge(kk_sum, 1)
                    nc.vector.tensor_scalar(e[:, :, :], two(6), 1e-12, None, ALU.max).then_inc(kk_clamped, 1)
                    dve.wait_ge(cleared, 2)
                    dve.wait_ge(kk_rstd, 1)
                    step(nc.vector.tensor_tensor(kh[:, :, :], kh[:, :, :], e[:, :, :], ALU.mult))
                    nc.vector.tensor_tensor(a[:, :, :], a[:, :, :], kh[:, :, :], ALU.mult).then_inc(used, 1)
                    dve.wait_ge(exps, 1)
                    for h, r in halves:
                        ins = nc.vector.tensor_tensor(ar[r, :, h, 1, :], pf[r, 0:4, :], e[r, :, :], ALU.mult)
                    ins.then_inc(used, 1)
                    dve.wait_ge(exps, 2)
                    nc.vector.tensor_tensor(kap[:, :, :], kt, e[:, :, :], ALU.mult)
                    nc.vector.tensor_tensor(bet[:, :, :], a[:, :, :], e[:, :, :], ALU.mult)
                    nc.vector.tensor_tensor(dm, dm, sw, ALU.subtract).then_inc(used, 1)
                    dve.wait_ge(exps, 3)
                    for h, r in halves:
                        nc.vector.tensor_tensor(ar[r, :, h, 0, :], kh[r, :, :], e[r, :, :], ALU.mult)
                    dve.wait_ge(v_turned, 1)
                    for t in range(NT):
                        dst = v_pad[:, t, :, :].rearrange("p (j h) c -> p j h c", h=2)
                        src = k.ps[:, t, :].rearrange("p (j h c) -> p j h c", h=2, c=64)
                        for h in range(2):
                            nc.vector.tensor_copy(dst[:, :, h, h * 64:h * 64 + 64], src[:, :, h, :])
                    dve.wait_ge(bonus_sum, 1)
                    nc.vector.tensor_tensor(bonus[:, :, :], two(2), pf[:, 8:12, :], ALU.mult)

        gram = k.sb("gram", [P, K_H, 4, P], ctx=mem)
        m = k.sb("m_target", [P, K_H, P], ctx=mem)
        inv = k.sb("inverse", [P, K_H, P], ctx=mem)
        inv_t = k.sb("inverse_t", [P, K_H, P], ctx=mem)
        z = k.sb("z_inv", [P, K_H, P], ctx=mem)
        block_m = k.sb("level_block", [P, K_H, P], ctx=mem)
        x = k.sb("x_rhs", [P, K_H, 64], ctx=mem)
        u_pad = k.sb("u_neg", [P, K_H, P], ctx=mem)
        s0 = k.sb("state", [P, N_M, P], ctx=mem)
        kb_tok = k.sb("kb_tok", [P, 2, N_M, P], ctx=mem)
        own = lambda t, c, h: t[:, c, h, h % 2 * 64:h % 2 * 64 + 64]
        for c in range(NT):
            cr = slice(c * P, (c + 1) * P)
            with k.stage("cleared", "gram_done", "gram_masked", "m_done", "z_done", "z_stored", "upd_done",
                         "inverse_ready", "block_ready", "x_done", "x_stored", "u_done", "u_stored", "y_done",
                         "kb_turned", "kb_stored", "s_done", "vec_chain") as (
                    block, cleared, gram_done, gram_masked, m_done, z_done, z_stored, upd_done,
                    inverse_ready, block_ready, x_done, x_stored, u_done, u_stored, y_done,
                    kb_turned, kb_stored, s_done, vec_chain):
                levels = [2 ** i for i in range(1, 7)]

                @block.gpsimd
                def _(pool):
                    if c == 0:
                        step = chain(pool, cleared)
                        step(nc.gpsimd.memset(u_pad[:, :, :], 0.0))
                        step(nc.gpsimd.memset(s0[:, :, :], 0.0))
                        step(nc.gpsimd.memset(gram[64:P, :, :, 0:64], 0.0))
                        step(nc.gpsimd.memset(m[0:64, :, 64:P], 0.0))

                @block.tensor
                def _(pe):
                    for h in range(K_H):
                        j = h // 2
                        if h >= 4:
                            pe.wait_ge(gram_masked, h - 3)
                        for n, src in enumerate((bet, kap)):
                            out = k.ps[:, h % 4, 256 * n:256 * n + 256].rearrange("p (q t) -> p q t", q=2)
                            nc.tensor.matmul(out[:, :, 64:P], src[:, j, cr], ar[:, j, h % 2, :, c * P + 64:(c + 1) * P],
                                             start=True, stop=True)
                            ins = nc.tensor.matmul(out[0:64, :, 0:64], src[:, j, c * P:c * P + 64],
                                                   ar[:, j, h % 2, :, c * P:c * P + 64], start=True, stop=True)
                        ins.then_inc(gram_done, 1)
                    for h in range(K_H):
                        j = h // 2
                        al = ar[:, j, h % 2, 0, :]
                        out = k.ps[:, 4 + h // 4, h % 4 * P:(h % 4 + 1) * P]
                        nc.tensor.matmul(out[:, 0:64], al[:, cr], bet[:, j, c * P:c * P + 64], start=True, stop=True)
                        ins = nc.tensor.matmul(out[64:P, 64:P], al[:, c * P + 64:(c + 1) * P],
                                               bet[:, j, c * P + 64:(c + 1) * P], start=True, stop=True)
                    ins.then_inc(m_done, 1)
                    if c == 0:
                        pe.wait_ge(gram_masked, K_H)
                        for n, src in enumerate((kap, bet)):
                            for j in range(N_M):
                                ins = nc.tensor.transpose(k.ps[:, n, j * P:(j + 1) * P], src[:, j, cr], k.const("ident"))
                        ins.then_inc(kb_turned, 1)
                        pe.wait_ge(kb_stored, 1)
                    pe.wait_ge(gram_masked, K_H)
                    for n, lv in enumerate(levels):
                        for g in range(2):
                            pe.wait_ge(block_ready, 2 * n + g + 1)
                            pe.wait_ge(inverse_ready, 2 * n + g + 1)
                            for h in range(4 * g, 4 * g + 4):
                                ins = nc.tensor.matmul(k.ps[:, g, h % 4 * P:(h % 4 + 1) * P], block_m[:, h, :],
                                                       inv_t[:, h, :], start=True, stop=True)
                            ins.then_inc(z_done, 1)
                        for g in range(2):
                            pe.wait_ge(z_stored, 2 * n + g + 1)
                            for h in range(4 * g, 4 * g + 4):
                                ins = nc.tensor.matmul(k.ps[:, 2 + g, h % 4 * P:(h % 4 + 1) * P], inv[:, h, :],
                                                       z[:, h, :], start=True, stop=True)
                            if n < len(levels) - 1:
                                for h in range(4 * g, 4 * g + 4):
                                    ins = nc.tensor.matmul(k.ps[:, 6 + g, h % 4 * P:(h % 4 + 1) * P], z[:, h, :],
                                                           inv[:, h, :], start=True, stop=True)
                            ins.then_inc(upd_done, 1)
                    for h in range(K_H):
                        out = k.ps[:, 0, h * 64:h * 64 + 64]
                        if c:
                            nc.tensor.matmul(out, ar[:, h // 2, h % 2, 0, cr], s0[:, h // 2, h % 2 * 64:h % 2 * 64 + 64],
                                             start=True, stop=False)
                        ins = nc.tensor.matmul(out, gram[:, h, 2, :], own(v_pad, c, h), start=c == 0, stop=True)
                    ins.then_inc(x_done, 1)
                    pe.wait_ge(x_stored, 1)
                    pe.wait_ge(inverse_ready, 2 * len(levels) + 2)
                    for h in range(K_H):
                        ins = nc.tensor.matmul(k.ps[:, 1, h * 64:h * 64 + 64], inv_t[:, h, :], x[:, h, :],
                                               start=True, stop=True)
                    ins.then_inc(u_done, 1)
                    pe.wait_ge(u_stored, 1)
                    for j in range(N_M):
                        out = k.ps[:, 2, j * P:(j + 1) * P]
                        for i in range(2):
                            h = 2 * j + i
                            nc.tensor.matmul(out, v_pad[:, c, h, :], gram[:, h, 3, :], start=i == 0, stop=False)
                            ins = nc.tensor.matmul(out, u_pad[:, h, :], gram[:, h, 1, :], start=False,
                                                   stop=c == 0 and i == 1)
                        if c:
                            for i in range(2):
                                ins = nc.tensor.matmul(out, s0[:, j, :], ar[:, j, i, 1, cr], start=False, stop=i == 1)
                    ins.then_inc(y_done, 1)
                    if c == 0:
                        for j in range(N_M):
                            for i in range(2):
                                h = 2 * j + i
                                out = k.ps[:, 3, j * P + i * 64:j * P + i * 64 + 64]
                                nc.tensor.matmul(out, kb_tok[:, 0, j, :], own(v_pad, 0, h), start=True, stop=False)
                                ins = nc.tensor.matmul(out, kb_tok[:, 1, j, :], u_pad[:, h, i * 64:i * 64 + 64],
                                                       start=False, stop=True)
                        ins.then_inc(s_done, 1)

                @block.scalar
                def _(act):
                    if c == 0:
                        act.wait_ge(kb_turned, 1)
                        nc.scalar.activation(kb_tok[:, :, :, :].rearrange("p n j c -> p n (j c)"), k.ps[:, 0:2, :],
                                             ACT.Copy).then_inc(kb_stored, 1)
                    for n in range(len(levels)):
                        for g in range(2):
                            act.wait_ge(z_done, 2 * n + g + 1)
                            nc.scalar.activation(z[:, 4 * g:4 * g + 4, :].rearrange("p i c -> p (i c)"), k.ps[:, g, :],
                                                 ACT.Copy).then_inc(z_stored, 1)
                    act.wait_ge(x_done, 1)
                    nc.scalar.activation(x[:, :, :].rearrange("p h c -> p (h c)"), k.ps[:, 0, :], ACT.Copy
                                         ).then_inc(x_stored, 1)
                    act.wait_ge(y_done, 1)
                    nc.scalar.activation(y_out[:, :, cr], k.ps[:, 2, :].rearrange("p (j c) -> p j c", c=P), ACT.Copy)

                @block.vector
                def _(dve):
                    step = chain(dve, vec_chain)
                    at = k.columns["strict"][0]
                    both = k.consts[:, at:at + 2 * P].rearrange("p (q c) -> p q c", q=2)
                    for h in range(K_H):
                        dve.wait_ge(gram_done, h + 1)
                        for n in range(2):
                            src = k.ps[:, h % 4, 256 * n:256 * n + 256].rearrange("p (q t) -> p q t", q=2)
                            dst = gram[:, h, 2 * n:2 * n + 2, :]
                            nc.vector.tensor_tensor(dst[:, :, 64:P], src[:, :, 64:P], both[:, :, 64:P], ALU.mult)
                            ins = nc.vector.tensor_tensor(dst[0:64, :, 0:64], src[0:64, :, 0:64], both[0:64, :, 0:64], ALU.mult)
                        ins.then_inc(gram_masked, 1)
                    dve.wait_ge(m_done, 1)
                    if c == 0:
                        dve.wait_ge(cleared, 4)
                    src = k.ps[:, 4:6, :].rearrange("p b (i c) -> p (b i) c", c=P)
                    nc.vector.tensor_copy(m[:, :, 0:64], src[:, :, 0:64])
                    step(nc.vector.tensor_copy(m[64:P, :, 64:P], src[64:P, :, 64:P]))
                    every = lambda name, n=K_H: k.const(name).rearrange("p (o c) -> p o c", o=1).broadcast_to([P, n, P])
                    step(nc.vector.tensor_tensor(inv[:, :, :], m[:, :, :], every("level_1"), ALU.mult))
                    nc.vector.tensor_tensor(inv[:, :, :], every("ident"), inv[:, :, :], ALU.subtract)
                    dve.wait_ge(gram_masked, K_H)
                    step(nc.vector.tensor_tensor(inv_t[:, :, :], gram[:, :, 0, :], every("level_1t"), ALU.mult))
                    nc.vector.tensor_tensor(inv_t[:, :, :], every("ident"), inv_t[:, :, :], ALU.subtract).then_inc(inverse_ready, 2)
                    for n, lv in enumerate(levels):
                        for g in range(2):
                            hs = slice(4 * g, 4 * g + 4)
                            if n:
                                dve.wait_ge(z_done, 2 * (n - 1) + g + 1)
                            nc.vector.tensor_tensor(block_m[:, hs, :], m[:, hs, :], every(f"level_{lv}", 4), ALU.mult
                                                    ).then_inc(block_ready, 1)
                        for g in range(2):
                            hs = slice(4 * g, 4 * g + 4)
                            dve.wait_ge(upd_done, 2 * n + g + 1)
                            dve.wait_ge(inverse_ready, 2 * n + g + 1)
                            if n < len(levels) - 1:
                                nc.vector.tensor_tensor(inv[:, hs, :], inv[:, hs, :],
                                                        k.ps[:, 6 + g, :].rearrange("p (i c) -> p i c", c=P), ALU.subtract)
                            nc.vector.tensor_tensor(inv_t[:, hs, :], inv_t[:, hs, :],
                                                    k.ps[:, 2 + g, :].rearrange("p (i c) -> p i c", c=P), ALU.subtract
                                                    ).then_inc(inverse_ready, 1)
                    dve.wait_ge(u_done, 1)
                    dst = u_pad[:, :, :].rearrange("p (j h) c -> p j h c", h=2)
                    src = k.ps[:, 1, :].rearrange("p (j h c) -> p j h c", h=2, c=64)
                    for h in range(2):
                        ins = nc.vector.tensor_scalar(dst[:, :, h, h * 64:h * 64 + 64], src[:, :, h, :], -1.0, None, ALU.mult)
                    ins.then_inc(u_stored, 1)
                    if c == 0:
                        dve.wait_ge(s_done, 1)
                        for h in range(2):
                            r = slice(h * 64, h * 64 + 64)
                            for j in range(N_M):
                                nc.vector.tensor_scalar(s0[r, j, r], k.ps[r, 3, j * P + h * 64:j * P + h * 64 + 64],
                                                        ends[r, 0, j:j + 1], ends[r, 3, j:j + 1], ALU.mult, ALU.mult)

        with k.stage("mean_done", "centred", "squared", "var_done", "ln_done", "rstd_done", "vec_chain") as (
                block, mean_done, centred, squared, var_done, ln_done, rstd_done, vec_chain):
            y2 = y_out.rearrange("p j s -> p (j s)")
            sq = gram[:, 0:2, :, :].rearrange("p a b c -> p (a b c)")
            rstd = gram[:, 2:4, :, :].rearrange("p a b c -> p (a b c)")
            banks = lambda t: t.rearrange("p (b s) -> p b s", b=2)

            @block.tensor
            def _(pe):
                for b in range(2):
                    ins = nc.tensor.matmul(k.ps[:, b, :], k.const("mean_64"), y2[:, b * 512:(b + 1) * 512], start=True, stop=True)
                ins.then_inc(mean_done, 1)
                pe.wait_ge(squared, 1)
                for b in range(2):
                    ins = nc.tensor.matmul(k.ps[:, 2 + b, :], k.const("mean_64"), sq[:, b * 512:(b + 1) * 512], start=True, stop=True)
                ins.then_inc(var_done, 1)

            @block.scalar
            def _(act):
                act.wait_ge(centred, 1)
                nc.scalar.activation(sq, y2, ACT.Square).then_inc(squared, 1)
                act.wait_ge(var_done, 1)
                nc.scalar.activation(banks(rstd), k.ps[:, 2:4, :], ACT.Ln, bias=k.eps[:, 2:3]).then_inc(ln_done, 1)
                act.wait_ge(ln_done, 1)
                nc.scalar.activation(rstd, rstd, ACT.Exp, scale=-0.5).then_inc(rstd_done, 1)

            @block.vector
            def _(dve):
                step = chain(dve, vec_chain)
                dve.wait_ge(mean_done, 1)
                nc.vector.tensor_tensor(banks(y2), banks(y2), k.ps[:, 0:2, :], ALU.subtract).then_inc(centred, 1)
                dve.wait_ge(rstd_done, 1)
                rs = rstd.rearrange("p (j s) -> p j s", j=N_M)
                for j in range(N_M):
                    ins = nc.vector.scalar_tensor_tensor(y_out[:, j, :], y_out[:, j, :], cols["rwkv_g"][:, j:j + 1],
                                                         rs[:, j, :], ALU.mult, ALU.mult)
                step(ins)
                step(nc.vector.tensor_tensor(y_out, y_out, bonus[:, :, :], ALU.add))
                nc.vector.tensor_tensor(y_out, y_out, g[:, :, :], ALU.mult)


def merge(k, l, cols, h, y, merged):
    nc, io = k.nc, k.io
    w_gate = io["w_gate_2"].rearrange("l (k p) c -> l p k c", p=P)
    w_branch = io["w_branch_2"].rearrange("l n (k p) c -> l n p k c", p=P)
    slabs = []
    for n in range(3):
        slabs += [w_gate[l, :, :, n * D + i * 512:n * D + (i + 1) * 512] for i in range(2)]
        slabs += [w_branch[l, n]]
    with ExitStack() as mem:
        gates = k.sb("gates", [P, ND, S], ctx=mem)
        with k.stage(*LOADED, "gate_done", "gate_stored", "product_done", "product_used", "vec_chain") as (block, *sems):
            loaded, (gate_done, gate_stored, product_done, product_used, vec_chain) = sems[:SLOTS], sems[SLOTS:]

            @block.sync
            def _(sp):
                for i, src in enumerate(slabs):
                    n, s = i // 3, i % 3
                    if n and s < 2:
                        sp.wait_ge(gate_done, (n - 1) * ND + 4 * (s + 1))
                    elif n:
                        sp.wait_ge(product_done, n * ND)
                    kk = src.shape[1]
                    sp.dma_start(slab_view(k, s, kk * P, SLAB // kk), src).then_inc(loaded[s], 16)

            @block.tensor
            def _(pe):
                for n in range(3):
                    for j in range(ND):
                        t = n * ND + j
                        if j % 4 == 0:
                            wait_slab(pe, loaded, 3 * n + j // 4)
                        if t >= 4:
                            pe.wait_ge(gate_stored, t - 3)
                        slab = slab_view(k, j // 4, D, 512)
                        for i in range(ND):
                            ins = nc.tensor.matmul(k.ps[:, t % 4, 0:S], slab[:, i, j % 4 * P:(j % 4 + 1) * P], h[:, i, :],
                                                   start=i == 0, stop=i == ND - 1)
                        ins.then_inc(gate_done, 1)
                    wait_slab(pe, loaded, 3 * n + 2)
                    slab = slab_view(k, 2, MW, D)
                    for j in range(ND):
                        t = n * ND + j
                        if t >= 4:
                            pe.wait_ge(product_used, t - 3)
                        for i in range(N_M):
                            ins = nc.tensor.matmul(k.ps[:, 4 + t % 4, 0:S], slab[:, i, j * P:(j + 1) * P],
                                                   y[:, n, i, :], start=i == 0, stop=i == N_M - 1)
                        ins.then_inc(product_done, 1)

            @block.scalar
            def _(act):
                for n in range(3):
                    for j in range(ND):
                        t = n * ND + j
                        act.wait_ge(gate_done, t + 1)
                        if n:
                            act.wait_ge(product_used, t - ND + 1)
                        nc.scalar.activation(gates[:, j, :], k.ps[:, t % 4, 0:S], ACT.Sigmoid,
                                             bias=cols["b_gate"][:, t:t + 1]).then_inc(gate_stored, 1)

            @block.vector
            def _(dve):
                step = chain(dve, vec_chain)
                for n in range(3):
                    for j in range(ND):
                        t = n * ND + j
                        dve.wait_ge(gate_stored, t + 1)
                        dve.wait_ge(product_done, t + 1)
                        ps = k.ps[:, 4 + t % 4, 0:S]
                        if n == 0:
                            ins = nc.vector.tensor_tensor(merged[:, j, :], ps, gates[:, j, :], ALU.mult)
                            ins.then_inc(product_used, 1)
                        else:
                            nc.vector.tensor_tensor(gates[:, j, :], ps, gates[:, j, :], ALU.mult).then_inc(vec_chain, 1)
                            dve.wait_ge(vec_chain, t - ND + 1)
                            dve.wait_ge(product_used, t - ND + 1)
                            nc.vector.tensor_tensor(merged[:, j, :], merged[:, j, :], gates[:, j, :], ALU.add
                                                    ).then_inc(product_used, 1)


def router(k, h2, w_router, b_router, pick, scatter, rest_t, overflow, h2_tok):
    nc = k.nc
    n_all = N_G + N_E
    with ExitStack() as mem:
        lg = k.sb("logits", [P, NT, n_all], ctx=mem)
        hit = k.sb("hit", [P, NT, N_E], ctx=mem)
        group = k.sb("group", [P, NT, N_G], ctx=mem)
        prob = k.sb("prob", [P, NT, 1], ctx=mem)
        grp_exp = k.sb("grp_exp", [P, NT, N_G], ctx=mem)
        chosen = [k.sb(f"chosen{i}", [P, NT, N_E], ctx=mem) for i in range(2)]
        top = [k.sb(f"top{i}", [P, NT, 1], ctx=mem) for i in range(3)]
        index = k.sb("index", [P, NT, 1], ctx=mem)
        mask = k.sb("mask", [P, NT, N_E], ctx=mem)
        rank = k.sb("rank", [P, NT, N_E], ctx=mem)
        weight = k.sb("weight", [P, NT, N_E], ctx=mem)
        rest = k.sb("rest", [P, NT, P], ctx=mem)
        pick_w = k.sb("pick_w", [P, NT, N_E, CAP], ctx=mem)
        with k.stage("cleared", "logits_done", "grp_in", "grp_out", "exp_in", "exp_out", "mask_done", "ranks_done",
                     "h2_turned", "h2_copied", "weights_done", "rest_turned", "turned", "copied", "vec_chain") as (
                block, cleared, logits_done, grp_in, grp_out, exp_in, exp_out, mask_done, ranks_done,
                h2_turned, h2_copied, weights_done, rest_turned, turned, copied, vec_chain):

            @block.gpsimd
            def _(pool):
                nc.gpsimd.memset(rest[:, :, :], 0.0).then_inc(cleared, 1)
                nc.gpsimd.memset(scatter[:, 0, :], 0.0)
                nc.gpsimd.memset(pick[:, :, N_E:, :], 0.0)

            @block.tensor
            def _(pe):
                for t in range(NT):
                    for j in range(ND):
                        ins = nc.tensor.matmul(k.ps[:, t, 0:n_all], h2[:, j, t * P:(t + 1) * P], w_router[:, j, :],
                                               start=j == 0, stop=j == ND - 1)
                ins.then_inc(logits_done, 1)
                for t in range(NT):
                    for j in range(ND):
                        ins = nc.tensor.transpose(k.ps[:, 4 + 2 * t + j // 4, j % 4 * P:(j % 4 + 1) * P],
                                                  h2[:, j, t * P:(t + 1) * P], k.const("ident"))
                ins.then_inc(h2_turned, 1)
                pe.wait_ge(mask_done, 1)
                ones = k.ones[:, 0:P]
                for n, pairs in enumerate((((k.const("strict"), 0),), ((k.const("strict"), 1), (ones, 0)),
                                           ((ones, 0), (ones, 1)))):
                    for i, (lhs, t) in enumerate(pairs):
                        ins = nc.tensor.matmul(k.ps[:, 2, n * N_E:(n + 1) * N_E], lhs, mask[:, t, :],
                                               start=i == 0, stop=i == len(pairs) - 1)
                ins.then_inc(ranks_done, 1)
                pe.wait_ge(weights_done, 1)
                for t in range(NT):
                    ins = nc.tensor.transpose(k.ps[:, 3, t * P:(t + 1) * P], rest[:, t, :], k.const("ident"))
                ins.then_inc(rest_turned, 1)
                pe.wait_ge(h2_copied, 1)
                for r in range(4):
                    if r >= 2:
                        pe.wait_ge(copied, r - 1)
                    for i in range(4):
                        for t in range(NT):
                            c = 256 * (i % 2) + t * P
                            e = 2 * (4 * r + i)
                            src = pick_w[:, t, e:e + 2, :].rearrange("p e c -> p (e c)")
                            ins = nc.tensor.transpose(k.ps[:, 4 + 2 * (r % 2) + i // 2, c:c + P], src, k.const("ident"))
                    ins.then_inc(turned, 1)

            @block.scalar
            def _(act):
                act.wait_ge(h2_turned, 1)
                nc.scalar.activation(h2_tok[:, :, :].rearrange("p t (b c) -> p (t b) c", b=2), k.ps[:, 4:8, :],
                                     ACT.Copy).then_inc(h2_copied, 1)
                act.wait_ge(grp_in, 1)
                nc.scalar.activation(grp_exp[:, :, :], grp_exp[:, :, :], ACT.Exp).then_inc(grp_out, 1)
                act.wait_ge(exp_in, 1)
                nc.scalar.activation(top[2][:, :, :], top[2][:, :, :], ACT.Exp).then_inc(exp_out, 1)
                for r in range(4):
                    act.wait_ge(turned, r + 1)
                    b = 4 + 2 * (r % 2)
                    nc.scalar.activation(scatter[:, 1 + 4 * r:5 + 4 * r, :],
                                         k.ps[:, b:b + 2, :].rearrange("p b (i s) -> p (b i) s", i=2), ACT.Copy
                                         ).then_inc(copied, 1)

            @block.vector
            def _(dve):
                step = chain(dve, vec_chain)
                wide = lambda a, n: a[:, :, :].broadcast_to([P, NT, n])
                iota = k.const("iota").rearrange("p (o c) -> p o c", o=1)

                def first_max(out, src, best, n):
                    ids = iota[:, :, 0:n].broadcast_to([P, NT, n])
                    step(nc.vector.tensor_reduce(best, src, AX.X, ALU.max))
                    step(nc.vector.tensor_tensor(out, src, wide(best, n), ALU.not_equal))
                    step(nc.vector.scalar_tensor_tensor(out, out, 64.0, ids, ALU.mult, ALU.add))
                    step(nc.vector.tensor_reduce(index[:, :, :], out, AX.X, ALU.min))
                    step(nc.vector.tensor_tensor(out, ids, wide(index[:, :, :], n), ALU.is_equal))

                dve.wait_ge(logits_done, 1)
                step(nc.vector.tensor_tensor(lg[:, :, :], k.ps[:, 0:NT, 0:n_all],
                                             b_router[:, :].rearrange("p (o c) -> p o c", o=1).broadcast_to([P, NT, n_all]),
                                             ALU.add))
                groups, experts = lg[:, :, 0:N_G], lg[:, :, N_G:]
                first_max(group[:, :, :], groups, top[0][:, :, :], N_G)
                nc.vector.tensor_tensor(grp_exp[:, :, :], groups, wide(top[0][:, :, :], N_G), ALU.subtract).then_inc(grp_in, 1)
                step(nc.vector.tensor_scalar(group[:, :, :], group[:, :, :], 1.0, BIG, ALU.subtract, ALU.mult))
                for t in range(NT):
                    e3 = experts[:, t, :].rearrange("p (g e) -> p g e", g=N_G)
                    g3 = group[:, t, :].rearrange("p (g o) -> p g o", o=1).broadcast_to([P, N_G, E_G])
                    ins = nc.vector.tensor_tensor(e3, e3, g3, ALU.add)
                step(ins)
                dve.wait_ge(grp_out, 1)
                step(nc.vector.tensor_reduce(prob[:, :, :], grp_exp[:, :, :], AX.X, ALU.add))
                step(nc.vector.reciprocal(prob[:, :, :], prob[:, :, :]))
                first_max(chosen[0][:, :, :], experts, top[0][:, :, :], N_E)
                step(nc.vector.scalar_tensor_tensor(hit[:, :, :], chosen[0][:, :, :], -4 * BIG, experts, ALU.mult, ALU.add))
                first_max(chosen[1][:, :, :], hit[:, :, :], top[1][:, :, :], N_E)
                nc.vector.tensor_tensor(mask[:, :, :], chosen[0][:, :, :], chosen[1][:, :, :], ALU.add).then_inc(mask_done, 1)
                nc.vector.tensor_tensor(top[2][:, :, :], top[1][:, :, :], top[0][:, :, :], ALU.subtract).then_inc(exp_in, 1)
                dve.wait_ge(exp_out, 1)
                step(nc.vector.tensor_scalar(top[0][:, :, :], top[2][:, :, :], 1.0, None, ALU.add))
                step(nc.vector.reciprocal(top[0][:, :, :], top[0][:, :, :]))
                step(nc.vector.tensor_tensor(top[0][:, :, :], top[0][:, :, :], prob[:, :, :], ALU.mult))
                step(nc.vector.tensor_tensor(top[1][:, :, :], top[0][:, :, :], top[2][:, :, :], ALU.mult))
                for i in range(2):
                    step(nc.vector.tensor_tensor(chosen[i][:, :, :], chosen[i][:, :, :], wide(top[i][:, :, :], N_E), ALU.mult))
                step(nc.vector.tensor_tensor(weight[:, :, :], chosen[0][:, :, :], chosen[1][:, :, :], ALU.add))
                dve.wait_ge(ranks_done, 1)
                ranks = k.ps[:, 2, 0:NT * N_E].rearrange("p (t e) -> p t e", t=NT)
                step(nc.vector.scalar_tensor_tensor(rank[:, :, :], ranks, 1.0, mask[:, :, :], ALU.add, ALU.mult))
                step(nc.vector.tensor_scalar(rank[:, :, :], rank[:, :, :], -1.0, None, ALU.add))
                step(nc.vector.tensor_reduce(index[:, 0, :], k.ps[:, 2, NT * N_E:(NT + 1) * N_E], AX.X, ALU.max))
                nc.vector.tensor_scalar(overflow[:, :], index[0:1, 0, :], float(CAP), None, ALU.is_gt)
                dve.wait_ge(cleared, 1)
                step(nc.vector.tensor_scalar(hit[:, :, :], rank[:, :, :], float(CAP), None, ALU.is_ge))
                nc.vector.tensor_tensor(rest[:, :, 0:N_E], hit[:, :, :], weight[:, :, :], ALU.mult)
                last = lambda a: a.rearrange("p (e o) -> p e o", o=1).broadcast_to([P, N_E, CAP])
                for t in range(NT):
                    step(nc.vector.tensor_tensor(pick[:, t, 0:N_E, :], iota.broadcast_to([P, N_E, CAP]),
                                                 last(rank[:, t, :]), ALU.is_equal))
                    ins = nc.vector.tensor_tensor(pick_w[:, t, :, :], pick[:, t, 0:N_E, :], last(weight[:, t, :]), ALU.mult)
                ins.then_inc(weights_done, 1)
                dve.wait_ge(rest_turned, 1)
                nc.vector.tensor_copy(rest_t[:, :], k.ps[:, 3, 0:S])


def experts(k, l, h2_tok, pick, scatter, gain):
    nc, io = k.nc, k.io
    kinds = [(io["w_exp_gate_2"].rearrange("l e (k p) f -> l e p k f", p=P), D),
             (io["w_exp_up_2"].rearrange("l e (k p) f -> l e p k f", p=P), D),
             (io["w_exp_down_2"].rearrange("l e (k p) d -> l e p k d", p=P), FF)]
    names = tuple(f"{kind}s_loaded" for kind in ("gate", "up", "down"))
    with ExitStack() as mem:
        more = k.sb("more_slots", [P, 3, SLAB], ctx=mem)
        rows = k.sb("gathered", [P, ND, 2 * CAP], ctx=mem)
        act_buf = k.sb("silu_rows", [P, FF], ctx=mem)
        gu = k.sb("gate_up_rows", [P, FF], ctx=mem)
        gu_t = k.sb("gate_up_turned", [P, N_F, P], ctx=mem)
        y_rows = k.sb("y_rows", [P, ND, P], ctx=mem)
        zero = k.sb("zero_rows", [P, 512], ctx=mem)
        picks = pick[:, :, :, :].rearrange("p t (n e) c -> p t n (e c)", e=2)

        def slab(i, n):
            buf = (k.ring, more)[i][:, n, :]
            return buf.rearrange("p (k c) -> p k c", k=kinds[n][1] // P)

        with k.stage(*names, "cleared", "gathered", "rows_ready", "gate_done", "up_done", "act_done", "gu_done",
                     "gu_turned", "gu_t_ready", "down_done", "halves_done", "y_stored", "scattered") as (block, *sems):
            loaded = sems[0:3]
            (cleared, gathered, rows_ready, gate_done, up_done, act_done, gu_done, gu_turned, gu_t_ready, down_done,
             halves_done, y_stored, scattered) = sems[3:]

            @block.gpsimd
            def _(pool):
                nc.gpsimd.memset(zero[:, :], 0.0).then_inc(cleared, 1)
                nc.gpsimd.memset(y_rows[:, :, :], 0.0).then_inc(y_stored, 2)

            @block.sync
            def _(sp):
                for n, (view, _) in enumerate(kinds):
                    for i in range(2):
                        sp.dma_start(slab(i, n), view[l, i]).then_inc(loaded[n], 16)
                with sp.Fori(1, N_PAIR) as pair:
                    for n, (view, _) in enumerate(kinds):
                        sp.wait_ge((gate_done, up_done, down_done)[n], pair)
                        for i in range(2):
                            sp.dma_start(slab(i, n), view[l, pair * 2 + i]).then_inc(loaded[n], 16)

            @block.tensor
            def _(pe):
                def gather(pair):
                    for j in range(ND):
                        for t in range(NT):
                            ins = nc.tensor.matmul(k.ps[:, 2 + j // 4, j % 4 * P:(j % 4 + 1) * P],
                                                   h2_tok[:, t, j * P:(j + 1) * P], picks[:, t, pair, :],
                                                   start=t == 0, stop=t == NT - 1)
                    ins.then_inc(gathered, 1)

                def both(bank, left, n, c0, steps):
                    for j in range(steps):
                        for i in range(2):
                            r = slice(i * CAP, (i + 1) * CAP)
                            ins = nc.tensor.matmul(k.ps[r, bank, :], left[:, j, r], slab(i, n)[:, j, c0:c0 + 512],
                                                   start=j == 0, stop=j == steps - 1)
                    return ins

                def scatter_rows(at):
                    pe.wait_ge(y_stored, at * 2 + 2)
                    for j in range(ND):
                        ins = nc.tensor.matmul(k.ps[:, 4 + j // 2, j % 2 * S:(j % 2 + 1) * S], y_rows[:, j, :],
                                               scatter[:, at, :], start=False, stop=False)
                    ins.then_inc(scattered, 1)

                pe.wait_ge(cleared, 1)
                for b in range(4):
                    nc.tensor.matmul(k.ps[:, 4 + b, :], zero[:, 0:P], zero[:, :], start=True, stop=False)
                gather(0)
                pe.wait_ge(y_stored, 2)
                with pe.Fori(0, N_PAIR) as pair:
                    pe.wait_ge(rows_ready, pair + 1)
                    pe.wait_ge(loaded[0], pair * 32 + 32)
                    pe.wait_ge(y_stored, pair * 2 + 1)
                    both(1, rows, 0, 0, ND).then_inc(gate_done, 1)
                    pe.wait_ge(loaded[1], pair * 32 + 32)
                    pe.wait_ge(y_stored, pair * 2 + 2)
                    both(0, rows, 1, 0, ND).then_inc(up_done, 1)
                    scatter_rows(pair)
                    pe.wait_ge(gu_done, pair + 1)
                    for f in range(N_F):
                        ins = nc.tensor.transpose(k.ps[:, 1, f * P:(f + 1) * P], gu[:, f * P:(f + 1) * P], k.const("ident"))
                    ins.then_inc(gu_turned, 1)
                    gather(pair + 1)
                    pe.wait_ge(loaded[2], pair * 32 + 32)
                    pe.wait_ge(gu_t_ready, pair + 1)
                    both(1, gu_t, 2, 0, N_F).then_inc(halves_done, 1)
                    both(0, gu_t, 2, 512, N_F).then_inc(down_done, 1)
                scatter_rows(N_PAIR)
                for b in range(4):
                    ins = nc.tensor.matmul(k.ps[:, 4 + b, :], zero[:, 0:P], zero[:, :], start=False, stop=True)
                ins.then_inc(cleared, 1)

            @block.scalar
            def _(act):
                y = y_rows[:, :, :].rearrange("p j c -> p (j c)")
                with act.Fori(0, N_PAIR) as pair:
                    act.wait_ge(gate_done, pair + 1)
                    nc.scalar.activation(act_buf[:, :], k.ps[:, 1, :], ACT.Silu).then_inc(act_done, 1)
                    act.wait_ge(halves_done, pair + 1)
                    nc.scalar.activation(y[:, 0:512], k.ps[:, 1, :], ACT.Copy).then_inc(y_stored, 1)
                    act.wait_ge(down_done, pair + 1)
                    nc.scalar.activation(y[:, 512:D], k.ps[:, 0, :], ACT.Copy).then_inc(y_stored, 1)

            @block.vector
            def _(dve):
                def take_rows(count):
                    dve.wait_ge(gathered, count)
                    nc.vector.tensor_copy(rows[:, :, :].rearrange("p (b j) c -> p b (j c)", b=2), k.ps[:, 2:4, :]
                                          ).then_inc(rows_ready, 1)

                take_rows(1)
                with dve.Fori(0, N_PAIR) as pair:
                    dve.wait_ge(act_done, pair + 1)
                    dve.wait_ge(up_done, pair + 1)
                    nc.vector.tensor_tensor(gu[:, :], act_buf[:, :], k.ps[:, 0, :], ALU.mult).then_inc(gu_done, 1)
                    dve.wait_ge(gu_turned, pair + 1)
                    nc.vector.tensor_copy(gu_t[:, :, :].rearrange("p f c -> p (f c)"), k.ps[:, 1, :]
                                          ).then_inc(gu_t_ready, 1)
                    take_rows(pair + 2)
                dve.wait_ge(cleared, 2)
                for j in range(ND):
                    nc.vector.scalar_tensor_tensor(k.x[:, j, :], k.ps[:, 4 + j // 2, j % 2 * S:(j % 2 + 1) * S],
                                                   gain[:, j:j + 1], k.x[:, j, :], ALU.mult, ALU.add)


def remaining_experts(k, l, h2, wide, rest_t, overflow, gain):
    nc, io = k.nc, k.io
    views = [io["w_exp_gate_2"].rearrange("l e (k p) f -> l e p k f", p=P),
             io["w_exp_up_2"].rearrange("l e (k p) f -> l e p k f", p=P),
             io["w_exp_down_2"].rearrange("l e (k p) d -> l e p k d", p=P)]
    with ExitStack() as mem:
        gate = k.sb("gate_act", [P, 2, 2, S], ctx=mem)
        gu = k.sb("gate_up", [P, 2, 2, S], ctx=mem)
        zero = k.sb("zero", [P, 512], ctx=mem)
        with k.stage(*LOADED, "rest_saved", "wide_loaded", "cleared", "sums_closed", "gate_done", "up_done", "act_done",
                     "scaled", "gu_done", "down_done") as (block, *sems):
            loaded, (rest_saved, wide_loaded, cleared, sums_closed, gate_done, up_done, act_done, scaled, gu_done, down_done) = (
                sems[:SLOTS], sems[SLOTS:])

            @block.gpsimd
            def _(pool):
                with pool.If(pool.value_load(overflow[0:1, 0:1], min_val=0, max_val=1) > 0):
                    nc.gpsimd.memset(zero[:, :], 0.0).then_inc(cleared, 1)

            @block.sync
            def _(sp):
                with sp.If(sp.value_load(overflow[0:1, 0:1], min_val=0, max_val=1) > 0):
                    sp.dma_start(io["expert_weights"], rest_t[0:N_E, :]).then_inc(rest_saved, 16)
                    sp.wait_ge(rest_saved, 16)
                    src = io["expert_weights"].rearrange("(o e) s -> o (e s)", o=1).broadcast_to([P, N_E * S])
                    sp.dma_start(wide[:, :, :].rearrange("p e s -> p (e s)"), src).then_inc(wide_loaded, 16)
                    for n, view in enumerate(views):
                        kk = view.shape[3]
                        sp.dma_start(slab_view(k, n, kk * P, SLAB // kk), view[l, 0]).then_inc(loaded[n], 16)
                    with sp.Fori(1, N_E) as e:
                        for n, (view, through) in enumerate(zip(views, (gate_done, up_done, down_done))):
                            kk = view.shape[3]
                            sp.wait_ge(through, e * 2 + n // 2)
                            sp.dma_start(slab_view(k, n, kk * P, SLAB // kk), view[l, e]).then_inc(loaded[n], 16)

            @block.tensor
            def _(pe):
                with pe.If(pe.value_load(overflow[0:1, 0:1], min_val=0, max_val=1) > 0):
                    pe.wait_ge(cleared, 1)
                    for b in range(4):
                        ins = nc.tensor.matmul(k.ps[:, 4 + b, :], zero[:, 0:P], zero[:, :], start=True, stop=False)
                    ins.then_inc(down_done, 1)
                    with pe.Fori(0, N_E) as e:
                        for half in range(2):
                            for n, (bank, done) in enumerate(((0, gate_done), (2, up_done))):
                                if half == 0:
                                    pe.wait_ge(loaded[n], e * 16 + 16)
                                if n == 0:
                                    pe.wait_ge(gu_done, e * 2 + 1)
                                slab = slab_view(k, n, D, FF)
                                for f in range(2):
                                    c = (2 * half + f) * P
                                    for j in range(ND):
                                        ins = nc.tensor.matmul(k.ps[:, bank + half, f * S:(f + 1) * S], slab[:, j, c:c + P],
                                                               h2[:, j, :], start=j == 0, stop=j == ND - 1)
                                ins.then_inc(done, 1)
                        slab = slab_view(k, 2, FF, D)
                        pe.wait_ge(loaded[2], e * 16 + 16)
                        for half in range(2):
                            pe.wait_ge(gu_done, e * 2 + half + 2)
                            for i in range(2):
                                for j in range(ND):
                                    ins = nc.tensor.matmul(k.ps[:, 4 + j // 2, j % 2 * S:(j % 2 + 1) * S],
                                                           slab[:, 2 * half + i, j * P:(j + 1) * P], gu[:, half, i, :],
                                                           start=False, stop=False)
                            ins.then_inc(down_done, 1)
                    for b in range(4):
                        ins = nc.tensor.matmul(k.ps[:, 4 + b, :], zero[:, 0:P], zero[:, :], start=False, stop=True)
                    ins.then_inc(sums_closed, 1)

            @block.scalar
            def _(act):
                with act.If(act.value_load(overflow[0:1, 0:1], min_val=0, max_val=1) > 0):
                    with act.Fori(0, N_E) as e:
                        for half in range(2):
                            act.wait_ge(gate_done, e * 2 + half + 1)
                            act.wait_ge(gu_done, e * 2 + 1)
                            nc.scalar.activation(gate[:, half, :, :].rearrange("p f s -> p (f s)"), k.ps[:, half, :],
                                                 ACT.Silu).then_inc(act_done, 1)

            @block.vector
            def _(dve):
                with dve.If(dve.value_load(overflow[0:1, 0:1], min_val=0, max_val=1) > 0):
                    dve.wait_ge(wide_loaded, 16)
                    dve.sem_inc(gu_done, 1)
                    with dve.Fori(0, N_E) as e:
                        for half in range(2):
                            dve.wait_ge(act_done, e * 2 + half + 1)
                            dve.wait_ge(up_done, e * 2 + half + 1)
                            dve.wait_ge(down_done, e * 2 + 1)
                            nc.vector.tensor_tensor(gate[:, half, :, :].rearrange("p f s -> p (f s)"),
                                                    gate[:, half, :, :].rearrange("p f s -> p (f s)"),
                                                    k.ps[:, 2 + half, :], ALU.mult).then_inc(scaled, 1)
                            dve.wait_ge(scaled, e * 2 + half + 1)
                            nc.vector.tensor_tensor(gu[:, half, :, :], gate[:, half, :, :],
                                                    wide[:, bass.ds(e, 1), :].broadcast_to([P, 2, S]), ALU.mult).then_inc(gu_done, 1)
                    dve.wait_ge(sums_closed, 1)
                    for j in range(ND):
                        nc.vector.scalar_tensor_tensor(k.x[:, j, :], k.ps[:, 4 + j // 2, j % 2 * S:(j % 2 + 1) * S],
                                                       gain[:, j:j + 1], k.x[:, j, :], ALU.mult, ALU.add)


def second_block(k):
    nc, io = k.nc, k.io
    with ExitStack() as mem:
        k.sin = k.sb("sin", [P, S], ctx=mem)
        k.cos = k.sb("cos", [P, S], ctx=mem)
        k.mod = k.sb("mod", [P, 6 * ND], ctx=mem)
        k.w_lora = k.sb("w_lora", [P, MW], ctx=mem)
        k.a_lora = k.sb("a_lora", [P, MW], ctx=mem)
        k.g_lora = k.sb("g_lora", [P, MW], ctx=mem)
        w_router = k.sb("w_router", [P, ND, N_G + N_E], ctx=mem)
        b_router = k.sb("b_router", [P, N_G + N_E], ctx=mem)
        rest_t = k.sb("rest_t", [P, S], ctx=mem)
        overflow = k.sb("overflow", [1, 1], I32, ctx=mem)
        tile_rows = lambda ap: ap.rearrange("(r c) -> r c", c=P)
        rotation_tables(k)
        with k.stage("cleared") as (block, cleared):
            @block.gpsimd
            def _(pool):
                nc.gpsimd.memset(k.w_lora[64:P, :], 0.0).then_inc(cleared, 1)
                pool.wait_ge(cleared, 1)
                nc.gpsimd.memset(k.a_lora[0:64, :], 0.0)
        k.clear_semaphores()

        with nc.Fori(0, LAYERS) as l:
            row = lambda name: tile_rows(io[name][l])
            cols = load_rows(k, [
                ("b_ada", 6 * ND, [(0, row("b_ada_2"))]), ("b_gate", 3 * ND, [(0, row("b_gate_2"))]),
                ("norm1", ND, [(0, row("norm1_g_2"))]), ("norm2", ND, [(0, row("norm2_g_2"))]),
                ("mu", N_K, [(0, row("rwkv_mu_2"))]), ("ret_g", N_M, [(0, row("ret_gn_g_2"))]),
                ("w0", N_M, [(0, row("rwkv_w0_2"))]), ("a0", N_M, [(0, row("rwkv_a0_2"))]),
                ("k_k", N_M, [(0, row("rwkv_k_k_2"))]), ("k_a", N_M, [(0, row("rwkv_k_a_2"))]),
                ("r_k", N_M, [(0, io["rwkv_r_k_2"][l].rearrange("(j h) c -> j (h c)", h=2))]),
                ("rwkv_g", N_M, [(0, row("rwkv_gn_g_2"))]),
                ("conv_w", 3 * N_M, [(0, io["conv_w_2"][l].rearrange("i (r c) -> (i r) c", c=P))]),
            ])
            with k.stage("small_loaded") as (block, loaded):
                @block.sync
                def _(sp):
                    wide = lambda name, n: io[name][l].rearrange("(o c) -> o c", o=1).broadcast_to([P, n])
                    for dst, src in (
                            (k.w_lora[0:64, :], io["rwkv_w_lora_2"][l]), (k.a_lora[64:P, :], io["rwkv_a_lora_2"][l]),
                            (k.g_lora[:, :], io["rwkv_g_lora_2"][l]),
                            (w_router[:, :, 0:N_G], io["w_router_group_2"].rearrange("l (k p) c -> l p k c", p=P)[l]),
                            (w_router[:, :, N_G:], io["w_router_expert_2"].rearrange("l (k p) c -> l p k c", p=P)[l]),
                            (b_router[:, 0:N_G], wide("b_router_group_2", N_G)),
                            (b_router[:, N_G:], wide("b_router_expert_2", N_E))):
                        sp.dma_start(dst, src).then_inc(loaded, 16)
                    sp.wait_ge(loaded, 16 * 7)
            ada_modulation(k, l, cols)
            mod = lambda i: k.mod[:, i * ND:(i + 1) * ND]
            with ExitStack() as tmp:
                h = k.sb("h", [P, ND, S], ctx=tmp)
                y = k.sb("y_branches", [P, 3, N_M, S], ctx=tmp)
                rms_norm(k, k.x[:, :, :], h[:, :, :], mod(1), mod(0))
                with ExitStack() as tmp2:
                    pr = k.sb("p_rwkv", [P, N_K, S + 1], ctx=tmp2)
                    with ExitStack() as tmp3:
                        p = k.sb("p", [P, 4 * N_M + 3 * N_M, S], ctx=tmp3)
                        branch_projections(k, l, h, p, pr)
                        retention_and_conv(k, cols, p, y[:, 0, :, :], y[:, 2, :, :])
                    k.clear_semaphores()
                    rwkv(k, cols, pr, y[:, 1, :, :])
                k.clear_semaphores()
                merged = k.sb("merged", [P, ND, S], ctx=tmp)
                merge(k, l, cols, h, y, merged)
                w_o = io["w_o_2"].rearrange("l (k p) c -> l p k c", p=P)
                add_product(k, [w_o[l, :, :, i * 512:(i + 1) * 512] for i in range(2)],
                            [(j // 4, j % 4 * P, j) for j in range(ND)], merged, mod(2))
            k.clear_semaphores()
            with ExitStack() as tmp:
                h2 = k.sb("h2", [P, ND, S], ctx=tmp)
                rms_norm(k, k.x[:, :, :], h2[:, :, :], mod(4), mod(3))
                with ExitStack() as tmp2:
                    h2_tok = k.sb("h2_tok", [P, NT, D], ctx=tmp2)
                    pick = k.sb("pick", [P, NT, N_E + 2, CAP], ctx=tmp2)
                    scatter = k.sb("scatter", [P, N_PAIR + 1, S], ctx=tmp2)
                    router(k, h2, w_router, b_router, pick, scatter, rest_t, overflow, h2_tok)
                    experts(k, l, h2_tok, pick, scatter, mod(5))
                wide = k.sb("expert_weights_wide", [P, N_E, S], ctx=tmp)
                remaining_experts(k, l, h2, wide, rest_t, overflow, mod(5))
            k.clear_semaphores()


def finish(k):
    nc, io = k.nc, k.io
    cols = load_rows(k, [("final", ND, [(0, io["final_norm_g_2"].rearrange("(r c) -> r c", c=P))])])
    with ExitStack() as mem:
        y = k.sb("y_final", [P, ND, S], ctx=mem)
        y_tok = k.sb("y_tok", [P, NT, D], ctx=mem)
        rms_norm(k, k.x[:, :, :], y[:, :, :], cols["final"])
        with k.stage("turned", "copied", "stored") as (block, turned, copied, stored):

            @block.tensor
            def _(pe):
                for t in range(NT):
                    for j in range(ND):
                        ins = nc.tensor.transpose(k.ps[:, 2 * t + j // 4, j % 4 * P:(j % 4 + 1) * P],
                                                  y[:, j, t * P:(t + 1) * P], k.const("ident"))
                    ins.then_inc(turned, 1)

            @block.vector
            def _(dve):
                for t in range(NT):
                    dve.wait_ge(turned, t + 1)
                    nc.vector.tensor_copy(y_tok[:, t, :].rearrange("p (b c) -> p b c", b=2),
                                          k.ps[:, 2 * t:2 * t + 2, :]).then_inc(copied, 1)

            @block.sync
            def _(sp):
                for t in range(NT):
                    sp.wait_ge(copied, t + 1)
                    sp.dma_start(io["out"][0, t * P:(t + 1) * P, :], y_tok[:, t, :]).then_inc(stored, 16)
                sp.wait_ge(stored, 16 * NT)


def program(nc, io):
    with ExitStack() as ctx:
        k = Core(nc, ctx, io)
        k.columns, n = layout(constants())
        k.consts = k.sb("constants", [P, n])
        k.eps = k.sb("eps", [P, 3])
        k.ones = k.sb("ones", [P, S])
        k.rows = k.sb("rows", [P, 2, P])
        k.cols = k.sb("cols", [P, 2 * P])
        k.x = k.sb("x", [P, ND, S])
        k.mods = k.sb("mods", [P, LAYERS * 6 * ND])
        k.ada_at = 0
        k.rstd = k.sb("rstd", [P, S])
        k.ring = k.sb("ring", [P, SLOTS, SLAB])
        k.ps = ctx.enter_context(nc.psum_tensor("ps", [P, 8, 512], F32))
        load_inputs(k)
        first_block(k)
        second_block(k)
        finish(k)


INPUTS = [
    "x", "norm_g", "w_in", "q_norm_g", "k_norm_g", "forget_b", "ssd_conv_w", "ssd_conv_b", "ssd_dt_bias", "ssd_a_log",
    "ssd_d", "ssd_norm_g", "lru_conv_w", "lru_conv_b", "lru_w_a", "lru_b_a", "lru_w_x", "lru_b_x", "lru_lambda", "w_out",
    "c_2", "positions_2", "norm1_g_2", "norm2_g_2", "final_norm_g_2", "w_ada_2", "b_ada_2", "w_in_2", "w_gate_2",
    "b_gate_2", "ret_gn_g_2", "rwkv_mu_2", "rwkv_w0_2", "rwkv_w_lora_2", "rwkv_a0_2", "rwkv_a_lora_2", "rwkv_g_lora_2",
    "rwkv_k_k_2", "rwkv_k_a_2", "rwkv_r_k_2", "rwkv_gn_g_2", "conv_w_2", "w_branch_2", "w_o_2", "w_router_group_2",
    "b_router_group_2", "w_router_expert_2", "b_router_expert_2", "w_exp_gate_2", "w_exp_up_2", "w_exp_down_2",
]


def kernel(**inputs):
    import concourse.bacc as bacc
    from concourse.bass_utils import run_bass_kernel_spmd

    nc = bacc.Bacc("TRN2", target_bir_lowering=False, num_devices=1)
    arrays = {name: np.ascontiguousarray(inputs[name]) for name in INPUTS}
    for name, pieces in (("constants", constants()), ("first_constants", first_constants())):
        arrays[name] = np.concatenate(list(pieces.values()), axis=1)
    io = {name: nc.dram_tensor(f"in_{name}", a.shape, mybir.dt.from_np(a.dtype), kind="ExternalInput").ap()
          for name, a in arrays.items()}
    io["out"] = nc.dram_tensor("out", (1, S, D), F32, kind="ExternalOutput").ap()
    io["expert_weights"] = nc.dram_tensor("expert_weights", (N_E, S), F32, kind="Internal").ap()
    program(nc, io)
    result = run_bass_kernel_spmd(nc, [{f"in_{name}": a for name, a in arrays.items()}], core_ids=[0])
    return result.results[0]["out"]
```
